# Optimizing a Trainium2 kernel written in Bass

```python
import math
import jax, jax.numpy as jnp
from jax import lax
import numpy as np

D_MODEL = 1024
BATCH = 1
SEQ = 256
DEPTH = 2

N_A_LAYERS = DEPTH // 2
N_B_LAYERS = DEPTH - N_A_LAYERS
HGRN_HEADS = 8
HGRN_DK = D_MODEL // HGRN_HEADS
HGRN_DV = D_MODEL // HGRN_HEADS
HGRN_CHUNK = 64
DIFF_HEADS = 8
DIFF_DH = D_MODEL // (2 * DIFF_HEADS)
DIFF_DV = 2 * DIFF_DH
Q_BLOCK = 128
N_EXPERTS = 16
N_GROUPS = 4
EXPERTS_PER_GROUP = N_EXPERTS // N_GROUPS
TOP_K = 2
D_EXPERT = 512
MOE_BLOCK = 128
DEEPNORM_ALPHA = (2.0 * DEPTH) ** 0.25
DEEPNORM_BETA = (8.0 * DEPTH) ** -0.25
LN_EPS = 1e-5
RMS_EPS = 1e-6

kernel_name = "yoco_hgrn2_diffattn_grouped_moe"

def layer_norm(x, g, b):
    xf = x.astype(jnp.float32)
    mu = jnp.mean(xf, axis=-1, keepdims=True)
    var = jnp.mean(jnp.square(xf - mu), axis=-1, keepdims=True)
    return ((xf - mu) * lax.rsqrt(var + LN_EPS) * g + b).astype(x.dtype)

def rms_norm(xf, g):
    return xf * lax.rsqrt(jnp.mean(jnp.square(xf), axis=-1, keepdims=True) + RMS_EPS) * g

def hgrn2_mixer(x, w_in, lb, norm_g, w_out):
    B, S, _ = x.shape
    H, DK, DV, C = HGRN_HEADS, HGRN_DK, HGRN_DV, HGRN_CHUNK
    f32 = jnp.float32
    proj = jnp.einsum('bsd,de->bse', x, w_in)
    q, fl, v, g = jnp.split(proj, 4, axis=-1)
    f = lb + (1.0 - lb) * jax.nn.sigmoid(fl.astype(f32))
    log_f = jnp.log(f)
    k = 1.0 - f

    def to_chunks(t):
        return t.astype(f32).reshape(B, S // C, C, H, t.shape[-1] // H).transpose(1, 0, 3, 2, 4)

    causal = jnp.tril(jnp.ones((C, C), dtype=bool))

    def step(state, inp):
        qc, kc, vc, lfc = inp
        b = jnp.cumsum(lfc, axis=2)
        ref = b[:, :, C // 2 - 1:C // 2, :]
        scores = jnp.einsum('bhtd,bhsd->bhts', qc * jnp.exp(b - ref), kc * jnp.exp(ref - b))
        scores = jnp.where(causal, scores, 0.0)
        o = (jnp.einsum('bhts,bhsv->bhtv', scores, vc)
             + jnp.einsum('bhtd,bhdv->bhtv', qc * jnp.exp(b), state))
        b_last = b[:, :, -1:, :]
        new_state = (jnp.exp(b_last)[:, :, 0, :, None] * state
                     + jnp.einsum('bhsd,bhsv->bhdv', kc * jnp.exp(b_last - b), vc))
        return new_state, o

    state0 = jnp.zeros((B, H, DK, DV), f32)
    _, o = lax.scan(step, state0, (to_chunks(q), to_chunks(k), to_chunks(v), to_chunks(log_f)))
    o = o.transpose(1, 0, 3, 2, 4).reshape(B, S, H, DV)
    o = rms_norm(o, norm_g).reshape(B, S, H * DV) * jax.nn.sigmoid(g.astype(f32))
    return jnp.einsum('bse,ed->bsd', o.astype(x.dtype), w_out)

def shared_kv(x, kv_w):
    B, S, _ = x.shape
    kv = jnp.einsum('bsd,de->bse', x, kv_w)
    kpart, vpart = jnp.split(kv, [2 * DIFF_HEADS * DIFF_DH], axis=-1)
    k = kpart.reshape(B, S, DIFF_HEADS, 2, DIFF_DH).transpose(0, 2, 3, 1, 4)
    v = vpart.reshape(B, S, DIFF_HEADS, DIFF_DV).transpose(0, 2, 1, 3)
    return k, v

def diff_attention(x, k, v, w_q, lam, subln_g, w_out, lambda_init):
    B, S, _ = x.shape
    H, DH, DV = DIFF_HEADS, DIFF_DH, DIFF_DV
    NB = S // Q_BLOCK
    q = jnp.einsum('bsd,de->bse', x, w_q).reshape(B, S, H, 2, DH).transpose(0, 2, 3, 1, 4)
    q = q * (DH ** -0.5)
    lamf = lam.astype(jnp.float32)
    lam_val = (jnp.exp(jnp.sum(lamf[0] * lamf[1])) - jnp.exp(jnp.sum(lamf[2] * lamf[3]))
               + lambda_init)
    q_blocks = q.reshape(B, H, 2, NB, Q_BLOCK, DH).transpose(3, 0, 1, 2, 4, 5)
    kpos = jnp.arange(S)

    def attend(inp):
        qb, bi = inp
        qpos = bi * Q_BLOCK + jnp.arange(Q_BLOCK)
        s = jnp.einsum('bhcqd,bhckd->bhcqk', qb, k).astype(jnp.float32)
        s = jnp.where(kpos[None, :] <= qpos[:, None], s, -jnp.inf)
        p = jax.nn.softmax(s, axis=-1)
        a = p[:, :, 0] - lam_val * p[:, :, 1]
        return jnp.einsum('bhqk,bhkv->bhqv', a.astype(v.dtype), v)

    o = lax.map(attend, (q_blocks, jnp.arange(NB)))
    o = o.transpose(1, 0, 3, 2, 4).reshape(B, S, H, DV).astype(jnp.float32)
    o = rms_norm(o, subln_g) * (1.0 - lambda_init)
    return jnp.einsum('bse,ed->bsd', o.reshape(B, S, H * DV).astype(x.dtype), w_out)

def moe_ffn(x, router_w, router_b, w_gate, w_up, w_down):
    B, S, D = x.shape
    NB = S // MOE_BLOCK
    xb = x.reshape(B, NB, MOE_BLOCK, D).transpose(1, 0, 2, 3).reshape(NB, B * MOE_BLOCK, D)
    expert_group = jnp.arange(N_EXPERTS) // EXPERTS_PER_GROUP

    def block(xt):
        probs = jax.nn.softmax((xt @ router_w).astype(jnp.float32), axis=-1)
        sel = probs + router_b
        gscore = lax.top_k(sel.reshape(-1, N_GROUPS, EXPERTS_PER_GROUP), TOP_K)[0].sum(-1)
        gbest = jnp.argmax(gscore, axis=-1)
        in_group = expert_group[None, :] == gbest[:, None]
        _, idx = lax.top_k(jnp.where(in_group, sel, -jnp.inf), TOP_K)
        gates = jnp.take_along_axis(probs, idx, axis=-1)
        gates = gates / jnp.sum(gates, axis=-1, keepdims=True)
        comb = jnp.sum(jax.nn.one_hot(idx, N_EXPERTS, dtype=jnp.float32) * gates[..., None], axis=1)
        h = (jax.nn.silu(jnp.einsum('td,edf->tef', xt, w_gate))
             * jnp.einsum('td,edf->tef', xt, w_up))
        h = h * comb[:, :, None].astype(h.dtype)
        return jnp.einsum('tef,efd->td', h, w_down)

    y = lax.map(block, xb)
    return y.reshape(NB, B, MOE_BLOCK, D).transpose(1, 0, 2, 3).reshape(B, S, D)

def setup_inputs(seed: int = 0) -> dict:
    key = jax.random.key(seed)
    ks = jax.random.split(key, 20)
    D = D_MODEL
    nrm = jax.random.normal
    f32 = jnp.float32
    d_a = HGRN_HEADS * HGRN_DK
    d_bq = 2 * DIFF_HEADS * DIFF_DH
    d_bv = DIFF_HEADS * DIFF_DV
    return {
        "x": nrm(ks[0], (BATCH, SEQ, D), f32),
        "a_w_in": nrm(ks[1], (N_A_LAYERS, D, 4 * d_a), f32) * D ** -0.5,
        "a_lb": nrm(ks[2], (N_A_LAYERS + 1, d_a), f32) * 0.1,
        "a_norm_g": 1.0 + 0.02 * nrm(ks[3], (N_A_LAYERS, HGRN_HEADS, HGRN_DV), f32),
        "a_w_out": nrm(ks[4], (N_A_LAYERS, d_a, D), f32) * d_a ** -0.5 * DEEPNORM_BETA,
        "kv_w": nrm(ks[5], (D, d_bq + d_bv), f32) * D ** -0.5,
        "b_w_q": nrm(ks[6], (N_B_LAYERS, D, d_bq), f32) * D ** -0.5,
        "b_lam": nrm(ks[7], (N_B_LAYERS, 4, DIFF_DH), f32) * 0.1,
        "b_subln_g": 1.0 + 0.02 * nrm(ks[8], (N_B_LAYERS, DIFF_DV), f32),
        "b_w_out": nrm(ks[9], (N_B_LAYERS, d_bv, D), f32) * d_bv ** -0.5 * DEEPNORM_BETA,
        "ln1_g": 1.0 + 0.02 * nrm(ks[10], (DEPTH, D), f32),
        "ln1_b": 0.02 * nrm(ks[11], (DEPTH, D), f32),
        "ln2_g": 1.0 + 0.02 * nrm(ks[12], (DEPTH, D), f32),
        "ln2_b": 0.02 * nrm(ks[13], (DEPTH, D), f32),
        "router_w": nrm(ks[14], (D, N_EXPERTS), f32) * D ** -0.5,
        "router_b": 0.01 * nrm(ks[15], (N_EXPERTS,), f32),
        "moe_w_gate": nrm(ks[16], (DEPTH, N_EXPERTS, D, D_EXPERT), f32) * D ** -0.5,
        "moe_w_up": nrm(ks[17], (DEPTH, N_EXPERTS, D, D_EXPERT), f32) * D ** -0.5,
        "moe_w_down": nrm(ks[18], (DEPTH, N_EXPERTS, D_EXPERT, D), f32) * D_EXPERT ** -0.5 * DEEPNORM_BETA,
    }

def reference(x, a_w_in, a_lb, a_norm_g, a_w_out, kv_w, b_w_q, b_lam, b_subln_g, b_w_out,
              ln1_g, ln1_b, ln2_g, ln2_b, router_w, router_b, moe_w_gate, moe_w_up, moe_w_down):
    lb_all = jnp.cumsum(jax.nn.softmax(a_lb.astype(jnp.float32), axis=0), axis=0)
    k_sh, v_sh = None, None
    for l in range(DEPTH):
        if l < N_A_LAYERS:
            mix = hgrn2_mixer(x, a_w_in[l], lb_all[l], a_norm_g[l], a_w_out[l])
        else:
            if l == N_A_LAYERS:
                k_sh, v_sh = shared_kv(x, kv_w)
            j = l - N_A_LAYERS
            lambda_init = 0.8 - 0.6 * math.exp(-0.3 * l)
            mix = diff_attention(x, k_sh, v_sh, b_w_q[j], b_lam[j], b_subln_g[j], b_w_out[j],
                                 lambda_init)
        x = layer_norm(DEEPNORM_ALPHA * x + mix, ln1_g[l], ln1_b[l])
        ffn = moe_ffn(x, router_w, router_b, moe_w_gate[l], moe_w_up[l], moe_w_down[l])
        x = layer_norm(DEEPNORM_ALPHA * x + ffn, ln2_g[l], ln2_b[l])
    return x


_drawn_inputs = setup_inputs


def setup_inputs(seed=0):
    import zlib

    import numpy as np

    out = dict(_drawn_inputs(seed))
    spreads = {}
    factors = {'a_norm_g': 4.729, 'b_subln_g': 5.101}
    for name, (base, spread) in spreads.items():
        noise = np.random.default_rng([zlib.crc32(name.encode()), seed]).standard_normal(out[name].shape)
        drawn = base * np.exp(spread * noise) if base else spread * noise
        out[name] = __import__('jax').numpy.asarray(drawn.astype(out[name].dtype))
    for name, factor in factors.items():
        out[name] = (out[name] * factor).astype(out[name].dtype)
    return out
```

```python
import math
from contextlib import ExitStack

import concourse.bass as bass
from concourse import mybir

F32 = mybir.dt.float32
BF16 = mybir.dt.bfloat16
I32 = mybir.dt.int32
ALU = mybir.AluOpType
ACT = mybir.ActivationFunctionType
AX = mybir.AxisListType

P = 128
D = 1024
T = 256
TT = T // P
KT = D // P
LAYERS = 2
HEADS = 8
CHUNK = 64
DH = 64
E = 16
GROUPS = 4
F = 512
FT = F // P
SLOTS = 64
PAIRS = E // 2
COLS = 512
ALPHA = (2.0 * LAYERS) ** 0.25
LAMBDA_INIT = 0.8 - 0.6 * math.exp(-0.3 * 1)
LN_EPS = 1e-5
RMS_EPS = 1e-6
BIG = 1e30
SCALE = DH ** -0.5

RING = 2
(V0, V1, HP0, HP1, HP2, HP3, G0, G1, AO0, AO1,
 K0, Q0, K1, Q1, BV0, BV1, BO0, BO1) = range(18)
HP = [HP0, HP1, HP2, HP3]
XT_BANK, GU_BANK, YT_BANK, YS_BANK = 4, 5, 6, 7


def build(nc, ins, out):
    ctx = ExitStack()
    with ctx:
        def sb(name, shape, dt=F32):
            return ctx.enter_context(nc.sbuf_tensor(name, shape, dt))

        def sem(name):
            return ctx.enter_context(nc.semaphore(name))

        dense = sb("dense", [P, RING, KT, COLS])
        w_gate = sb("w_gate", [P, 2, KT, F])
        w_up = sb("w_up", [P, 2, KT, F])
        w_down = sb("w_down", [P, 2, FT, D])
        x = sb("x_sb", [P, TT, D])
        xT = sb("xT", [P, KT, T])
        ln_gb = sb("ln_gb", [P, 2, D])
        ident = sb("ident", [P, P])
        causal = sb("causal", [P, P], I32)
        later = sb("later", [P, P])
        ones = sb("ones", [P, P])
        zeros16 = sb("zeros16", [P, P], BF16)
        iota = sb("iota", [P, T])
        seg = sb("seg", [P, 2 * T])
        amask = sb("amask", [P, 3 * P])
        first_g = sb("first_g", [P, GROUPS])
        first_e = sb("first_e", [P, E])
        prow = sb("prow", [25, P])
        pcol = sb("pcol", [P, 25])
        lb = sb("lb", [P, 2 * HEADS])
        lam_in = sb("lam_in", [P, 4, DH])
        lam = sb("lam", [P, 8])
        lam_p = sb("lam_p", [P, 2, DH])
        router = sb("router", [P, KT, E])
        router_bias = sb("router_bias", [P, E])
        stats = sb("stats", [P, TT, 2, 6])
        mv = sb("mv", [P, TT, 2])
        rs = sb("rs", [P, 5, 2 * HEADS])
        ss = sb("ss", [P, 2 * HEADS])
        o3 = sb("o3", [P, 3, D])
        o = o3[:, 0:TT, :]
        scratch = sb("scratch", [P, 2 * TT * D + 12 * 2 * T])
        place = [0]

        def carve(*shape, parts=P):
            size = math.prod(shape)
            ap = scratch[0:parts, place[0]:place[0] + size]
            place[0] += size
            names = "abc"[:len(shape)]
            if len(shape) == 1:
                return ap
            return ap.rearrange(f"p ({' '.join(names)}) -> p {' '.join(names)}", **dict(zip(names, shape)))

        v = carve(TT, D)
        g = carve(TT, D)
        mix = carve(12, 2 * T)
        sg, kk, b, d1, d2, e1, qe, qb, ke, kb, scm, f = (mix[:, i, :] for i in range(12))
        lf, e3, e2, e4 = sg, b, d1, d2
        third = o3[:, 2, :].rearrange("p (a h n) -> p a h n", a=4, h=2)
        kbs, kbT, state = third[:, 0], third[:, 1], third[:, 2]
        qbs = sb("qbs", [P, 2, 2, P])
        iota_i = e1[:, 0:T].bitcast(I32)
        qT = g[:, :, :].rearrange("p a (h t) -> p (a h) t", t=T)
        kT = mix[:, 0:4, :].rearrange("p a (h t) -> p (a h) t", t=T)
        s_in = mix[:, 4:8, :].rearrange("p (u c) n -> p u c n", u=2)
        s_ex = mix[:, 8:12, :].rearrange("p (u c) n -> p u c n", u=2)
        aT = mix[:, 4:6, :].rearrange("p u (s n) -> p u s n", n=P)
        amx = sb("amx", [P, 2, 4])
        asum = sb("asum", [P, 2, 4])
        arec = sb("arec", [P, 2, 4])
        rt = sb("rt", [P, 12, TT * E])
        rg = sb("rg", [P, 12, TT * E])
        slot = sb("slot", [P, TT, E + 2])
        gate = sb("gate", [P, TT, E + 2])
        count_f = sb("count_f", [1, 4, E])
        chunks = sb("chunks", [1, E], I32)
        place[0] = 0
        pick_ab = [carve(TT, SLOTS) for _ in range(2)]
        pick_g = carve(TT, 2, SLOTS)
        xe = [carve(KT, SLOTS) for _ in range(2)]
        silu = carve(FT * SLOTS)
        hT = carve(2, FT * SLOTS)
        yT = carve(KT, 2, SLOTS)
        ys = carve(D)
        put = carve(T)
        o_pick = carve(TT, SLOTS)
        o_pick_g = carve(TT, SLOTS)
        o_xe = carve(KT, SLOTS)
        o_hT = carve(FT * SLOTS)
        o_yT = carve(KT, SLOTS)
        o_ys = carve(D, parts=SLOTS)
        o_put = carve(T, parts=SLOTS)
        assert place[0] <= scratch.shape[1]

        ps = ctx.enter_context(nc.psum_tensor("ps", [P, 8, COLS], F32))

        x_in = sem("x_in")
        small_in = sem("small_in")
        router_in = sem("router_in")
        ln_in = sem("ln_in")
        dense_in = [sem(f"dense_in{r}") for r in range(RING)]
        gate_in = [sem(f"gate_in{e}") for e in range(2)]
        up_in = [sem(f"up_in{e}") for e in range(2)]
        down_in = [sem(f"down_in{e}") for e in range(2)]
        out_sem = sem("out_sem")
        consts_ready = sem("consts_ready")
        pool_step = sem("pool_step")
        dve_step = sem("dve_step")
        act_step = sem("act_step")
        pcol_ready = sem("pcol_ready")
        lam_exp_ready = sem("lam_exp_ready")
        lam_sum_ready = sem("lam_sum_ready")
        proj_ready = sem("proj_ready")
        tp_ready = sem("tp_ready")
        xT_act = sem("xT_act")
        xT_dve = sem("xT_dve")
        v_act = sem("v_act")
        v_dve = sem("v_dve")
        sg_ready = sem("sg_ready")
        f_ready = sem("f_ready")
        lf_ready = sem("lf_ready")
        d_ready = sem("d_ready")
        kk_ready = sem("kk_ready")
        ex_ready = sem("ex_ready")
        q_used = sem("q_used")
        q_ready = sem("q_ready")
        k_ready = sem("k_ready")
        sc_ready = sem("sc_ready")
        scm_ready = sem("scm_ready")
        kbt_ps = sem("kbt_ps")
        kbt_ready = sem("kbt_ready")
        st_ps = sem("st_ps")
        st_ready = sem("st_ready")
        o_ps = sem("o_ps")
        o_ready = sem("o_ready")
        g_ready = sem("g_ready")
        var_ready = sem("var_ready")
        root_ready = sem("root_ready")
        o_done = [sem(f"o_done{t}") for t in range(TT)]
        res_done = sem("res_done")
        ln_stat = sem("ln_stat")
        x_done = [sem(f"x_done{t}") for t in range(TT)]
        kq_act = sem("kq_act")
        kq_dve = sem("kq_dve")
        s_ps = sem("s_ps")
        s_ready = sem("s_ready")
        s_ready_raw = sem("s_ready_raw")
        p_ready = sem("p_ready")
        a_ready = sem("a_ready")
        at_ps = sem("at_ps")
        at_ready = sem("at_ready")
        logit_ps = sem("logit_ps")
        logit_ready = sem("logit_ready")
        rexp_ready = sem("rexp_ready")
        routed = sem("routed")
        rank_ps = sem("rank_ps")
        slots_ready = sem("slots_ready")
        xe_ps = sem("xe_ps")
        xe_ready = sem("xe_ready")
        pick_ready = sem("pick_ready")
        pickg_ready = sem("pickg_ready")
        gu_ps = sem("gu_ps")
        silu_ready = sem("silu_ready")
        h_done = sem("h_done")
        yt_ps = sem("yt_ps")
        yt_done = sem("yt_done")
        ys_ps = sem("ys_ps")
        ys_done = sem("ys_done")
        put_ps = sem("put_ps")
        put_done = sem("put_done")
        acc_ps = sem("acc_ps")
        o_free = sem("o_free")
        op_ready = sem("op_ready")
        opg_ready = sem("opg_ready")
        oxe_ps = sem("oxe_ps")
        oxe_ready = sem("oxe_ready")
        ogu_ps = sem("ogu_ps")
        osilu_ready = sem("osilu_ready")
        oh_done = sem("oh_done")
        oyt_ps = sem("oyt_ps")
        oyt_done = sem("oyt_done")
        oput_ps = sem("oput_ps")
        oput_done = sem("oput_done")
        oys_ps = sem("oys_ps")
        oys_done = sem("oys_done")

        taken = {}
        for n in (V0, V1):
            taken[n, 0], taken[n, 1] = (v_act, n + 1), (v_dve, n + 1)
        for hp, n in enumerate(HP):
            taken[n, 0], taken[n, 1] = (sg_ready, hp + 1), (q_used, hp + 1)
        for i, n in enumerate((G0, G1)):
            taken[n, 0], taken[n, 1] = (g_ready, 2 * i + 1), (g_ready, 2 * i + 2)
        for i, n in enumerate((AO0, AO1)):
            taken[n, 0], taken[n, 1] = (res_done, 2 * i + 1), (res_done, 2 * i + 2)
        for i, n in enumerate((K0, Q0, K1, Q1)):
            taken[n, 0], taken[n, 1] = (kq_act, i + 1), (kq_dve, i + 1)
        for i, n in enumerate((BV0, BV1)):
            taken[n, 0], taken[n, 1] = (v_act, i + 3), (v_dve, i + 3)

        def dense_use(n):
            return n // RING + 1

        block = ctx.enter_context(nc.Block())

        @block.sync
        def _(sp):
            def cols(w, first):
                return w[:, first:first + COLS].rearrange("(k p) n -> p k n", p=P)

            w_in, kv = ins["a_w_in"][0], ins["kv_w"]
            w_q, a_out, b_out = ins["b_w_q"][0], ins["a_w_out"][0], ins["b_w_out"][0]
            source = {V0: (w_in, 2 * D), V1: (w_in, 2 * D + COLS), G0: (w_in, 3 * D), G1: (w_in, 3 * D + COLS),
                      AO0: (a_out, 0), AO1: (a_out, COLS), K0: (kv, 0), K1: (kv, COLS), Q0: (w_q, 0),
                      Q1: (w_q, COLS), BV0: (kv, D), BV1: (kv, D + COLS), BO0: (b_out, 0), BO1: (b_out, COLS)}

            def load_dense(n):
                if n >= RING:
                    sp.wait_ge(proj_ready, 2 * (n - RING) + 2)
                r = n % RING
                if n in HP:
                    half = COLS // 2
                    first = (n - HP0) * half
                    for i, at in enumerate((D + first, first)):
                        sp.dma_start(dense[:, r, :, i * half:(i + 1) * half],
                                     w_in[:, at:at + half].rearrange("(k p) n -> p k n", p=P)
                                     ).then_inc(dense_in[r], 16)
                else:
                    w = cols(*source[n])
                    for half in (slice(0, KT // 2), slice(KT // 2, KT)):
                        sp.dma_start(dense[:, r, half, :], w[:, half, :]).then_inc(dense_in[r], 16)

            wg, wu, wd = ins["moe_w_gate"], ins["moe_w_up"], ins["moe_w_down"]

            def load_expert(layer, e, which, index):
                pick_e = (lambda w: w[layer, bass.ds(index, 1)].rearrange("one (k p) n -> p (one k) n", p=P))
                if which == 0:
                    sp.dma_start(w_gate[:, e, :, :], pick_e(wg)).then_inc(gate_in[e], 16)
                elif which == 1:
                    sp.dma_start(w_up[:, e, :, :], pick_e(wu)).then_inc(up_in[e], 16)
                else:
                    sp.dma_start(w_down[:, e, :, :], pick_e(wd)).then_inc(down_in[e], 16)

            sp.dma_start(x[:, 0, :], ins["x"][0, 0:P, :]).then_inc(x_in, 16)
            sp.dma_start(x[:, 1, :], ins["x"][0, P:T, :]).then_inc(x_in, 16)
            for layer in range(LAYERS):
                blocks = range(V0, AO1 + 1) if layer == 0 else range(K0, BO1 + 1)
                first = [(e, which) for e in range(2) for which in range(3)]
                for i, n in enumerate(blocks):
                    if i >= RING and first:
                        e, which = first.pop(0)
                        if layer:
                            q = PAIRS - 1
                            if which < 2:
                                sp.wait_ge(gu_ps, 2 * q + 1 + e)
                            else:
                                sp.wait_ge(yt_ps, 2 * q + 1 + e)
                        load_expert(layer, e, which, e)
                    load_dense(n)
                for e, which in first:
                    if layer:
                        q = PAIRS - 1
                        sp.wait_ge(gu_ps if which < 2 else yt_ps, 2 * q + 1 + e)
                    load_expert(layer, e, which, e)
                with sp.Fori(1, PAIRS, 1) as p:
                    for e in range(2):
                        sp.wait_ge(gu_ps, 2 * (PAIRS * layer + p) - 1 + e)
                        load_expert(layer, e, 0, 2 * p + e)
                        load_expert(layer, e, 1, 2 * p + e)
                        sp.wait_ge(yt_ps, 2 * (PAIRS * layer + p) - 1 + e)
                        load_expert(layer, e, 2, 2 * p + e)
            for t in range(TT):
                sp.wait_ge(x_done[t], 4)
                sp.dma_start(out[0, t * P:(t + 1) * P, :], x[:, t, :]).then_inc(out_sem, 16)
            sp.wait_ge(out_sem, 16 * TT)

        @block.gpsimd
        def _(pool):
            steps = [0]

            def step(instr):
                steps[0] += 1
                instr.then_inc(pool_step, 1)
                pool.wait_ge(pool_step, steps[0])

            step(pool.memset(ones[:, :], 1.0))
            pool.affine_select(out=ident[:, :], in_=ones[:, :], compare_op=ALU.is_equal, fill=0.0,
                               base=0, pattern=[[-1, P]], channel_multiplier=1).then_inc(consts_ready, 1)
            pool.affine_select(out=later[:, :], in_=ones[:, :], compare_op=ALU.is_gt, fill=0.0,
                               base=0, pattern=[[1, P]], channel_multiplier=-1).then_inc(consts_ready, 1)
            step(pool.memset(causal[:, :], 1))
            step(pool.affine_select(out=causal[:, :], in_=causal[:, :], compare_op=ALU.is_ge, fill=0.0,
                                    base=0, pattern=[[1, P]], channel_multiplier=-1))
            step(pool.memset(seg[:, :], 1.0))
            pool.memset(seg[:, :].rearrange("p (c n) -> p c n", n=CHUNK)[:, :, 0:1], 0.0).then_inc(consts_ready, 1)
            step(pool.memset(amask[:, :], 0.0))
            for at in (0, 2 * P):
                part = amask[:, at:at + P]
                step(pool.affine_select(out=part, in_=part, compare_op=ALU.is_ge, fill=-BIG,
                                        base=0, pattern=[[-1, P]], channel_multiplier=1))
            step(pool.iota(iota_i[:, :], pattern=[[1, T]], base=0, channel_multiplier=0))
            step(pool.tensor_copy(iota[:, :], iota_i[:, :]))
            step(pool.tensor_scalar(first_g[:, :], iota[:, 0:GROUPS], -1.0, float(GROUPS), ALU.mult, ALU.add))
            step(pool.tensor_scalar(first_e[:, :], iota[:, 0:E], -1.0, float(E), ALU.mult, ALU.add))
            step(pool.memset(zeros16[:, :], 0.0))
            step(pool.memset(slot[:, :, :], -1.0))
            step(pool.memset(gate[:, :, :], 0.0))
            pool.memset(scm, 0.0).then_inc(consts_ready, 1)

            for hp in range(4):
                pool.wait_ge(ex_ready, hp + 1)
                pool.wait_ge(kk_ready, hp + 1)
                if hp:
                    pool.wait_ge(kbt_ps, hp)
                pool.tensor_tensor(ke, kk, e2, ALU.mult).then_inc(pool_step, 1)
                pool.tensor_tensor(kb, kk, e4, ALU.mult).then_inc(pool_step, 1)
                steps[0] += 2
                pool.wait_ge(pool_step, steps[0])
                for h in range(2):
                    at = h * T
                    pool.tensor_scalar(kbs[:, h, 0:CHUNK], kb[:, at:at + CHUNK],
                                       e3[:, at + 2 * CHUNK - 1:at + 2 * CHUNK], None, ALU.mult)
                    last = pool.tensor_copy(kbs[:, h, CHUNK:P], kb[:, at + CHUNK:at + P])
                last.then_inc(k_ready, 1)

            for layer in range(LAYERS):
                pool.wait_ge(slots_ready, layer + 1)
                if layer:
                    pool.wait_ge(put_ps, (PAIRS + 1) * layer)
                pool.memset(pick_g[:, :, :, :], 0.0).then_inc(pickg_ready, 1)
                with pool.Fori(0, PAIRS, 1) as i:
                    pool.wait_ge(put_ps, (PAIRS + 1) * layer + i + 1)
                    pool.wait_ge(pick_ready, (2 * PAIRS + 2) * layer + 2 * i + 2)
                    pool.wait_ge(slots_ready, layer + 1)
                    for e in range(2):
                        last = pool.tensor_tensor(pick_g[:, :, e, :], pick_ab[e],
                                                  gate[:, :, bass.ds(2 * i + e, 1)].to_broadcast([P, TT, SLOTS]),
                                                  ALU.mult)
                    last.then_inc(pickg_ready, 1)

        @block.scalar
        def _(act):
            def load_ln(i):
                layer, which = divmod(i, 2)
                for j, name in enumerate(("g", "b")):
                    row = ins[f"ln{which + 1}_{name}"][layer:layer + 1, :]
                    act.dma_start(ln_gb[:, j, :], row.broadcast_to([P, D])).then_inc(ln_in, 16)

            act.dma_start(prow[0:16, :], ins["a_lb"].rearrange("l (h d) -> (l h) d", d=P)).then_inc(small_in, 16)
            act.dma_start(prow[16:24, :], ins["a_norm_g"][0]).then_inc(small_in, 16)
            act.dma_start(prow[24:25, :], ins["b_subln_g"]).then_inc(small_in, 16)
            act.dma_start(lam_in[:, :, :].rearrange("p a d -> p (a d)"),
                           ins["b_lam"].rearrange("l a d -> l (a d)").broadcast_to([P, 4 * DH])).then_inc(small_in, 16)
            act.dma_start(router[:, :, :], ins["router_w"].rearrange("(k p) e -> p k e", p=P)).then_inc(router_in, 16)
            act.dma_start(router_bias[:, :], ins["router_b"].rearrange("(a e) -> a e", a=1)
                           .broadcast_to([P, E])).then_inc(router_in, 16)
            load_ln(0)

            def reload_ln(i):
                for t in range(TT):
                    act.wait_ge(x_done[t], i)
                load_ln(i)

            def transposed(call, scale=None):
                for i, bank in enumerate((0, 2)):
                    act.wait_ge(tp_ready, 4 * call + bank + 1)
                    if scale is None:
                        nc.scalar.activation(xT[:, 2 * bank:2 * bank + 2, :].rearrange("p k t -> p (k t)"),
                                             ps[:, bank, :], ACT.Copy).then_inc(xT_act, 1)
                    else:
                        for j in range(2):
                            last = nc.scalar.activation(xT[:, 2 * bank + j, :], ps[:, bank, j * T:(j + 1) * T],
                                                        ACT.Identity, scale=scale(2 * bank + j))
                        last.then_inc(xT_act, 1)

            def take(n, j, dst, sem_done, func=ACT.Copy):
                act.wait_ge(proj_ready, 2 * n + j + 1)
                nc.scalar.activation(dst, ps[:, 4 + 2 * (n % 2) + j, :], func).then_inc(sem_done, 1)

            def heads_out(k):
                if k > 4:
                    act.wait_ge(o_ready, k)
                act.wait_ge(o_ps, k + 1)
                hp = k % 4
                bank = 3 if k < 4 else 2 + k % 2
                junk = f if k < 4 else mix[:, 6, :]
                src = ps[:, bank, :].rearrange("p (h t d) -> p h t d", h=2, t=TT)
                for h in range(2):
                    for t in range(TT):
                        at = 2 * hp + h
                        nc.scalar.activation(junk[:, (2 * h + t) * P:(2 * h + t + 1) * P], src[:, h, t, :], ACT.Square,
                                             accum_out=ss[:, t * HEADS + at:t * HEADS + at + 1])
                last = nc.scalar.activation(o[:, :, 2 * hp * P:(2 * hp + 2) * P].rearrange("p t (h d) -> p h t d", h=2),
                                            src, ACT.Copy)
                last.then_inc(o_ready, 1)

            def root(i, width):
                act.wait_ge(var_ready, i + 1)
                nc.scalar.activation(rs[:, 1, 0:width], rs[:, 0, 0:width], ACT.Sqrt).then_inc(root_ready, 1)

            roots = iter(range(6))
            act.wait_ge(pcol_ready, 2)
            nc.scalar.activation(lb[:, :], lb[:, :], ACT.Exp).then_inc(lam_exp_ready, 1)
            act.wait_ge(lam_sum_ready, 2)
            nc.scalar.activation(lam[:, 2:4], lam[:, 0:2], ACT.Exp).then_inc(lam_exp_ready, 1)

            transposed(0)
            for n in (V0, V1):
                take(n, 0, v[:, 0, n * COLS:(n + 1) * COLS], v_act)
            for hp in range(4):
                take(HP[hp], 0, sg, sg_ready, ACT.Sigmoid)
                act.wait_ge(f_ready, hp + 1)
                nc.scalar.activation(lf, f, ACT.Ln).then_inc(lf_ready, 1)
                act.wait_ge(d_ready, hp + 1)
                if hp:
                    act.wait_ge(k_ready, hp)
                    act.wait_ge(q_ready, hp)
                nc.scalar.activation(e3, b, ACT.Exp)
                nc.scalar.activation(e1, d1, ACT.Exp)
                nc.scalar.activation(e2, d1, ACT.Exp, scale=-1.0)
                nc.scalar.activation(e4, d2, ACT.Exp).then_inc(ex_ready, 1)
                if hp:
                    heads_out(hp - 1)
                act.wait_ge(kbt_ps, hp + 1)
                nc.scalar.activation(kbT[:, :, :].rearrange("p h d -> p (h d)"), ps[:, 1, 0:2 * P],
                                     ACT.Copy).then_inc(kbt_ready, 1)
            for i, n in enumerate((G0, G1)):
                for j in range(2):
                    take(n, j, g[:, j, i * COLS:(i + 1) * COLS], g_ready, ACT.Sigmoid)
            heads_out(3)
            root(next(roots), 2 * HEADS)
            transposed(1, lambda k: pcol[:, 16 + k:17 + k])

            def moe(layer):
                def overflow(count, done):
                    with act.If(count > 1):
                        with act.Fori(1, count, 1):
                            act.wait_ge(oxe_ps, done)
                            nc.scalar.activation(o_xe[:, :, :].rearrange("p k s -> p (k s)"), ps[:, XT_BANK, :],
                                                 ACT.Copy).then_inc(oxe_ready, 1)
                            act.wait_ge(ogu_ps, done)
                            nc.scalar.activation(silu[:, :], ps[:, GU_BANK, 0:FT * SLOTS],
                                                 ACT.Silu).then_inc(osilu_ready, 1)
                            act.reg_add(done, done, 1)

                def take_xe(e, value):
                    act.wait_ge(xe_ps, value)
                    nc.scalar.activation(xe[e].rearrange("p k s -> p (k s)"), ps[:, XT_BANK, :],
                                         ACT.Copy).then_inc(xe_ready, 1)

                g0 = (2 * PAIRS + 1) * layer
                act.wait_ge(slots_ready, layer + 1)
                take_xe(0, g0 + 1)
                with act.Fori(0, PAIRS, 1) as i:
                    count_a = act.value_load(chunks[0:1, bass.ds(2 * i, 1)], min_val=0, max_val=T // SLOTS)
                    count_b = act.value_load(chunks[0:1, bass.ds(2 * i + 1, 1)], min_val=0, max_val=T // SLOTS)
                    for e, count in enumerate((count_a, count_b)):
                        overflow(count, done)
                        act.wait_ge(gu_ps, 2 * (PAIRS * layer + i) + 1 + e)
                        nc.scalar.activation(silu[:, :], ps[:, GU_BANK, 0:FT * SLOTS],
                                             ACT.Silu).then_inc(silu_ready, 1)
                        take_xe(1 - e, g0 + 2 * i + 2 + e)

            def router_exp(layer):
                act.wait_ge(logit_ready, layer + 1)
                nc.scalar.activation(rt[:, 1, :], rt[:, 0, :], ACT.Exp).then_inc(rexp_ready, 1)

            done = act.alloc_register("act_done")
            act.reg_mov(done, 1)
            root(next(roots), TT)
            transposed(2)
            reload_ln(1)
            router_exp(0)
            moe(0)
            root(next(roots), TT)
            transposed(3)
            reload_ln(2)
            def take_kq(i):
                dst = (kT, qT)[i % 2]
                take((K0, Q0, K1, Q1)[i], 0, dst[:, 4 * (i // 2):4 * (i // 2) + 2, :].rearrange("p h t -> p (h t)"), kq_act)

            def probabilities(h):
                u = h % 2
                act.wait_ge(s_ready, h + 1)
                if h >= 2:
                    act.wait_ge(a_ready, h - 1)
                for c in range(2):
                    for qt, (lo, hi) in enumerate(((0, P), (P, 3 * P))):
                        at = 2 * qt + c
                        last = nc.scalar.activation(s_ex[:, u, c, lo:hi], s_in[:, u, c, lo:hi], ACT.Exp,
                                                    bias=amx[:, u, at:at + 1], scale=SCALE,
                                                    accum_out=asum[:, u, at:at + 1])
                last.then_inc(p_ready, 1)

            for i in range(3):
                take_kq(i)
            probabilities(0)
            take_kq(3)
            for h in range(1, 4):
                probabilities(h)
            take(BV0, 0, v[:, 0, 0:COLS], v_act)
            for h in range(4, 6):
                probabilities(h)
            take(BV1, 0, v[:, 0, COLS:D], v_act)
            for h in range(6, 8):
                probabilities(h)
            act.wait_ge(p_ready, HEADS)
            for hp in range(4):
                for h in (2 * hp, 2 * hp + 1):
                    act.wait_ge(at_ps, h + 1)
                    nc.scalar.activation(aT[:, h % 2, 0:3, :].rearrange("p s n -> p (s n)"), ps[:, h % 2, 0:3 * P],
                                         ACT.Copy).then_inc(at_ready, 1)
                if hp:
                    heads_out(4 + hp - 1)
            heads_out(7)
            root(next(roots), 2 * HEADS)
            transposed(4, lambda k: pcol[:, 24:25])
            root(next(roots), TT)
            transposed(5)
            reload_ln(3)
            router_exp(1)
            moe(1)
            root(next(roots), TT)

        @block.vector
        def _(dve):
            V = nc.vector
            steps = [0]

            def step(instr):
                steps[0] += 1
                instr.then_inc(dve_step, 1)
                dve.wait_ge(dve_step, steps[0])

            def transposed(call, scale=None):
                for bank in (1, 3):
                    dve.wait_ge(tp_ready, 4 * call + bank + 1)
                    if scale is None:
                        V.tensor_copy(xT[:, 2 * bank:2 * bank + 2, :].rearrange("p k t -> p (k t)"),
                                      ps[:, bank, :]).then_inc(xT_dve, 1)
                    else:
                        for j in range(2):
                            last = V.tensor_scalar(xT[:, 2 * bank + j, :], ps[:, bank, j * T:(j + 1) * T],
                                                   scale(2 * bank + j), None, ALU.mult)
                        last.then_inc(xT_dve, 1)

            def take(n, j, dst, sem_done):
                dve.wait_ge(proj_ready, 2 * n + j + 1)
                V.tensor_copy(dst, ps[:, 4 + 2 * (n % 2) + j, :]).then_inc(sem_done, 1)

            def rstd(i, width):
                dve.wait_ge(root_ready, i + 1)
                var, root, y, t = (rs[:, r, 0:width] for r in range(4))
                step(V.reciprocal(y, root))
                step(V.tensor_tensor(t, y, y, ALU.mult))
                step(V.tensor_tensor(t, t, var, ALU.mult))
                step(V.tensor_scalar(t, t, -0.5, 1.5, ALU.mult, ALU.add))
                return V.tensor_tensor(y, y, t, ALU.mult)

            norms = iter(range(4))
            roots = iter(range(6))

            def layer_norm():
                i = next(norms)
                for t in range(TT):
                    for j in range(2):
                        V.bn_stats(stats[:, t, j, :], x[:, t, j * COLS:(j + 1) * COLS])
                step(V.memset(rs[:, 4, :], 0.0))
                for t in range(TT):
                    last = V.bn_aggr(mv[:, t, :], stats[:, t, :, :].rearrange("p a b -> p (a b)"))
                step(last)
                V.tensor_scalar(rs[:, 0, 0:TT].unsqueeze(2), mv[:, :, 1:2], LN_EPS, None, ALU.add).then_inc(var_ready, 1)
                instr = rstd(next(roots), TT)
                instr.then_inc(ln_stat, 1)
                dve.wait_ge(ln_stat, i + 1)
                dve.wait_ge(ln_in, 32 * (i + 1))
                for t in range(TT):
                    step(V.scalar_tensor_tensor(x[:, t, :], x[:, t, :], mv[:, t, 0:1], ln_gb[:, 0, :],
                                                ALU.subtract, ALU.mult))
                    V.scalar_tensor_tensor(x[:, t, :], x[:, t, :], rs[:, 2, t:t + 1], ln_gb[:, 1, :],
                                           ALU.mult, ALU.add).then_inc(x_done[t], 1)

            def residual_projection(n):
                for j in range(TT):
                    dve.wait_ge(proj_ready, 2 * n + j + 1)
                    cols = x[:, j, (n % 2) * COLS:(n % 2 + 1) * COLS]
                    V.scalar_tensor_tensor(cols, cols, ALPHA, ps[:, 4 + 2 * (n % 2) + j, :],
                                           ALU.mult, ALU.add).then_inc(res_done, 1)

            dve.wait_ge(small_in, 64)
            for i in range(2):
                step(V.tensor_tensor(lam_p[:, i, :], lam_in[:, 2 * i, :], lam_in[:, 2 * i + 1, :], ALU.mult))
                V.reduce_sum(lam[:, i:i + 1], lam_p[:, i, :], axis=AX.X).then_inc(lam_sum_ready, 1)
            dve.wait_ge(pcol_ready, 1)
            step(V.tensor_copy(pcol[:, :], ps[:, 7, 0:25]))
            a0, a1 = pcol[:, 0:8], pcol[:, 8:16]
            step(V.tensor_tensor(rs[:, 0, 0:8], a0, a1, ALU.max))
            step(V.tensor_tensor(lb[:, 0:8], a0, rs[:, 0, 0:8], ALU.subtract))
            V.tensor_tensor(lb[:, 8:16], a1, rs[:, 0, 0:8], ALU.subtract).then_inc(pcol_ready, 1)
            dve.wait_ge(lam_exp_ready, 1)
            step(V.tensor_tensor(rs[:, 0, 0:8], lb[:, 0:8], lb[:, 8:16], ALU.add))
            step(V.reciprocal(rs[:, 1, 0:8], rs[:, 0, 0:8]))
            step(V.tensor_tensor(lb[:, 0:8], lb[:, 0:8], rs[:, 1, 0:8], ALU.mult))
            step(V.tensor_scalar(lb[:, 8:16], lb[:, 0:8], -1.0, 1.0, ALU.mult, ALU.add))
            step(V.tensor_scalar(pcol[:, 24:25], pcol[:, 24:25], 1.0 - LAMBDA_INIT, None, ALU.mult))
            dve.wait_ge(lam_exp_ready, 2)
            step(V.tensor_tensor(lam[:, 5:6], lam[:, 3:4], lam[:, 2:3], ALU.subtract))
            step(V.tensor_scalar(lam[:, 4:5], lam[:, 5:6], -LAMBDA_INIT, None, ALU.add))

            dve.wait_ge(consts_ready, 4)
            transposed(0)
            for n in (V0, V1):
                take(n, 1, v[:, 1, n * COLS:(n + 1) * COLS], v_dve)

            def chunks_of(ap):
                return ap.rearrange("p (c n) -> p c n", n=CHUNK)

            def state_out(hp):
                dve.wait_ge(st_ps, hp + 1)
                V.tensor_copy(state[:, :, :].rearrange("p h d -> p (h d)"), ps[:, 2, 0:2 * P]).then_inc(st_ready, 1)

            for hp in range(4):
                dve.wait_ge(sg_ready, hp + 1)
                if hp:
                    dve.wait_ge(k_ready, hp)
                for h in range(2):
                    at = 2 * hp + h
                    last = V.tensor_scalar(f[:, h * T:(h + 1) * T], sg[:, h * T:(h + 1) * T],
                                           lb[:, 8 + at:9 + at], lb[:, at:at + 1], ALU.mult, ALU.add)
                last.then_inc(f_ready, 1)
                dve.wait_ge(f_ready, hp + 1)
                V.tensor_scalar(kk, f, -1.0, 1.0, ALU.mult, ALU.add).then_inc(kk_ready, 1)
                dve.wait_ge(lf_ready, hp + 1)
                step(V.tensor_tensor_scan(b, seg[:, :], lf, 0.0, ALU.mult, ALU.add))
                bc = chunks_of(b)
                V.tensor_tensor(chunks_of(d1), bc, bc[:, :, CHUNK // 2 - 1:CHUNK // 2].to_broadcast([P, 8, CHUNK]),
                                ALU.subtract)
                V.tensor_tensor(chunks_of(d2), bc[:, :, CHUNK - 1:CHUNK].to_broadcast([P, 8, CHUNK]), bc,
                                ALU.subtract).then_inc(d_ready, 1)
                dve.wait_ge(ex_ready, hp + 1)
                dve.wait_ge(proj_ready, 2 * HP[hp] + 2)
                if hp:
                    dve.wait_ge(sc_ready, hp)
                q = ps[:, 4 + 2 * (HP[hp] % 2) + 1, :]
                V.tensor_tensor(qe, q, e1, ALU.mult)
                V.tensor_tensor(qb, q, e3, ALU.mult).then_inc(q_used, 1)
                dve.wait_ge(q_used, hp + 1)
                if hp >= 2:
                    dve.wait_ge(o_ps, hp - 1)
                for h in range(2):
                    at = h * T + P
                    V.tensor_copy(qbs[:, hp % 2, h, 0:CHUNK], qb[:, at:at + CHUNK])
                    last = V.tensor_scalar(qbs[:, hp % 2, h, CHUNK:P], qb[:, at + CHUNK:at + P],
                                           e3[:, at + CHUNK - 1:at + CHUNK], None, ALU.mult)
                last.then_inc(q_ready, 1)
                if hp:
                    state_out(hp - 1)
                dve.wait_ge(sc_ready, hp + 1)
                V.copy_predicated(scm.rearrange("p (u t) -> p u t", t=P),
                                  causal[:, :].unsqueeze(1).to_broadcast([P, 4, P]),
                                  ps[:, 0, :].rearrange("p (u t) -> p u t", t=P)).then_inc(scm_ready, 1)
            state_out(3)

            def rms(call, pairs):
                dve.wait_ge(o_ready, pairs)
                V.tensor_scalar(rs[:, 0, :], ss[:, :], 1.0 / P, RMS_EPS, ALU.mult, ALU.add).then_inc(var_ready, 1)
                step(rstd(call, 2 * HEADS))

            def by_head(t):
                return (o[:, t, :].rearrange("p (h d) -> p h d", h=HEADS),
                        rs[:, 2, t * HEADS:(t + 1) * HEADS].unsqueeze(2).to_broadcast([P, HEADS, P]))

            rms(next(roots), 4)
            dve.wait_ge(g_ready, 4)
            for t in range(TT):
                oh, r = by_head(t)
                step(V.tensor_tensor(oh, oh, r, ALU.mult))
                V.tensor_tensor(o[:, t, :], o[:, t, :], g[:, t, :], ALU.mult).then_inc(o_done[t], 1)
            transposed(1, lambda k: pcol[:, 16 + k:17 + k])
            residual_projection(AO0)
            residual_projection(AO1)
            dve.wait_ge(res_done, 4)
            layer_norm()
            transposed(2)

            def route(layer):
                N = TT * E

                def te(ap):
                    return ap.rearrange("p (t e) -> p t e", t=TT)

                def pick_first(src, width, const, tmp, result):
                    n = TT
                    m, eq, val = tmp
                    step(V.reduce_max(m, src, axis=AX.X))
                    step(V.tensor_tensor(eq, src, m.unsqueeze(2).to_broadcast([P, n, width]), ALU.is_equal))
                    step(V.tensor_tensor(val, eq, const.unsqueeze(1).to_broadcast([P, n, width]), ALU.mult))
                    step(V.reduce_max(m, val, axis=AX.X))
                    step(V.tensor_tensor(result, val, m.unsqueeze(2).to_broadcast([P, n, width]), ALU.is_equal))

                lg, ex, probs, sel, ohg4, selm, oh1, oh2, both, pm, tmp_a, tmp_b = (rt[:, i, :] for i in range(12))
                m2 = rg[:, 0, 0:TT]
                dve.wait_ge(logit_ps, layer + 1)
                raw = te(ps[:, XT_BANK, 0:N])
                step(V.reduce_max(m2, raw, axis=AX.X))
                V.tensor_tensor(te(lg), raw, m2.unsqueeze(2).to_broadcast([P, TT, E]), ALU.subtract
                                ).then_inc(logit_ready, 1)
                dve.wait_ge(rexp_ready, layer + 1)
                step(V.reduce_sum(m2, te(ex), axis=AX.X))
                step(V.reciprocal(rg[:, 1, 0:TT], m2))
                step(V.tensor_tensor(te(probs), te(ex), rg[:, 1, 0:TT].unsqueeze(2).to_broadcast([P, TT, E]), ALU.mult))
                step(V.tensor_tensor(te(sel), te(probs), router_bias[:, :].unsqueeze(1).to_broadcast([P, TT, E]), ALU.add))
                quad = sel.rearrange("p (g a b) -> p g a b", a=2, b=2)
                NG = TT * GROUPS
                hi = rg[:, 2, 0:2 * NG].rearrange("p (g a) -> p g a", a=2)
                lo = rg[:, 3, 0:2 * NG].rearrange("p (g a) -> p g a", a=2)
                V.tensor_tensor(hi, quad[:, :, :, 0], quad[:, :, :, 1], ALU.max)
                step(V.tensor_tensor(lo, quad[:, :, :, 0], quad[:, :, :, 1], ALU.min))
                best, next1, next2, gs = (rg[:, i, 0:NG] for i in (4, 5, 6, 7))
                V.tensor_tensor(best, hi[:, :, 0], hi[:, :, 1], ALU.max)
                V.tensor_tensor(next1, hi[:, :, 0], hi[:, :, 1], ALU.min)
                step(V.tensor_tensor(next2, lo[:, :, 0], lo[:, :, 1], ALU.max))
                step(V.tensor_tensor(next1, next1, next2, ALU.max))
                step(V.tensor_tensor(gs, best, next1, ALU.add))

                def tg(ap):
                    return ap.rearrange("p (t g) -> p t g", t=TT)

                ohg = rg[:, 8, 0:NG]
                pick_first(tg(gs), GROUPS, first_g[:, :], (m2, tg(rg[:, 9, 0:NG]), tg(rg[:, 10, 0:NG])), tg(ohg))
                g4 = ohg.unsqueeze(2).to_broadcast([P, NG, 4])
                pen = rg[:, 11, 0:NG]
                V.tensor_scalar(pen, ohg, BIG, -BIG, ALU.mult, ALU.add)
                step(V.tensor_tensor(tmp_a.rearrange("p (g e) -> p g e", e=4),
                                     sel.rearrange("p (g e) -> p g e", e=4), g4, ALU.mult))
                step(V.tensor_tensor(selm.rearrange("p (g e) -> p g e", e=4), tmp_a.rearrange("p (g e) -> p g e", e=4),
                                     pen.unsqueeze(2).to_broadcast([P, NG, 4]), ALU.add))
                pick_first(te(selm), E, first_e[:, :], (m2, te(tmp_a), te(tmp_b)), te(oh1))
                step(V.scalar_tensor_tensor(selm, oh1, -BIG, selm, ALU.mult, ALU.add))
                pick_first(te(selm), E, first_e[:, :], (m2, te(tmp_a), te(tmp_b)), te(oh2))
                V.tensor_tensor(both, oh1, oh2, ALU.add).then_inc(routed, 1)
                dve.wait_ge(routed, layer + 1)
                step(V.tensor_tensor(pm, probs, both, ALU.mult))
                step(V.reduce_sum(m2, te(pm), axis=AX.X))
                step(V.reciprocal(rg[:, 1, 0:TT], m2))
                V.tensor_tensor(gate[:, :, 0:E], te(pm), rg[:, 1, 0:TT].unsqueeze(2).to_broadcast([P, TT, E]), ALU.mult)
                dve.wait_ge(rank_ps, layer + 1)
                step(V.scalar_tensor_tensor(tmp_a, ps[:, GU_BANK, 0:N], 1.0, both, ALU.add, ALU.mult))
                V.tensor_scalar(slot[:, :, 0:E], te(tmp_a), -1.0, None, ALU.add)
                step(V.tensor_copy(count_f[0:1, 0, :], ps[0:1, GU_BANK, N:N + E]))
                step(V.tensor_scalar(count_f[0:1, 1, :], count_f[0:1, 0, :], float(SLOTS), None, ALU.is_gt))
                for c in range(2, T // SLOTS):
                    step(V.tensor_scalar(count_f[0:1, 2, :], count_f[0:1, 0, :], float(c * SLOTS), None, ALU.is_gt))
                    step(V.tensor_tensor(count_f[0:1, 1, :], count_f[0:1, 1, :], count_f[0:1, 2, :], ALU.add))
                V.tensor_scalar(chunks[:, :], count_f[0:1, 1, :], 1.0, None, ALU.add).then_inc(slots_ready, 1)
                dve.wait_ge(slots_ready, layer + 1)

            def moe(layer):
                def pick_expert(e, index):
                    V.tensor_tensor(pick_ab[e], iota[:, 0:SLOTS].unsqueeze(1).to_broadcast([P, TT, SLOTS]),
                                    slot[:, :, bass.ds(index, 1)].to_broadcast([P, TT, SLOTS]),
                                    ALU.is_equal).then_inc(pick_ready, 1)

                def overflow(count, done, index):
                    with dve.If(count > 1):
                        with dve.Fori(1, count, 1) as c:
                            dve.wait_ge(o_free, done)
                            V.tensor_tensor(o_pick, iota[:, bass.ds(SLOTS * c, SLOTS)].unsqueeze(1)
                                            .to_broadcast([P, TT, SLOTS]),
                                            slot[:, :, bass.ds(index, 1)].to_broadcast([P, TT, SLOTS]),
                                            ALU.is_equal).then_inc(op_ready, 1)
                            dve.wait_ge(op_ready, done)
                            V.tensor_tensor(o_pick_g, o_pick, gate[:, :, bass.ds(index, 1)].to_broadcast([P, TT, SLOTS]),
                                            ALU.mult).then_inc(opg_ready, 1)
                            dve.wait_ge(osilu_ready, done)
                            V.tensor_tensor(o_hT[:, :], ps[:, GU_BANK, FT * SLOTS:2 * FT * SLOTS], silu[:, :],
                                            ALU.mult).then_inc(oh_done, 1)
                            dve.wait_ge(oput_ps, done)
                            V.tensor_copy(o_put[:, :], ps[0:SLOTS, XT_BANK, 0:T]).then_inc(oput_done, 1)
                            dve.wait_ge(oyt_ps, done)
                            V.tensor_copy(o_yT[:, :, :].rearrange("p k s -> p (k s)"), ps[:, YT_BANK, :]
                                          ).then_inc(oyt_done, 1)
                            dve.wait_ge(oys_ps, done)
                            V.tensor_copy(o_ys[:, 0:COLS], ps[0:SLOTS, YS_BANK, :])
                            V.tensor_copy(o_ys[:, COLS:D], ps[0:SLOTS, GU_BANK, :]).then_inc(oys_done, 1)
                            dve.reg_add(done, done, 1)

                def combine(index):
                    dve.wait_ge(ys_ps, 2 * index + 1)
                    V.tensor_copy(ys[:, 0:COLS], ps[:, YS_BANK, :]).then_inc(ys_done, 1)
                    dve.wait_ge(put_ps, index + 1)
                    V.tensor_copy(put[:, :], ps[:, YT_BANK, 0:T]).then_inc(put_done, 1)
                    dve.wait_ge(ys_ps, 2 * index + 2)
                    V.tensor_copy(ys[:, COLS:D], ps[:, YS_BANK, :]).then_inc(ys_done, 1)

                V.memset(yT[:, :, :, :], 0.0).then_inc(yt_done, 1)
                V.memset(hT[:, :, :], 0.0).then_inc(h_done, 1)
                for e in range(2):
                    pick_expert(e, e)
                with dve.Fori(0, PAIRS, 1) as i:
                    count_a = dve.value_load(chunks[0:1, bass.ds(2 * i, 1)], min_val=0, max_val=T // SLOTS)
                    count_b = dve.value_load(chunks[0:1, bass.ds(2 * i + 1, 1)], min_val=0, max_val=T // SLOTS)
                    for e, count in enumerate((count_a, count_b)):
                        overflow(count, done, 2 * i + e)
                        n = 2 * (PAIRS * layer + i) + 1 + e
                        dve.wait_ge(silu_ready, n)
                        V.tensor_tensor(hT[:, e, :], ps[:, GU_BANK, FT * SLOTS:2 * FT * SLOTS], silu[:, :],
                                        ALU.mult).then_inc(h_done, 1)
                        if e == 0:
                            combine((PAIRS + 1) * layer + i)
                        dve.wait_ge(pickg_ready, (PAIRS + 1) * layer + i + 2)
                        pick_expert(e, 2 * i + 2 + e)
                        dve.wait_ge(yt_ps, n)
                        V.tensor_copy(yT[:, :, e, :], ps[:, YT_BANK, :].rearrange("p (k s) -> p k s", s=SLOTS)
                                      ).then_inc(yt_done, 1)
                combine((PAIRS + 1) * layer + PAIRS)
                dve.wait_ge(acc_ps, (PAIRS + 1) * (layer + 1))
                for t in range(TT):
                    for j in range(2):
                        cols = x[:, t, j * COLS:(j + 1) * COLS]
                        last = V.scalar_tensor_tensor(cols, cols, ALPHA, ps[:, 2 * t + j, :], ALU.mult, ALU.add)
                step(last)

            done = dve.alloc_register("dve_done")
            dve.reg_mov(done, 1)
            dve.wait_ge(router_in, 32)
            route(0)
            moe(0)
            layer_norm()
            transposed(3)

            def take_kq(i):
                dst = (kT, qT)[i % 2]
                take((K0, Q0, K1, Q1)[i], 1, dst[:, 4 * (i // 2) + 2:4 * (i // 2) + 4, :].rearrange("p h t -> p (h t)"),
                     kq_dve)

            def masked_scores(h):
                u = h % 2
                dve.wait_ge(s_ps, h + 1)
                if h >= 2:
                    dve.wait_ge(p_ready, h - 1)
                V.tensor_tensor(s_in[:, u, :, 0:3 * P], ps[:, 2 * u:2 * u + 2, 0:3 * P],
                                amask[:, :].unsqueeze(1).to_broadcast([P, 2, 3 * P]), ALU.add).then_inc(s_ready_raw, 1)
                dve.wait_ge(s_ready_raw, h + 1)
                V.reduce_max(amx[:, u, 0:2], s_in[:, u, :, 0:P], axis=AX.X)
                step(V.reduce_max(amx[:, u, 2:4], s_in[:, u, :, P:3 * P], axis=AX.X))
                V.tensor_scalar(amx[:, u, :], amx[:, u, :], -SCALE, None, ALU.mult).then_inc(s_ready, 1)

            def weights(h):
                u = h % 2
                dve.wait_ge(p_ready, h + 1)
                step(V.reciprocal(arec[:, u, :], asum[:, u, :]))
                r = arec[:, u, :].rearrange("p (t c) -> p t c", c=2)
                step(V.tensor_scalar(r[:, :, 1:2], r[:, :, 1:2], lam[:, 4:5], None, ALU.mult))
                spans = ((0, 1), (1, 3))

                def tiles(c, lo, hi):
                    return s_ex[:, u, c, lo * P:hi * P].rearrange("p (s n) -> p s n", n=P)

                a = o3[:, :, h * P:(h + 1) * P]
                for t, (lo, hi) in enumerate(spans):
                    last = V.tensor_scalar(a[:, lo:hi, :], tiles(0, lo, hi), arec[:, u, 2 * t:2 * t + 1],
                                           None, ALU.mult)
                step(last)
                for t, (lo, hi) in enumerate(spans):
                    last = V.scalar_tensor_tensor(a[:, lo:hi, :], tiles(1, lo, hi), arec[:, u, 2 * t + 1:2 * t + 2],
                                                  a[:, lo:hi, :], ALU.mult, ALU.add)
                last.then_inc(a_ready, 1)

            take_kq(0)
            take_kq(1)
            masked_scores(0)
            for h in range(1, HEADS):
                masked_scores(h)
                if h == 1:
                    take_kq(2)
                if h == 6:
                    take(BV1, 1, v[:, 1, COLS:D], v_dve)
                weights(h - 1)
                if h == 2:
                    take_kq(3)
                if h == 4:
                    take(BV0, 1, v[:, 1, 0:COLS], v_dve)
            weights(HEADS - 1)
            rms(next(roots), 8)
            for t in range(TT):
                oh, r = by_head(t)
                V.tensor_tensor(oh, oh, r, ALU.mult).then_inc(o_done[t], 1)
            transposed(4, lambda k: pcol[:, 24:25])
            residual_projection(BO0)
            residual_projection(BO1)
            dve.wait_ge(res_done, 8)
            layer_norm()
            transposed(5)
            route(1)
            moe(1)
            layer_norm()

        @block.tensor
        def _(pe):
            mm = nc.tensor.matmul

            def transposes(call, src):
                for t in range(TT):
                    for k in range(KT):
                        at = (k % 2) * T + t * P
                        last = nc.tensor.transpose(ps[:, k // 2, at:at + P], src[:, t, k * P:(k + 1) * P], ident[:, :])
                        if t == 1 and k % 2:
                            last.then_inc(tp_ready, 1)
                    if t == 0:
                        yield

            def transpose_all(call, src, ready, value):
                pe.wait_ge(ready[0], value)
                for _ in transposes(call, src):
                    pe.wait_ge(ready[1], value)
                pe.wait_ge(xT_act, 2 * (call + 1))
                pe.wait_ge(xT_dve, 2 * (call + 1))

            def free(n, j):
                if (n - 2, j) in taken and n not in (K0, Q0):
                    pe.wait_ge(*taken[n - 2, j])

            def arrive(n):
                pe.wait_ge(dense_in[n % RING], 32 * dense_use(n))

            def rows(n, j):
                free(n, j)
                for k in range(KT):
                    last = mm(ps[:, 4 + 2 * (n % 2) + j, :], xT[:, k, j * P:(j + 1) * P], dense[:, n % RING, k, :],
                              start=k == 0, stop=k == KT - 1)
                last.then_inc(proj_ready, 1)

            def columns(n, j):
                free(n, j)
                for i in range(2):
                    c = (2 * j + i) * P
                    for k in range(KT):
                        last = mm(ps[:, 4 + 2 * (n % 2) + j, i * T:(i + 1) * T], dense[:, n % RING, k, c:c + P],
                                  xT[:, k, :], start=k == 0, stop=k == KT - 1)
                last.then_inc(proj_ready, 1)

            pe.wait_ge(consts_ready, 1)
            pe.wait_ge(small_in, 64)
            nc.tensor.transpose(ps[:, 7, 0:25], prow[:, :], ident[0:25, 0:25]).then_inc(pcol_ready, 1)

            pe.wait_ge(x_in, 32)
            for _ in transposes(0, x):
                pass
            pe.wait_ge(xT_act, 2)
            pe.wait_ge(xT_dve, 2)
            pe.wait_ge(pcol_ready, 2)

            def scores(hp):
                pe.wait_ge(q_ready, hp + 1)
                pe.wait_ge(k_ready, hp + 1)
                if hp:
                    pe.wait_ge(scm_ready, hp)
                    pe.wait_ge(kbt_ready, hp)
                for u in range(4):
                    at = u * P
                    mm(ps[:, 0, at:at + P], ke[:, at:at + P], qe[:, at:at + P], start=True, stop=True)
                    last = mm(ps[0:CHUNK, 0, at + CHUNK:at + P], kb[:, at:at + CHUNK], qb[:, at + CHUNK:at + P],
                              start=True, stop=True)
                last.then_inc(sc_ready, 1)
                for h in range(2):
                    last = nc.tensor.transpose(ps[:, 1, h * P:(h + 1) * P], kbs[:, h, :], ident[:, :])
                last.then_inc(kbt_ps, 1)

            def states(hp):
                pe.wait_ge(kbt_ready, hp + 1)
                if hp == 0:
                    pe.wait_ge(v_act, 2)
                    pe.wait_ge(v_dve, 2)
                else:
                    pe.wait_ge(st_ready, hp)
                for h in range(2):
                    head = (2 * hp + h) * P
                    last = mm(ps[:, 2, h * P:(h + 1) * P], kbT[:, h, :], v[:, 0, head:head + P], start=True, stop=True)
                last.then_inc(st_ps, 1)

            def outputs(hp):
                pe.wait_ge(scm_ready, hp + 1)
                pe.wait_ge(st_ready, hp + 1)
                if hp:
                    pe.wait_ge(o_ready, hp)
                for h in range(2):
                    head = (2 * hp + h) * P
                    for t in range(TT):
                        at = (2 * h + t) * P
                        last = mm(ps[:, 3, at:at + P], scm[:, at:at + P], v[:, t, head:head + P],
                                  start=True, stop=t == 0)
                        if t:
                            last = mm(ps[:, 3, at:at + P], qbs[:, hp % 2, h, :], state[:, h, :], start=False, stop=True)
                last.then_inc(o_ps, 1)

            for n in (V0, V1):
                arrive(n)
                rows(n, 0)
                rows(n, 1)
            arrive(HP0)
            columns(HP0, 0)
            columns(HP0, 1)
            for hp, n in enumerate((HP1, HP2, HP3, G0, G1)):
                part = columns if n in HP else rows
                arrive(n)
                part(n, 0)
                if hp >= 1:
                    states(hp - 1)
                part(n, 1)
                if hp >= 1:
                    outputs(hp - 1)
                if hp < 4:
                    scores(hp)
            transpose_all(1, o, o_done, 1)
            for n in (AO0, AO1):
                arrive(n)
                rows(n, 0)
                rows(n, 1)

            def moe(layer):
                pe.wait_ge(router_in, 32)
                for t in range(TT):
                    for k in range(KT):
                        last = mm(ps[:, XT_BANK, t * E:(t + 1) * E], xT[:, k, t * P:(t + 1) * P], router[:, k, :],
                                  start=k == 0, stop=k == KT - 1)
                last.then_inc(logit_ps, 1)
                for bank in range(4):
                    mm(ps[:, bank, :], zeros16[:, :], zeros16[:, :].unsqueeze(1).to_broadcast([P, COLS // P, P]),
                       start=True, stop=True)
                pe.wait_ge(routed, layer + 1)
                both = rt[:, 8, :]
                N = TT * E
                mm(ps[:, GU_BANK, 0:E], later[:, :], both[:, 0:E], start=True, stop=True)
                mm(ps[:, GU_BANK, E:N], later[:, :], both[:, E:N], start=True, stop=False)
                mm(ps[:, GU_BANK, E:N], ones[:, :], both[:, 0:E], start=False, stop=True)
                mm(ps[:, GU_BANK, N:N + E], ones[:, :], both[:, 0:E], start=True, stop=False)
                mm(ps[:, GU_BANK, N:N + E], ones[:, :], both[:, E:N], start=False, stop=True).then_inc(rank_ps, 1)

                def gather(onehot):
                    for k in range(KT):
                        for t in range(TT):
                            last = mm(ps[:, XT_BANK, k * SLOTS:(k + 1) * SLOTS], x[:, t, k * P:(k + 1) * P],
                                      onehot[:, t, :], start=t == 0, stop=t == TT - 1)
                    return last

                def gate_up(e, tokens):
                    for w, base in ((w_gate, 0), (w_up, FT)):
                        for j in range(FT):
                            at = (base + j) * SLOTS
                            for k in range(KT):
                                last = mm(ps[:, GU_BANK, at:at + SLOTS], w[:, e, k, j * P:(j + 1) * P],
                                          tokens[:, k, :], start=k == 0, stop=k == KT - 1)
                    return last

                def down(e, h):
                    for k in range(KT):
                        for j in range(FT):
                            last = mm(ps[:, YT_BANK, k * SLOTS:(k + 1) * SLOTS], w_down[:, e, j, k * P:(k + 1) * P],
                                      h[:, j * SLOTS:(j + 1) * SLOTS], start=j == 0, stop=j == FT - 1)
                    return last

                def add_up(matrix, rows_):
                    for t in range(TT):
                        for j in range(2):
                            last = mm(ps[:, 2 * t + j, :], matrix[:, t * P:(t + 1) * P], rows_[:, j * COLS:(j + 1) * COLS],
                                      start=False, stop=True, skip_group_check=True)
                    return last

                def overflow(e, count, pair, done):
                    with pe.If(count > 1):
                        with pe.Fori(1, count, 1):
                            g1 = (2 * PAIRS + 1) * layer
                            pe.wait_ge(xe_ready, g1 + 2 * i + 1 + e)
                            pe.wait_ge(op_ready, done)
                            gather(o_pick).then_inc(oxe_ps, 1)
                            pe.wait_ge(gate_in[e], 16 * pair + 16)
                            pe.wait_ge(up_in[e], 16 * pair + 16)
                            pe.wait_ge(h_done, g1 + 2 * i + 1 + e)
                            pe.wait_ge(oxe_ready, done)
                            gate_up(e, o_xe).then_inc(ogu_ps, 1)
                            pe.wait_ge(opg_ready, done)
                            pe.wait_ge(consts_ready, 1)
                            for t in range(TT):
                                last = mm(ps[0:SLOTS, XT_BANK, t * P:(t + 1) * P], o_pick_g[:, t, :], ident[:, :],
                                          start=True, stop=True)
                            last.then_inc(oput_ps, 1)
                            pe.wait_ge(down_in[e], 16 * pair + 16)
                            pe.wait_ge(yt_done, g1 + 2 * i + 1 + e)
                            pe.wait_ge(oh_done, done)
                            down(e, o_hT).then_inc(oyt_ps, 1)
                            pe.wait_ge(oyt_done, done)
                            if e:
                                pe.wait_ge(ys_done, 2 * ((PAIRS + 1) * layer + i) + 2)
                            for k in range(KT):
                                bank = (YS_BANK, GU_BANK)[k // 4]
                                last = mm(ps[0:SLOTS, bank, (k % 4) * P:(k % 4 + 1) * P], o_yT[:, k, :], ident[:, :],
                                          start=True, stop=True)
                            last.then_inc(oys_ps, 1)
                            pe.wait_ge(oput_done, done)
                            pe.wait_ge(oys_done, done)
                            add_up(o_put, o_ys).then_inc(o_free, 1)
                            pe.reg_add(done, done, 1)

                def turn(index, half):
                    for k in range(4):
                        last = nc.tensor.transpose(ps[:, YS_BANK, k * P:(k + 1) * P],
                                                   yT[:, 4 * half + k, :, :].rearrange("p e s -> p (e s)"), ident[:, :])
                    last.then_inc(ys_ps, 1)

                def turn_picks():
                    for t in range(TT):
                        last = nc.tensor.transpose(ps[:, YT_BANK, t * P:(t + 1) * P],
                                                   pick_g[:, t, :, :].rearrange("p e s -> p (e s)"), ident[:, :])
                    last.then_inc(put_ps, 1)

                g0 = (2 * PAIRS + 1) * layer
                c0 = (PAIRS + 1) * layer
                k0 = (2 * PAIRS + 2) * layer
                pe.wait_ge(slots_ready, layer + 1)
                pe.wait_ge(pick_ready, k0 + 1)
                gather(pick_ab[0]).then_inc(xe_ps, 1)
                with pe.Fori(0, PAIRS, 1) as i:
                    count_a = pe.value_load(chunks[0:1, bass.ds(2 * i, 1)], min_val=0, max_val=T // SLOTS)
                    count_b = pe.value_load(chunks[0:1, bass.ds(2 * i + 1, 1)], min_val=0, max_val=T // SLOTS)
                    pair = PAIRS * layer + i
                    overflow(0, count_a, pair, done)
                    pe.wait_ge(gate_in[0], 16 * pair + 16)
                    pe.wait_ge(up_in[0], 16 * pair + 16)
                    pe.wait_ge(xe_ready, g0 + 2 * i + 1)
                    pe.wait_ge(h_done, g0 + 2 * i + 1)
                    gate_up(0, xe[0]).then_inc(gu_ps, 1)
                    pe.wait_ge(yt_done, g0 + 2 * i + 1)
                    turn(c0 + i, 0)
                    pe.wait_ge(pickg_ready, c0 + i + 1)
                    turn_picks()
                    pe.wait_ge(pick_ready, k0 + 2 * i + 2)
                    gather(pick_ab[1]).then_inc(xe_ps, 1)
                    pe.wait_ge(ys_done, 2 * (c0 + i) + 1)
                    turn(c0 + i, 1)
                    pe.wait_ge(down_in[0], 16 * pair + 16)
                    pe.wait_ge(h_done, g0 + 2 * i + 2)
                    pe.wait_ge(put_done, c0 + i + 1)
                    down(0, hT[:, 0, :]).then_inc(yt_ps, 1)
                    overflow(1, count_b, pair, done)
                    pe.wait_ge(gate_in[1], 16 * pair + 16)
                    pe.wait_ge(up_in[1], 16 * pair + 16)
                    pe.wait_ge(xe_ready, g0 + 2 * i + 2)
                    gate_up(1, xe[1]).then_inc(gu_ps, 1)
                    pe.wait_ge(ys_done, 2 * (c0 + i) + 2)
                    add_up(put, ys).then_inc(acc_ps, 1)
                    pe.wait_ge(pick_ready, k0 + 2 * i + 3)
                    gather(pick_ab[0]).then_inc(xe_ps, 1)
                    pe.wait_ge(down_in[1], 16 * pair + 16)
                    pe.wait_ge(h_done, g0 + 2 * i + 3)
                    pe.wait_ge(yt_done, g0 + 2 * i + 2)
                    down(1, hT[:, 1, :]).then_inc(yt_ps, 1)
                pe.wait_ge(yt_done, g0 + 2 * PAIRS + 1)
                turn(c0 + PAIRS, 0)
                pe.wait_ge(pickg_ready, c0 + PAIRS + 1)
                turn_picks()
                pe.wait_ge(ys_done, 2 * (c0 + PAIRS) + 1)
                turn(c0 + PAIRS, 1)
                pe.wait_ge(put_done, c0 + PAIRS + 1)
                pe.wait_ge(ys_done, 2 * (c0 + PAIRS) + 2)
                add_up(put, ys).then_inc(acc_ps, 1)

            done = pe.alloc_register("pe_done")
            pe.reg_mov(done, 1)
            pe.sem_inc(o_free, 1)
            transpose_all(2, x, x_done, 1)
            moe(0)

            transpose_all(3, x, x_done, 2)

            def attention_scores(h):
                u = h % 2
                if h >= 2:
                    pe.wait_ge(s_ready_raw, h - 1)
                for c in range(2):
                    part = slice(c * DH, (c + 1) * DH)
                    mm(ps[:, 2 * u + c, 0:P], qT[part, h, 0:P], kT[part, h, 0:P], start=True, stop=True)
                    last = mm(ps[:, 2 * u + c, P:3 * P], qT[part, h, P:T], kT[part, h, :], start=True, stop=True)
                last.then_inc(s_ps, 1)

            def block_of(n, part, between=()):
                arrive(n)
                part(n, 0)
                for h in between[:1]:
                    attention_scores(h)
                part(n, 1)
                for h in between[1:]:
                    attention_scores(h)

            block_of(K0, columns)
            block_of(Q0, columns)
            arrive(K1)
            columns(K1, 0)
            pe.wait_ge(kq_act, 2)
            pe.wait_ge(kq_dve, 2)
            attention_scores(0)
            attention_scores(1)
            columns(K1, 1)
            block_of(Q1, columns, (2, 3))
            arrive(BV0)
            rows(BV0, 0)
            pe.wait_ge(kq_act, 4)
            pe.wait_ge(kq_dve, 4)
            attention_scores(4)
            rows(BV0, 1)
            attention_scores(5)
            block_of(BV1, rows, (6, 7))
            pe.wait_ge(v_act, 4)
            pe.wait_ge(v_dve, 4)

            def attention_turn(h):
                pe.wait_ge(a_ready, h + 1)
                if h == 0:
                    pe.wait_ge(s_ready_raw, HEADS)
                if h >= 2:
                    pe.wait_ge(at_ready, h - 1)
                for s in range(3):
                    last = nc.tensor.transpose(ps[:, h % 2, s * P:(s + 1) * P], o3[:, s, h * P:(h + 1) * P],
                                               ident[:, :])
                last.then_inc(at_ps, 1)

            def attention_out(h):
                hp, u = divmod(h, 2)
                pe.wait_ge(at_ready, h + 1)
                if hp >= 2 and u == 0:
                    pe.wait_ge(o_ready, 4 + hp - 1)
                bank = 2 + hp % 2
                cols = slice(h * P, (h + 1) * P)
                at = 2 * u * P
                mm(ps[:, bank, at:at + P], aT[:, u, 0, :], v[:, 0, cols], start=True, stop=True)
                mm(ps[:, bank, at + P:at + 2 * P], aT[:, u, 1, :], v[:, 0, cols], start=True, stop=False)
                last = mm(ps[:, bank, at + P:at + 2 * P], aT[:, u, 2, :], v[:, 1, cols], start=False, stop=True)
                if u:
                    last.then_inc(o_ps, 1)

            attention_turn(0)
            for h in range(HEADS):
                if h + 1 < HEADS:
                    attention_turn(h + 1)
                attention_out(h)
            transpose_all(4, o, o_done, 2)
            for n in (BO0, BO1):
                arrive(n)
                rows(n, 0)
                rows(n, 1)
            transpose_all(5, x, x_done, 3)
            moe(1)


def kernel(**inputs):
    import numpy as _np
    import concourse.bacc as _bacc
    from concourse import mybir as _mybir
    from concourse.bass_utils import run_bass_kernel_spmd as _run

    nc = _bacc.Bacc("TRN2", target_bir_lowering=False, num_devices=1, dynamic_dma_scratch_size=1024)
    arrays, aps = {}, {}
    for name, a in inputs.items():
        a = _np.ascontiguousarray(a)
        arrays[f"in_{name}"] = a
        aps[name] = nc.dram_tensor(f"in_{name}", a.shape, _mybir.dt.from_np(a.dtype), kind="ExternalInput").ap()
    out = nc.dram_tensor("out", (1, T, D), _mybir.dt.float32, kind="ExternalOutput").ap()
    build(nc, aps, out)
    r = _run(nc, [arrays], core_ids=[0])
    return r.results[0]["out"]
```

```python
import math
from contextlib import ExitStack

import concourse.bass as bass
from concourse import mybir

F32 = mybir.dt.float32
BF16 = mybir.dt.bfloat16
I32 = mybir.dt.int32
ALU = mybir.AluOpType
ACT = mybir.ActivationFunctionType
AX = mybir.AxisListType

P = 128
D = 1024
T = 256
TT = T // P
KT = D // P
LAYERS = 2
HEADS = 8
CHUNK = 64
DH = 64
E = 16
GROUPS = 4
F = 512
FT = F // P
SLOTS = 64
PAIRS = E // 2
COLS = 512
ALPHA = (2.0 * LAYERS) ** 0.25
LAMBDA_INIT = 0.8 - 0.6 * math.exp(-0.3 * 1)
LN_EPS = 1e-5
RMS_EPS = 1e-6
BIG = 1e30
SCALE = DH ** -0.5

RING = 2
(V0, V1, HP0, HP1, HP2, HP3, G0, G1, AO0, AO1,
 K0, Q0, K1, Q1, BV0, BV1, BO0, BO1) = range(18)
HP = [HP0, HP1, HP2, HP3]
BANK_A, BANK_B, BANK_C, BANK_D = 4, 5, 6, 7


def build(nc, ins, out):
    ctx = ExitStack()
    with ctx:
        def sb(name, shape, dt=F32):
            return ctx.enter_context(nc.sbuf_tensor(name, shape, dt))

        def sem(name):
            return ctx.enter_context(nc.semaphore(name))

        dense = sb("dense", [P, RING, KT, COLS])
        w_gate = sb("w_gate", [P, 2, KT, F])
        w_up = sb("w_up", [P, 2, KT, F])
        w_down = sb("w_down", [P, 2, FT, D])
        x = sb("x_sb", [P, TT, D])
        xT = sb("xT", [P, KT, T])
        ln_gb = sb("ln_gb", [P, 2, D])
        ident = sb("ident", [P, P])
        causal = sb("causal", [P, P], I32)
        later = sb("later", [P, P])
        ones = sb("ones", [P, P])
        zeros16 = sb("zeros16", [P, P], BF16)
        iota = sb("iota", [P, T])
        seg = sb("seg", [P, 2 * T])
        amask = sb("amask", [P, 3 * P])
        first_g = sb("first_g", [P, GROUPS])
        first_e = sb("first_e", [P, E])
        prow = sb("prow", [25, P])
        pcol = sb("pcol", [P, 25])
        lb = sb("lb", [P, 2 * HEADS])
        lam_in = sb("lam_in", [P, 4, DH])
        lam = sb("lam", [P, 8])
        lam_p = sb("lam_p", [P, 2, DH])
        router = sb("router", [P, KT, E])
        router_bias = sb("router_bias", [P, E])
        stats = sb("stats", [P, TT, 2, 6])
        mv = sb("mv", [P, TT, 2])
        rs = sb("rs", [P, 5, 2 * HEADS])
        ss = sb("ss", [P, 2 * HEADS])
        o3 = sb("o3", [P, 3, D])
        o = o3[:, 0:TT, :]
        scratch = sb("scratch", [P, 2 * TT * D + 12 * 2 * T])
        place = [0]

        def carve(*shape, parts=P):
            size = math.prod(shape)
            ap = scratch[0:parts, place[0]:place[0] + size]
            place[0] += size
            names = "abc"[:len(shape)]
            if len(shape) == 1:
                return ap
            return ap.rearrange(f"p ({' '.join(names)}) -> p {' '.join(names)}", **dict(zip(names, shape)))

        v = carve(TT, D)
        g = carve(TT, D)
        mix = carve(12, 2 * T)
        sg, kk, b, d1, d2, e1, qe, qb, ke, kb, scm, f = (mix[:, i, :] for i in range(12))
        lf, e3, e2, e4 = sg, b, d1, d2
        third = o3[:, 2, :].rearrange("p (a h n) -> p a h n", a=4, h=2)
        kbs, kbT, state = third[:, 0], third[:, 1], third[:, 2]
        qbs = sb("qbs", [P, 2, 2, P])
        iota_i = e1[:, 0:T].bitcast(I32)
        qT = g[:, :, :].rearrange("p a (h t) -> p (a h) t", t=T)
        kT = mix[:, 0:4, :].rearrange("p a (h t) -> p (a h) t", t=T)
        s_in = mix[:, 4:8, :].rearrange("p (u c) n -> p u c n", u=2)
        s_ex = mix[:, 8:12, :].rearrange("p (u c) n -> p u c n", u=2)
        aT = mix[:, 4:6, :].rearrange("p u (s n) -> p u s n", n=P)
        amx = sb("amx", [P, 2, 4])
        asum = sb("asum", [P, 2, 4])
        arec = sb("arec", [P, 2, 4])
        rt = sb("rt", [P, 12, TT * E])
        rg = sb("rg", [P, 12, TT * E])
        slot = sb("slot", [P, TT, E + 2])
        gate = sb("gate", [P, TT, E + 2])
        count_f = sb("count_f", [1, 4, E])
        chunks = sb("chunks", [1, E], I32)
        extra = sb("extra", [1, E], I32)
        place[0] = 0
        pick = carve(TT, 2, SLOTS)
        pick_g = carve(TT, 2, SLOTS)
        xe = carve(KT, 2 * SLOTS)
        silu = carve(F)
        hid = carve(F)
        hT = carve(FT, 2 * SLOTS)
        ys = carve(D)
        put = carve(T)
        o_pick = carve(TT, SLOTS)
        o_pick_g = carve(TT, SLOTS)
        o_xe = carve(KT, SLOTS)
        o_silu = carve(F)
        o_h = carve(F, parts=SLOTS)
        o_hT = carve(FT, SLOTS)
        o_ys = carve(D, parts=SLOTS)
        o_put = carve(T, parts=SLOTS)
        assert place[0] <= scratch.shape[1]

        ps = ctx.enter_context(nc.psum_tensor("ps", [P, 8, COLS], F32))

        x_in = sem("x_in")
        small_in = sem("small_in")
        router_in = sem("router_in")
        ln_in = sem("ln_in")
        dense_in = [sem(f"dense_in{r}") for r in range(RING)]
        gate_in = sem("gate_in")
        up_in = sem("up_in")
        down_in = sem("down_in")
        out_sem = sem("out_sem")
        consts_ready = sem("consts_ready")
        pool_step = sem("pool_step")
        dve_step = sem("dve_step")
        act_step = sem("act_step")
        pcol_ready = sem("pcol_ready")
        lam_exp_ready = sem("lam_exp_ready")
        lam_sum_ready = sem("lam_sum_ready")
        proj_ready = sem("proj_ready")
        tp_ready = sem("tp_ready")
        xT_act = sem("xT_act")
        xT_dve = sem("xT_dve")
        v_act = sem("v_act")
        v_dve = sem("v_dve")
        sg_ready = sem("sg_ready")
        f_ready = sem("f_ready")
        lf_ready = sem("lf_ready")
        d_ready = sem("d_ready")
        kk_ready = sem("kk_ready")
        ex_ready = sem("ex_ready")
        q_used = sem("q_used")
        q_ready = sem("q_ready")
        k_ready = sem("k_ready")
        sc_ready = sem("sc_ready")
        scm_ready = sem("scm_ready")
        kbt_ps = sem("kbt_ps")
        kbt_ready = sem("kbt_ready")
        st_ps = sem("st_ps")
        st_ready = sem("st_ready")
        o_ps = sem("o_ps")
        o_ready = sem("o_ready")
        g_ready = sem("g_ready")
        var_ready = sem("var_ready")
        root_ready = sem("root_ready")
        o_done = [sem(f"o_done{t}") for t in range(TT)]
        res_done = sem("res_done")
        ln_stat = sem("ln_stat")
        x_done = [sem(f"x_done{t}") for t in range(TT)]
        kq_act = sem("kq_act")
        kq_dve = sem("kq_dve")
        s_ps = sem("s_ps")
        s_ready = sem("s_ready")
        s_ready_raw = sem("s_ready_raw")
        p_ready = sem("p_ready")
        a_ready = sem("a_ready")
        at_ps = sem("at_ps")
        at_ready = sem("at_ready")
        logit_ps = sem("logit_ps")
        logit_ready = sem("logit_ready")
        rexp_ready = sem("rexp_ready")
        routed = sem("routed")
        rank_ps = sem("rank_ps")
        slots_ready = sem("slots_ready")
        pick_ready = sem("pick_ready")
        pickg_ready = sem("pickg_ready")
        xe_ps = sem("xe_ps")
        xe_act = sem("xe_act")
        xe_dve = sem("xe_dve")
        gate_ps = sem("gate_ps")
        silu_ready = sem("silu_ready")
        up_ps = sem("up_ps")
        h_ready = sem("h_ready")
        ht_ps = sem("ht_ps")
        ht_ready = sem("ht_ready")
        put_ps = sem("put_ps")
        put_done = sem("put_done")
        yc_ps = sem("yc_ps")
        yd_ps = sem("yd_ps")
        ys_act = sem("ys_act")
        ys_dve = sem("ys_dve")
        acc_ps = sem("acc_ps")
        o_free = sem("o_free")
        op_ready = sem("op_ready")
        opg_ready = sem("opg_ready")
        oxe_ps = sem("oxe_ps")
        oxe_ready = sem("oxe_ready")
        oput_ps = sem("oput_ps")
        oput_done = sem("oput_done")
        ogu_ps = sem("ogu_ps")
        osilu_ready = sem("osilu_ready")
        oh_done = sem("oh_done")
        oht_ps = sem("oht_ps")
        oht_ready = sem("oht_ready")
        oy_ps = sem("oy_ps")
        oys_done = sem("oys_done")

        taken = {}
        for n in (V0, V1):
            taken[n, 0], taken[n, 1] = (v_act, n + 1), (v_dve, n + 1)
        for hp, n in enumerate(HP):
            taken[n, 0], taken[n, 1] = (sg_ready, hp + 1), (q_used, hp + 1)
        for i, n in enumerate((G0, G1)):
            taken[n, 0], taken[n, 1] = (g_ready, 2 * i + 1), (g_ready, 2 * i + 2)
        for i, n in enumerate((AO0, AO1)):
            taken[n, 0], taken[n, 1] = (res_done, 2 * i + 1), (res_done, 2 * i + 2)
        for i, n in enumerate((K0, Q0, K1, Q1)):
            taken[n, 0], taken[n, 1] = (kq_act, i + 1), (kq_dve, i + 1)
        for i, n in enumerate((BV0, BV1)):
            taken[n, 0], taken[n, 1] = (v_act, i + 3), (v_dve, i + 3)

        def dense_use(n):
            return n // RING + 1

        block = ctx.enter_context(nc.Block())

        @block.sync
        def _(sp):
            def cols(w, first):
                return w[:, first:first + COLS].rearrange("(k p) n -> p k n", p=P)

            w_in, kv = ins["a_w_in"][0], ins["kv_w"]
            w_q, a_out, b_out = ins["b_w_q"][0], ins["a_w_out"][0], ins["b_w_out"][0]
            source = {V0: (w_in, 2 * D), V1: (w_in, 2 * D + COLS), G0: (w_in, 3 * D), G1: (w_in, 3 * D + COLS),
                      AO0: (a_out, 0), AO1: (a_out, COLS), K0: (kv, 0), K1: (kv, COLS), Q0: (w_q, 0),
                      Q1: (w_q, COLS), BV0: (kv, D), BV1: (kv, D + COLS), BO0: (b_out, 0), BO1: (b_out, COLS)}

            def load_dense(n):
                if n >= RING:
                    sp.wait_ge(proj_ready, 2 * (n - RING) + 2)
                r = n % RING
                if n in HP:
                    half = COLS // 2
                    first = (n - HP0) * half
                    for i, at in enumerate((D + first, first)):
                        sp.dma_start(dense[:, r, :, i * half:(i + 1) * half],
                                     w_in[:, at:at + half].rearrange("(k p) n -> p k n", p=P)
                                     ).then_inc(dense_in[r], 16)
                else:
                    w = cols(*source[n])
                    for half in (slice(0, KT // 2), slice(KT // 2, KT)):
                        sp.dma_start(dense[:, r, half, :], w[:, half, :]).then_inc(dense_in[r], 16)

            wg, wu, wd = ins["moe_w_gate"], ins["moe_w_up"], ins["moe_w_down"]

            def load_matrix(layer, which, e, index):
                src, dst, arrived = ((wg, w_gate, gate_in), (wu, w_up, up_in), (wd, w_down, down_in))[which]
                sp.dma_start(dst[:, e, :, :], src[layer, bass.ds(index, 1)].rearrange("one (k p) n -> p (one k) n", p=P)
                             ).then_inc(arrived, 16)

            def read_by(which, pairs):
                sp.wait_ge((gate_ps, up_ps, yd_ps)[which], pairs)

            finished = sp.alloc_register("sp_finished")
            sp.reg_mov(finished, 1)

            def count_overflow(pair):
                for e in range(2):
                    count = sp.value_load(extra[0:1, bass.ds(2 * pair + e, 1)], min_val=0, max_val=T // SLOTS)
                    sp.reg_add(finished, finished, count)

            sp.dma_start(x[:, 0, :], ins["x"][0, 0:P, :]).then_inc(x_in, 16)
            sp.dma_start(x[:, 1, :], ins["x"][0, P:T, :]).then_inc(x_in, 16)
            for layer in range(LAYERS):
                blocks = list(range(V0, AO1 + 1)) if layer == 0 else list(range(K0 + RING, BO1 + 1))
                if layer:
                    count_overflow(PAIRS - 1)
                    sp.wait_ge(o_free, finished)
                first = [(which, e) for which in range(3) for e in range(2)]
                for i, n in enumerate(blocks):
                    if (layer or i >= RING) and first:
                        which, e = first.pop(0)
                        if layer:
                            read_by(which, PAIRS)
                        load_matrix(layer, which, e, e)
                    load_dense(n)
                if layer == 0:
                    for n in range(K0, K0 + RING):
                        load_dense(n)
                sp.wait_ge(slots_ready, layer + 1)
                with sp.Fori(1, PAIRS, 1) as p:
                    pairs = PAIRS * layer + p
                    count_overflow(p - 1)
                    for which in range(3):
                        read_by(which, pairs)
                        sp.wait_ge(o_free, finished)
                        for e in range(2):
                            load_matrix(layer, which, e, 2 * p + e)
            for t in range(TT):
                sp.wait_ge(x_done[t], 4)
                sp.dma_start(out[0, t * P:(t + 1) * P, :], x[:, t, :]).then_inc(out_sem, 16)
            sp.wait_ge(out_sem, 16 * TT)

        @block.gpsimd
        def _(pool):
            steps = [0]

            def step(instr):
                steps[0] += 1
                instr.then_inc(pool_step, 1)
                pool.wait_ge(pool_step, steps[0])

            step(pool.memset(ones[:, :], 1.0))
            pool.affine_select(out=ident[:, :], in_=ones[:, :], compare_op=ALU.is_equal, fill=0.0,
                               base=0, pattern=[[-1, P]], channel_multiplier=1).then_inc(consts_ready, 1)
            pool.affine_select(out=later[:, :], in_=ones[:, :], compare_op=ALU.is_gt, fill=0.0,
                               base=0, pattern=[[1, P]], channel_multiplier=-1).then_inc(consts_ready, 1)
            step(pool.memset(causal[:, :], 1))
            step(pool.affine_select(out=causal[:, :], in_=causal[:, :], compare_op=ALU.is_ge, fill=0.0,
                                    base=0, pattern=[[1, P]], channel_multiplier=-1))
            step(pool.memset(seg[:, :], 1.0))
            pool.memset(seg[:, :].rearrange("p (c n) -> p c n", n=CHUNK)[:, :, 0:1], 0.0).then_inc(consts_ready, 1)
            step(pool.memset(amask[:, :], 0.0))
            for at in (0, 2 * P):
                part = amask[:, at:at + P]
                step(pool.affine_select(out=part, in_=part, compare_op=ALU.is_ge, fill=-BIG,
                                        base=0, pattern=[[-1, P]], channel_multiplier=1))
            step(pool.iota(iota_i[:, :], pattern=[[1, T]], base=0, channel_multiplier=0))
            step(pool.tensor_copy(iota[:, :], iota_i[:, :]))
            step(pool.tensor_scalar(first_g[:, :], iota[:, 0:GROUPS], -1.0, float(GROUPS), ALU.mult, ALU.add))
            step(pool.tensor_scalar(first_e[:, :], iota[:, 0:E], -1.0, float(E), ALU.mult, ALU.add))
            step(pool.memset(zeros16[:, :], 0.0))
            step(pool.memset(slot[:, :, :], -1.0))
            step(pool.memset(gate[:, :, :], 0.0))
            pool.memset(scm, 0.0).then_inc(consts_ready, 1)

            for hp in range(4):
                pool.wait_ge(ex_ready, hp + 1)
                pool.wait_ge(kk_ready, hp + 1)
                if hp:
                    pool.wait_ge(kbt_ps, hp)
                pool.tensor_tensor(ke, kk, e2, ALU.mult).then_inc(pool_step, 1)
                pool.tensor_tensor(kb, kk, e4, ALU.mult).then_inc(pool_step, 1)
                steps[0] += 2
                pool.wait_ge(pool_step, steps[0])
                for h in range(2):
                    at = h * T
                    pool.tensor_scalar(kbs[:, h, 0:CHUNK], kb[:, at:at + CHUNK],
                                       e3[:, at + 2 * CHUNK - 1:at + 2 * CHUNK], None, ALU.mult)
                    last = pool.tensor_copy(kbs[:, h, CHUNK:P], kb[:, at + CHUNK:at + P])
                last.then_inc(k_ready, 1)

            for layer in range(LAYERS):
                with pool.Fori(0, PAIRS, 1) as i:
                    pool.wait_ge(put_ps, PAIRS * layer + i + 1)
                    pool.wait_ge(pick_ready, (PAIRS + 1) * layer + i + 1)
                    pool.wait_ge(slots_ready, layer + 1)
                    pool.tensor_tensor(pick_g[:, :, :, :], pick[:, :, :, :],
                                       gate[:, :, bass.ds(2 * i, 2)].unsqueeze(3).to_broadcast([P, TT, 2, SLOTS]),
                                       ALU.mult).then_inc(pickg_ready, 1)

        @block.scalar
        def _(act):
            def load_ln(i):
                layer, which = divmod(i, 2)
                for j, name in enumerate(("g", "b")):
                    row = ins[f"ln{which + 1}_{name}"][layer:layer + 1, :]
                    act.dma_start(ln_gb[:, j, :], row.broadcast_to([P, D])).then_inc(ln_in, 16)

            act.dma_start(prow[0:16, :], ins["a_lb"].rearrange("l (h d) -> (l h) d", d=P)).then_inc(small_in, 16)
            act.dma_start(prow[16:24, :], ins["a_norm_g"][0]).then_inc(small_in, 16)
            act.dma_start(prow[24:25, :], ins["b_subln_g"]).then_inc(small_in, 16)
            act.dma_start(lam_in[:, :, :].rearrange("p a d -> p (a d)"),
                           ins["b_lam"].rearrange("l a d -> l (a d)").broadcast_to([P, 4 * DH])).then_inc(small_in, 16)
            act.dma_start(router[:, :, :], ins["router_w"].rearrange("(k p) e -> p k e", p=P)).then_inc(router_in, 16)
            act.dma_start(router_bias[:, :], ins["router_b"].rearrange("(a e) -> a e", a=1)
                           .broadcast_to([P, E])).then_inc(router_in, 16)
            load_ln(0)

            def reload_ln(i):
                for t in range(TT):
                    act.wait_ge(x_done[t], i)
                load_ln(i)

            def transposed(call, scale=None):
                for i, bank in enumerate((0, 2)):
                    act.wait_ge(tp_ready, 4 * call + bank + 1)
                    if scale is None:
                        nc.scalar.activation(xT[:, 2 * bank:2 * bank + 2, :].rearrange("p k t -> p (k t)"),
                                             ps[:, bank, :], ACT.Copy).then_inc(xT_act, 1)
                    else:
                        for j in range(2):
                            last = nc.scalar.activation(xT[:, 2 * bank + j, :], ps[:, bank, j * T:(j + 1) * T],
                                                        ACT.Identity, scale=scale(2 * bank + j))
                        last.then_inc(xT_act, 1)

            def take(n, j, dst, sem_done, func=ACT.Copy):
                act.wait_ge(proj_ready, 2 * n + j + 1)
                nc.scalar.activation(dst, ps[:, 4 + 2 * (n % 2) + j, :], func).then_inc(sem_done, 1)

            def heads_out(k):
                if k > 4:
                    act.wait_ge(o_ready, k)
                act.wait_ge(o_ps, k + 1)
                hp = k % 4
                bank = 3 if k < 4 else 2 + k % 2
                junk = f if k < 4 else mix[:, 6, :]
                src = ps[:, bank, :].rearrange("p (h t d) -> p h t d", h=2, t=TT)
                for h in range(2):
                    for t in range(TT):
                        at = 2 * hp + h
                        nc.scalar.activation(junk[:, (2 * h + t) * P:(2 * h + t + 1) * P], src[:, h, t, :], ACT.Square,
                                             accum_out=ss[:, t * HEADS + at:t * HEADS + at + 1])
                last = nc.scalar.activation(o[:, :, 2 * hp * P:(2 * hp + 2) * P].rearrange("p t (h d) -> p h t d", h=2),
                                            src, ACT.Copy)
                last.then_inc(o_ready, 1)

            def root(i, width):
                act.wait_ge(var_ready, i + 1)
                nc.scalar.activation(rs[:, 1, 0:width], rs[:, 0, 0:width], ACT.Sqrt).then_inc(root_ready, 1)

            roots = iter(range(6))
            act.wait_ge(pcol_ready, 2)
            nc.scalar.activation(lb[:, :], lb[:, :], ACT.Exp).then_inc(lam_exp_ready, 1)
            act.wait_ge(lam_sum_ready, 2)
            nc.scalar.activation(lam[:, 2:4], lam[:, 0:2], ACT.Exp).then_inc(lam_exp_ready, 1)

            transposed(0)
            for n in (V0, V1):
                take(n, 0, v[:, 0, n * COLS:(n + 1) * COLS], v_act)
            for hp in range(4):
                take(HP[hp], 0, sg, sg_ready, ACT.Sigmoid)
                act.wait_ge(f_ready, hp + 1)
                nc.scalar.activation(lf, f, ACT.Ln).then_inc(lf_ready, 1)
                act.wait_ge(d_ready, hp + 1)
                if hp:
                    act.wait_ge(k_ready, hp)
                    act.wait_ge(q_ready, hp)
                nc.scalar.activation(e3, b, ACT.Exp)
                nc.scalar.activation(e1, d1, ACT.Exp)
                nc.scalar.activation(e2, d1, ACT.Exp, scale=-1.0)
                nc.scalar.activation(e4, d2, ACT.Exp).then_inc(ex_ready, 1)
                if hp:
                    heads_out(hp - 1)
                act.wait_ge(kbt_ps, hp + 1)
                nc.scalar.activation(kbT[:, :, :].rearrange("p h d -> p (h d)"), ps[:, 1, 0:2 * P],
                                     ACT.Copy).then_inc(kbt_ready, 1)
            for i, n in enumerate((G0, G1)):
                for j in range(2):
                    take(n, j, g[:, j, i * COLS:(i + 1) * COLS], g_ready, ACT.Sigmoid)
            heads_out(3)
            root(next(roots), 2 * HEADS)
            transposed(1, lambda k: pcol[:, 16 + k:17 + k])

            def moe(layer):
                def overflow(count, done):
                    with act.If(count > 1):
                        with act.Fori(1, count, 1):
                            act.wait_ge(oxe_ps, done)
                            nc.scalar.activation(o_xe[:, :, :].rearrange("p k s -> p (k s)"), ps[:, BANK_A, :],
                                                 ACT.Copy).then_inc(oxe_ready, 1)
                            act.wait_ge(ogu_ps, done)
                            nc.scalar.activation(o_silu[SLOTS:P, :], ps[0:SLOTS, BANK_C, :],
                                                 ACT.Silu).then_inc(osilu_ready, 1)
                            act.wait_ge(oht_ps, done)
                            nc.scalar.activation(o_hT[:, :, :].rearrange("p j s -> p (j s)"),
                                                 ps[:, BANK_A, 0:FT * SLOTS], ACT.Copy).then_inc(oht_ready, 1)
                            act.reg_add(done, done, 1)

                def take_xe(value):
                    act.wait_ge(xe_ps, value)
                    nc.scalar.activation(xe[:, 0:KT // 2, :].rearrange("p k s -> p (k s)"), ps[:, BANK_C, :],
                                         ACT.Copy).then_inc(xe_act, 1)

                c0 = (PAIRS + 1) * layer
                act.wait_ge(slots_ready, layer + 1)
                nc.scalar.activation(ys[:, 0:COLS], seg[:, :], ACT.Copy, scale=0.0).then_inc(ys_act, 1)
                take_xe(c0 + 1)
                with act.Fori(0, PAIRS, 1) as i:
                    count_a = act.value_load(chunks[0:1, bass.ds(2 * i, 1)], min_val=0, max_val=T // SLOTS)
                    count_b = act.value_load(chunks[0:1, bass.ds(2 * i + 1, 1)], min_val=0, max_val=T // SLOTS)
                    pair = PAIRS * layer + i
                    act.wait_ge(gate_ps, pair + 1)
                    nc.scalar.activation(silu[:, :], ps[:, BANK_A, :], ACT.Silu).then_inc(silu_ready, 1)
                    take_xe(c0 + i + 2)
                    act.wait_ge(ht_ps, pair + 1)
                    nc.scalar.activation(hT[:, :, :].rearrange("p j s -> p (j s)"), ps[:, BANK_A, :],
                                         ACT.Copy).then_inc(ht_ready, 1)
                    act.wait_ge(yc_ps, pair + 1)
                    nc.scalar.activation(ys[:, 0:COLS], ps[:, BANK_C, :], ACT.Copy).then_inc(ys_act, 1)
                    overflow(count_a, done)
                    overflow(count_b, done)

            def router_exp(layer):
                act.wait_ge(logit_ready, layer + 1)
                nc.scalar.activation(rt[:, 1, :], rt[:, 0, :], ACT.Exp).then_inc(rexp_ready, 1)

            done = act.alloc_register("act_done")
            act.reg_mov(done, 1)
            root(next(roots), TT)
            transposed(2)
            reload_ln(1)
            router_exp(0)
            moe(0)
            root(next(roots), TT)
            transposed(3)
            reload_ln(2)
            def take_kq(i):
                dst = (kT, qT)[i % 2]
                take((K0, Q0, K1, Q1)[i], 0, dst[:, 4 * (i // 2):4 * (i // 2) + 2, :].rearrange("p h t -> p (h t)"), kq_act)

            def probabilities(h):
                u = h % 2
                act.wait_ge(s_ready, h + 1)
                if h >= 2:
                    act.wait_ge(a_ready, h - 1)
                for c in range(2):
                    for qt, (lo, hi) in enumerate(((0, P), (P, 3 * P))):
                        at = 2 * qt + c
                        last = nc.scalar.activation(s_ex[:, u, c, lo:hi], s_in[:, u, c, lo:hi], ACT.Exp,
                                                    bias=amx[:, u, at:at + 1], scale=SCALE,
                                                    accum_out=asum[:, u, at:at + 1])
                last.then_inc(p_ready, 1)

            for i in range(3):
                take_kq(i)
            probabilities(0)
            take_kq(3)
            for h in range(1, 4):
                probabilities(h)
            take(BV0, 0, v[:, 0, 0:COLS], v_act)
            for h in range(4, 6):
                probabilities(h)
            take(BV1, 0, v[:, 0, COLS:D], v_act)
            for h in range(6, 8):
                probabilities(h)
            act.wait_ge(p_ready, HEADS)
            for hp in range(4):
                for h in (2 * hp, 2 * hp + 1):
                    act.wait_ge(at_ps, h + 1)
                    nc.scalar.activation(aT[:, h % 2, 0:3, :].rearrange("p s n -> p (s n)"), ps[:, h % 2, 0:3 * P],
                                         ACT.Copy).then_inc(at_ready, 1)
                if hp:
                    heads_out(4 + hp - 1)
            heads_out(7)
            root(next(roots), 2 * HEADS)
            transposed(4, lambda k: pcol[:, 24:25])
            root(next(roots), TT)
            transposed(5)
            reload_ln(3)
            router_exp(1)
            moe(1)
            root(next(roots), TT)

        @block.vector
        def _(dve):
            V = nc.vector
            steps = [0]

            def step(instr):
                steps[0] += 1
                instr.then_inc(dve_step, 1)
                dve.wait_ge(dve_step, steps[0])

            def transposed(call, scale=None):
                for bank in (1, 3):
                    dve.wait_ge(tp_ready, 4 * call + bank + 1)
                    if scale is None:
                        V.tensor_copy(xT[:, 2 * bank:2 * bank + 2, :].rearrange("p k t -> p (k t)"),
                                      ps[:, bank, :]).then_inc(xT_dve, 1)
                    else:
                        for j in range(2):
                            last = V.tensor_scalar(xT[:, 2 * bank + j, :], ps[:, bank, j * T:(j + 1) * T],
                                                   scale(2 * bank + j), None, ALU.mult)
                        last.then_inc(xT_dve, 1)

            def take(n, j, dst, sem_done):
                dve.wait_ge(proj_ready, 2 * n + j + 1)
                V.tensor_copy(dst, ps[:, 4 + 2 * (n % 2) + j, :]).then_inc(sem_done, 1)

            def rstd(i, width):
                dve.wait_ge(root_ready, i + 1)
                var, root, y, t = (rs[:, r, 0:width] for r in range(4))
                step(V.reciprocal(y, root))
                step(V.tensor_tensor(t, y, y, ALU.mult))
                step(V.tensor_tensor(t, t, var, ALU.mult))
                step(V.tensor_scalar(t, t, -0.5, 1.5, ALU.mult, ALU.add))
                return V.tensor_tensor(y, y, t, ALU.mult)

            norms = iter(range(4))
            roots = iter(range(6))

            def layer_norm():
                i = next(norms)
                for t in range(TT):
                    for j in range(2):
                        V.bn_stats(stats[:, t, j, :], x[:, t, j * COLS:(j + 1) * COLS])
                step(V.memset(rs[:, 4, :], 0.0))
                for t in range(TT):
                    last = V.bn_aggr(mv[:, t, :], stats[:, t, :, :].rearrange("p a b -> p (a b)"))
                step(last)
                V.tensor_scalar(rs[:, 0, 0:TT].unsqueeze(2), mv[:, :, 1:2], LN_EPS, None, ALU.add).then_inc(var_ready, 1)
                instr = rstd(next(roots), TT)
                instr.then_inc(ln_stat, 1)
                dve.wait_ge(ln_stat, i + 1)
                dve.wait_ge(ln_in, 32 * (i + 1))
                for t in range(TT):
                    step(V.scalar_tensor_tensor(x[:, t, :], x[:, t, :], mv[:, t, 0:1], ln_gb[:, 0, :],
                                                ALU.subtract, ALU.mult))
                    V.scalar_tensor_tensor(x[:, t, :], x[:, t, :], rs[:, 2, t:t + 1], ln_gb[:, 1, :],
                                           ALU.mult, ALU.add).then_inc(x_done[t], 1)

            def residual_projection(n):
                for j in range(TT):
                    dve.wait_ge(proj_ready, 2 * n + j + 1)
                    cols = x[:, j, (n % 2) * COLS:(n % 2 + 1) * COLS]
                    V.scalar_tensor_tensor(cols, cols, ALPHA, ps[:, 4 + 2 * (n % 2) + j, :],
                                           ALU.mult, ALU.add).then_inc(res_done, 1)

            dve.wait_ge(small_in, 64)
            for i in range(2):
                step(V.tensor_tensor(lam_p[:, i, :], lam_in[:, 2 * i, :], lam_in[:, 2 * i + 1, :], ALU.mult))
                V.reduce_sum(lam[:, i:i + 1], lam_p[:, i, :], axis=AX.X).then_inc(lam_sum_ready, 1)
            dve.wait_ge(pcol_ready, 1)
            step(V.tensor_copy(pcol[:, :], ps[:, 7, 0:25]))
            a0, a1 = pcol[:, 0:8], pcol[:, 8:16]
            step(V.tensor_tensor(rs[:, 0, 0:8], a0, a1, ALU.max))
            step(V.tensor_tensor(lb[:, 0:8], a0, rs[:, 0, 0:8], ALU.subtract))
            V.tensor_tensor(lb[:, 8:16], a1, rs[:, 0, 0:8], ALU.subtract).then_inc(pcol_ready, 1)
            dve.wait_ge(lam_exp_ready, 1)
            step(V.tensor_tensor(rs[:, 0, 0:8], lb[:, 0:8], lb[:, 8:16], ALU.add))
            step(V.reciprocal(rs[:, 1, 0:8], rs[:, 0, 0:8]))
            step(V.tensor_tensor(lb[:, 0:8], lb[:, 0:8], rs[:, 1, 0:8], ALU.mult))
            step(V.tensor_scalar(lb[:, 8:16], lb[:, 0:8], -1.0, 1.0, ALU.mult, ALU.add))
            step(V.tensor_scalar(pcol[:, 24:25], pcol[:, 24:25], 1.0 - LAMBDA_INIT, None, ALU.mult))
            dve.wait_ge(lam_exp_ready, 2)
            step(V.tensor_tensor(lam[:, 5:6], lam[:, 3:4], lam[:, 2:3], ALU.subtract))
            step(V.tensor_scalar(lam[:, 4:5], lam[:, 5:6], -LAMBDA_INIT, None, ALU.add))

            dve.wait_ge(consts_ready, 4)
            transposed(0)
            for n in (V0, V1):
                take(n, 1, v[:, 1, n * COLS:(n + 1) * COLS], v_dve)

            def chunks_of(ap):
                return ap.rearrange("p (c n) -> p c n", n=CHUNK)

            def state_out(hp):
                dve.wait_ge(st_ps, hp + 1)
                V.tensor_copy(state[:, :, :].rearrange("p h d -> p (h d)"), ps[:, 2, 0:2 * P]).then_inc(st_ready, 1)

            for hp in range(4):
                dve.wait_ge(sg_ready, hp + 1)
                if hp:
                    dve.wait_ge(k_ready, hp)
                for h in range(2):
                    at = 2 * hp + h
                    last = V.tensor_scalar(f[:, h * T:(h + 1) * T], sg[:, h * T:(h + 1) * T],
                                           lb[:, 8 + at:9 + at], lb[:, at:at + 1], ALU.mult, ALU.add)
                last.then_inc(f_ready, 1)
                dve.wait_ge(f_ready, hp + 1)
                V.tensor_scalar(kk, f, -1.0, 1.0, ALU.mult, ALU.add).then_inc(kk_ready, 1)
                dve.wait_ge(lf_ready, hp + 1)
                step(V.tensor_tensor_scan(b, seg[:, :], lf, 0.0, ALU.mult, ALU.add))
                bc = chunks_of(b)
                V.tensor_tensor(chunks_of(d1), bc, bc[:, :, CHUNK // 2 - 1:CHUNK // 2].to_broadcast([P, 8, CHUNK]),
                                ALU.subtract)
                V.tensor_tensor(chunks_of(d2), bc[:, :, CHUNK - 1:CHUNK].to_broadcast([P, 8, CHUNK]), bc,
                                ALU.subtract).then_inc(d_ready, 1)
                dve.wait_ge(ex_ready, hp + 1)
                dve.wait_ge(proj_ready, 2 * HP[hp] + 2)
                if hp:
                    dve.wait_ge(sc_ready, hp)
                q = ps[:, 4 + 2 * (HP[hp] % 2) + 1, :]
                V.tensor_tensor(qe, q, e1, ALU.mult)
                V.tensor_tensor(qb, q, e3, ALU.mult).then_inc(q_used, 1)
                dve.wait_ge(q_used, hp + 1)
                if hp >= 2:
                    dve.wait_ge(o_ps, hp - 1)
                for h in range(2):
                    at = h * T + P
                    V.tensor_copy(qbs[:, hp % 2, h, 0:CHUNK], qb[:, at:at + CHUNK])
                    last = V.tensor_scalar(qbs[:, hp % 2, h, CHUNK:P], qb[:, at + CHUNK:at + P],
                                           e3[:, at + CHUNK - 1:at + CHUNK], None, ALU.mult)
                last.then_inc(q_ready, 1)
                if hp:
                    state_out(hp - 1)
                dve.wait_ge(sc_ready, hp + 1)
                V.copy_predicated(scm.rearrange("p (u t) -> p u t", t=P),
                                  causal[:, :].unsqueeze(1).to_broadcast([P, 4, P]),
                                  ps[:, 0, :].rearrange("p (u t) -> p u t", t=P)).then_inc(scm_ready, 1)
            state_out(3)

            def rms(call, pairs):
                dve.wait_ge(o_ready, pairs)
                V.tensor_scalar(rs[:, 0, :], ss[:, :], 1.0 / P, RMS_EPS, ALU.mult, ALU.add).then_inc(var_ready, 1)
                step(rstd(call, 2 * HEADS))

            def by_head(t):
                return (o[:, t, :].rearrange("p (h d) -> p h d", h=HEADS),
                        rs[:, 2, t * HEADS:(t + 1) * HEADS].unsqueeze(2).to_broadcast([P, HEADS, P]))

            rms(next(roots), 4)
            dve.wait_ge(g_ready, 4)
            for t in range(TT):
                oh, r = by_head(t)
                step(V.tensor_tensor(oh, oh, r, ALU.mult))
                V.tensor_tensor(o[:, t, :], o[:, t, :], g[:, t, :], ALU.mult).then_inc(o_done[t], 1)
            transposed(1, lambda k: pcol[:, 16 + k:17 + k])
            residual_projection(AO0)
            residual_projection(AO1)
            dve.wait_ge(res_done, 4)
            layer_norm()
            transposed(2)

            def route(layer):
                N = TT * E

                def te(ap):
                    return ap.rearrange("p (t e) -> p t e", t=TT)

                def pick_first(src, width, const, tmp, result):
                    n = TT
                    m, eq, val = tmp
                    step(V.reduce_max(m, src, axis=AX.X))
                    step(V.tensor_tensor(eq, src, m.unsqueeze(2).to_broadcast([P, n, width]), ALU.is_equal))
                    step(V.tensor_tensor(val, eq, const.unsqueeze(1).to_broadcast([P, n, width]), ALU.mult))
                    step(V.reduce_max(m, val, axis=AX.X))
                    step(V.tensor_tensor(result, val, m.unsqueeze(2).to_broadcast([P, n, width]), ALU.is_equal))

                lg, ex, probs, sel, ohg4, selm, oh1, oh2, both, pm, tmp_a, tmp_b = (rt[:, i, :] for i in range(12))
                m2 = rg[:, 0, 0:TT]
                dve.wait_ge(logit_ps, layer + 1)
                raw = te(ps[:, BANK_A, 0:N])
                step(V.reduce_max(m2, raw, axis=AX.X))
                V.tensor_tensor(te(lg), raw, m2.unsqueeze(2).to_broadcast([P, TT, E]), ALU.subtract
                                ).then_inc(logit_ready, 1)
                dve.wait_ge(rexp_ready, layer + 1)
                step(V.reduce_sum(m2, te(ex), axis=AX.X))
                step(V.reciprocal(rg[:, 1, 0:TT], m2))
                step(V.tensor_tensor(te(probs), te(ex), rg[:, 1, 0:TT].unsqueeze(2).to_broadcast([P, TT, E]), ALU.mult))
                step(V.tensor_tensor(te(sel), te(probs), router_bias[:, :].unsqueeze(1).to_broadcast([P, TT, E]), ALU.add))
                quad = sel.rearrange("p (g a b) -> p g a b", a=2, b=2)
                NG = TT * GROUPS
                hi = rg[:, 2, 0:2 * NG].rearrange("p (g a) -> p g a", a=2)
                lo = rg[:, 3, 0:2 * NG].rearrange("p (g a) -> p g a", a=2)
                V.tensor_tensor(hi, quad[:, :, :, 0], quad[:, :, :, 1], ALU.max)
                step(V.tensor_tensor(lo, quad[:, :, :, 0], quad[:, :, :, 1], ALU.min))
                best, next1, next2, gs = (rg[:, i, 0:NG] for i in (4, 5, 6, 7))
                V.tensor_tensor(best, hi[:, :, 0], hi[:, :, 1], ALU.max)
                V.tensor_tensor(next1, hi[:, :, 0], hi[:, :, 1], ALU.min)
                step(V.tensor_tensor(next2, lo[:, :, 0], lo[:, :, 1], ALU.max))
                step(V.tensor_tensor(next1, next1, next2, ALU.max))
                step(V.tensor_tensor(gs, best, next1, ALU.add))

                def tg(ap):
                    return ap.rearrange("p (t g) -> p t g", t=TT)

                ohg = rg[:, 8, 0:NG]
                pick_first(tg(gs), GROUPS, first_g[:, :], (m2, tg(rg[:, 9, 0:NG]), tg(rg[:, 10, 0:NG])), tg(ohg))
                g4 = ohg.unsqueeze(2).to_broadcast([P, NG, 4])
                pen = rg[:, 11, 0:NG]
                V.tensor_scalar(pen, ohg, BIG, -BIG, ALU.mult, ALU.add)
                step(V.tensor_tensor(tmp_a.rearrange("p (g e) -> p g e", e=4),
                                     sel.rearrange("p (g e) -> p g e", e=4), g4, ALU.mult))
                step(V.tensor_tensor(selm.rearrange("p (g e) -> p g e", e=4), tmp_a.rearrange("p (g e) -> p g e", e=4),
                                     pen.unsqueeze(2).to_broadcast([P, NG, 4]), ALU.add))
                pick_first(te(selm), E, first_e[:, :], (m2, te(tmp_a), te(tmp_b)), te(oh1))
                step(V.scalar_tensor_tensor(selm, oh1, -BIG, selm, ALU.mult, ALU.add))
                pick_first(te(selm), E, first_e[:, :], (m2, te(tmp_a), te(tmp_b)), te(oh2))
                V.tensor_tensor(both, oh1, oh2, ALU.add).then_inc(routed, 1)
                dve.wait_ge(routed, layer + 1)
                step(V.tensor_tensor(pm, probs, both, ALU.mult))
                step(V.reduce_sum(m2, te(pm), axis=AX.X))
                step(V.reciprocal(rg[:, 1, 0:TT], m2))
                V.tensor_tensor(gate[:, :, 0:E], te(pm), rg[:, 1, 0:TT].unsqueeze(2).to_broadcast([P, TT, E]), ALU.mult)
                dve.wait_ge(rank_ps, layer + 1)
                step(V.scalar_tensor_tensor(tmp_a, ps[:, BANK_B, 0:N], 1.0, both, ALU.add, ALU.mult))
                V.tensor_scalar(slot[:, :, 0:E], te(tmp_a), -1.0, None, ALU.add)
                step(V.tensor_copy(count_f[0:1, 0, :], ps[0:1, BANK_B, N:N + E]))
                step(V.tensor_scalar(count_f[0:1, 1, :], count_f[0:1, 0, :], float(SLOTS), None, ALU.is_gt))
                for c in range(2, T // SLOTS):
                    step(V.tensor_scalar(count_f[0:1, 2, :], count_f[0:1, 0, :], float(c * SLOTS), None, ALU.is_gt))
                    step(V.tensor_tensor(count_f[0:1, 1, :], count_f[0:1, 1, :], count_f[0:1, 2, :], ALU.add))
                V.tensor_copy(extra[:, :], count_f[0:1, 1, :])
                V.tensor_scalar(chunks[:, :], count_f[0:1, 1, :], 1.0, None, ALU.add).then_inc(slots_ready, 1)
                dve.wait_ge(slots_ready, layer + 1)

            def moe(layer):
                def pick_pair(index):
                    V.tensor_tensor(pick[:, :, :, :],
                                    iota[:, 0:SLOTS].unsqueeze(1).unsqueeze(1).to_broadcast([P, TT, 2, SLOTS]),
                                    slot[:, :, bass.ds(index, 2)].unsqueeze(3).to_broadcast([P, TT, 2, SLOTS]),
                                    ALU.is_equal).then_inc(pick_ready, 1)

                def overflow(count, done, index):
                    with dve.If(count > 1):
                        with dve.Fori(1, count, 1) as c:
                            dve.wait_ge(o_free, done)
                            V.tensor_tensor(o_pick, iota[:, bass.ds(SLOTS * c, SLOTS)].unsqueeze(1)
                                            .to_broadcast([P, TT, SLOTS]),
                                            slot[:, :, bass.ds(index, 1)].to_broadcast([P, TT, SLOTS]),
                                            ALU.is_equal).then_inc(op_ready, 1)
                            dve.wait_ge(op_ready, done)
                            V.tensor_tensor(o_pick_g, o_pick, gate[:, :, bass.ds(index, 1)].to_broadcast([P, TT, SLOTS]),
                                            ALU.mult).then_inc(opg_ready, 1)
                            dve.wait_ge(oput_ps, done)
                            V.tensor_copy(o_put[:, :], ps[0:SLOTS, BANK_B, 0:T]).then_inc(oput_done, 1)
                            dve.wait_ge(ogu_ps, done)
                            dve.wait_ge(osilu_ready, done)
                            V.tensor_tensor(o_h[:, :], ps[SLOTS:P, BANK_D, :], o_silu[SLOTS:P, :],
                                            ALU.mult).then_inc(oh_done, 1)
                            dve.wait_ge(oy_ps, done)
                            V.tensor_copy(o_ys[:, 0:COLS], ps[0:SLOTS, BANK_C, :])
                            V.tensor_copy(o_ys[:, COLS:D], ps[SLOTS:P, BANK_D, :]).then_inc(oys_done, 1)
                            dve.reg_add(done, done, 1)

                c0 = (PAIRS + 1) * layer
                V.memset(ys[:, COLS:D], 0.0).then_inc(ys_dve, 1)
                V.memset(put[:, :], 0.0).then_inc(put_done, 1)
                pick_pair(0)

                def take_xe(value):
                    dve.wait_ge(xe_ps, value)
                    V.tensor_copy(xe[:, KT // 2:KT, :].rearrange("p k s -> p (k s)"), ps[:, BANK_D, :]
                                  ).then_inc(xe_dve, 1)

                take_xe(c0 + 1)
                with dve.Fori(0, PAIRS, 1) as i:
                    count_a = dve.value_load(chunks[0:1, bass.ds(2 * i, 1)], min_val=0, max_val=T // SLOTS)
                    count_b = dve.value_load(chunks[0:1, bass.ds(2 * i + 1, 1)], min_val=0, max_val=T // SLOTS)
                    pair = PAIRS * layer + i
                    dve.wait_ge(pickg_ready, pair + 1)
                    pick_pair(2 * i + 2)
                    dve.wait_ge(up_ps, pair + 1)
                    dve.wait_ge(silu_ready, pair + 1)
                    V.tensor_tensor(hid[:, :], ps[:, BANK_B, :], silu[:, :], ALU.mult).then_inc(h_ready, 1)
                    take_xe(c0 + i + 2)
                    dve.wait_ge(put_ps, pair + 2)
                    V.tensor_copy(put[:, :], ps[:, BANK_B, 0:T]).then_inc(put_done, 1)
                    dve.wait_ge(yd_ps, pair + 1)
                    V.tensor_copy(ys[:, COLS:D], ps[:, BANK_D, :]).then_inc(ys_dve, 1)
                    for e, count in enumerate((count_a, count_b)):
                        overflow(count, done, 2 * i + e)
                dve.wait_ge(acc_ps, (PAIRS + 1) * (layer + 1))
                for t in range(TT):
                    for j in range(2):
                        cols = x[:, t, j * COLS:(j + 1) * COLS]
                        last = V.scalar_tensor_tensor(cols, cols, ALPHA, ps[:, 2 * t + j, :], ALU.mult, ALU.add)
                step(last)

            done = dve.alloc_register("dve_done")
            dve.reg_mov(done, 1)
            dve.wait_ge(router_in, 32)
            route(0)
            moe(0)
            layer_norm()
            transposed(3)

            def take_kq(i):
                dst = (kT, qT)[i % 2]
                take((K0, Q0, K1, Q1)[i], 1, dst[:, 4 * (i // 2) + 2:4 * (i // 2) + 4, :].rearrange("p h t -> p (h t)"),
                     kq_dve)

            def masked_scores(h):
                u = h % 2
                dve.wait_ge(s_ps, h + 1)
                if h >= 2:
                    dve.wait_ge(p_ready, h - 1)
                V.tensor_tensor(s_in[:, u, :, 0:3 * P], ps[:, 2 * u:2 * u + 2, 0:3 * P],
                                amask[:, :].unsqueeze(1).to_broadcast([P, 2, 3 * P]), ALU.add).then_inc(s_ready_raw, 1)
                dve.wait_ge(s_ready_raw, h + 1)
                V.reduce_max(amx[:, u, 0:2], s_in[:, u, :, 0:P], axis=AX.X)
                step(V.reduce_max(amx[:, u, 2:4], s_in[:, u, :, P:3 * P], axis=AX.X))
                V.tensor_scalar(amx[:, u, :], amx[:, u, :], -SCALE, None, ALU.mult).then_inc(s_ready, 1)

            def weights(h):
                u = h % 2
                dve.wait_ge(p_ready, h + 1)
                step(V.reciprocal(arec[:, u, :], asum[:, u, :]))
                r = arec[:, u, :].rearrange("p (t c) -> p t c", c=2)
                step(V.tensor_scalar(r[:, :, 1:2], r[:, :, 1:2], lam[:, 4:5], None, ALU.mult))
                spans = ((0, 1), (1, 3))

                def tiles(c, lo, hi):
                    return s_ex[:, u, c, lo * P:hi * P].rearrange("p (s n) -> p s n", n=P)

                a = o3[:, :, h * P:(h + 1) * P]
                for t, (lo, hi) in enumerate(spans):
                    last = V.tensor_scalar(a[:, lo:hi, :], tiles(0, lo, hi), arec[:, u, 2 * t:2 * t + 1],
                                           None, ALU.mult)
                step(last)
                for t, (lo, hi) in enumerate(spans):
                    last = V.scalar_tensor_tensor(a[:, lo:hi, :], tiles(1, lo, hi), arec[:, u, 2 * t + 1:2 * t + 2],
                                                  a[:, lo:hi, :], ALU.mult, ALU.add)
                last.then_inc(a_ready, 1)

            take_kq(0)
            take_kq(1)
            masked_scores(0)
            for h in range(1, HEADS):
                masked_scores(h)
                if h == 1:
                    take_kq(2)
                if h == 6:
                    take(BV1, 1, v[:, 1, COLS:D], v_dve)
                weights(h - 1)
                if h == 2:
                    take_kq(3)
                if h == 4:
                    take(BV0, 1, v[:, 1, 0:COLS], v_dve)
            weights(HEADS - 1)
            rms(next(roots), 8)
            for t in range(TT):
                oh, r = by_head(t)
                V.tensor_tensor(oh, oh, r, ALU.mult).then_inc(o_done[t], 1)
            transposed(4, lambda k: pcol[:, 24:25])
            residual_projection(BO0)
            residual_projection(BO1)
            dve.wait_ge(res_done, 8)
            layer_norm()
            transposed(5)
            route(1)
            moe(1)
            layer_norm()

        @block.tensor
        def _(pe):
            mm = nc.tensor.matmul

            def transposes(call, src):
                for t in range(TT):
                    for k in range(KT):
                        at = (k % 2) * T + t * P
                        last = nc.tensor.transpose(ps[:, k // 2, at:at + P], src[:, t, k * P:(k + 1) * P], ident[:, :])
                        if t == 1 and k % 2:
                            last.then_inc(tp_ready, 1)
                    if t == 0:
                        yield

            def transpose_all(call, src, ready, value):
                pe.wait_ge(ready[0], value)
                for _ in transposes(call, src):
                    pe.wait_ge(ready[1], value)
                pe.wait_ge(xT_act, 2 * (call + 1))
                pe.wait_ge(xT_dve, 2 * (call + 1))

            def free(n, j):
                if (n - 2, j) in taken and n not in (K0, Q0):
                    pe.wait_ge(*taken[n - 2, j])

            def arrive(n):
                pe.wait_ge(dense_in[n % RING], 32 * dense_use(n))

            def rows(n, j):
                free(n, j)
                for k in range(KT):
                    last = mm(ps[:, 4 + 2 * (n % 2) + j, :], xT[:, k, j * P:(j + 1) * P], dense[:, n % RING, k, :],
                              start=k == 0, stop=k == KT - 1)
                last.then_inc(proj_ready, 1)

            def columns(n, j):
                free(n, j)
                for i in range(2):
                    c = (2 * j + i) * P
                    for k in range(KT):
                        last = mm(ps[:, 4 + 2 * (n % 2) + j, i * T:(i + 1) * T], dense[:, n % RING, k, c:c + P],
                                  xT[:, k, :], start=k == 0, stop=k == KT - 1)
                last.then_inc(proj_ready, 1)

            pe.wait_ge(consts_ready, 1)
            pe.wait_ge(small_in, 64)
            nc.tensor.transpose(ps[:, 7, 0:25], prow[:, :], ident[0:25, 0:25]).then_inc(pcol_ready, 1)

            pe.wait_ge(x_in, 32)
            for _ in transposes(0, x):
                pass
            pe.wait_ge(xT_act, 2)
            pe.wait_ge(xT_dve, 2)
            pe.wait_ge(pcol_ready, 2)

            def scores(hp):
                pe.wait_ge(q_ready, hp + 1)
                pe.wait_ge(k_ready, hp + 1)
                if hp:
                    pe.wait_ge(scm_ready, hp)
                    pe.wait_ge(kbt_ready, hp)
                for u in range(4):
                    at = u * P
                    mm(ps[:, 0, at:at + P], ke[:, at:at + P], qe[:, at:at + P], start=True, stop=True)
                    last = mm(ps[0:CHUNK, 0, at + CHUNK:at + P], kb[:, at:at + CHUNK], qb[:, at + CHUNK:at + P],
                              start=True, stop=True)
                last.then_inc(sc_ready, 1)
                for h in range(2):
                    last = nc.tensor.transpose(ps[:, 1, h * P:(h + 1) * P], kbs[:, h, :], ident[:, :])
                last.then_inc(kbt_ps, 1)

            def states(hp):
                pe.wait_ge(kbt_ready, hp + 1)
                if hp == 0:
                    pe.wait_ge(v_act, 2)
                    pe.wait_ge(v_dve, 2)
                else:
                    pe.wait_ge(st_ready, hp)
                for h in range(2):
                    head = (2 * hp + h) * P
                    last = mm(ps[:, 2, h * P:(h + 1) * P], kbT[:, h, :], v[:, 0, head:head + P], start=True, stop=True)
                last.then_inc(st_ps, 1)

            def outputs(hp):
                pe.wait_ge(scm_ready, hp + 1)
                pe.wait_ge(st_ready, hp + 1)
                if hp:
                    pe.wait_ge(o_ready, hp)
                for h in range(2):
                    head = (2 * hp + h) * P
                    for t in range(TT):
                        at = (2 * h + t) * P
                        last = mm(ps[:, 3, at:at + P], scm[:, at:at + P], v[:, t, head:head + P],
                                  start=True, stop=t == 0)
                        if t:
                            last = mm(ps[:, 3, at:at + P], qbs[:, hp % 2, h, :], state[:, h, :], start=False, stop=True)
                last.then_inc(o_ps, 1)

            for n in (V0, V1):
                arrive(n)
                rows(n, 0)
                rows(n, 1)
            arrive(HP0)
            columns(HP0, 0)
            columns(HP0, 1)
            for hp, n in enumerate((HP1, HP2, HP3, G0, G1)):
                part = columns if n in HP else rows
                arrive(n)
                part(n, 0)
                if hp >= 1:
                    states(hp - 1)
                part(n, 1)
                if hp >= 1:
                    outputs(hp - 1)
                if hp < 4:
                    scores(hp)
            transpose_all(1, o, o_done, 1)
            for n in (AO0, AO1):
                arrive(n)
                rows(n, 0)
                rows(n, 1)

            def moe(layer):
                pe.wait_ge(router_in, 32)
                for t in range(TT):
                    for k in range(KT):
                        last = mm(ps[:, BANK_A, t * E:(t + 1) * E], xT[:, k, t * P:(t + 1) * P], router[:, k, :],
                                  start=k == 0, stop=k == KT - 1)
                last.then_inc(logit_ps, 1)
                for bank in range(4):
                    mm(ps[:, bank, :], zeros16[:, :], zeros16[:, :].unsqueeze(1).to_broadcast([P, COLS // P, P]),
                       start=True, stop=True)
                pe.wait_ge(routed, layer + 1)
                both = rt[:, 8, :]
                N = TT * E
                mm(ps[:, BANK_B, 0:E], later[:, :], both[:, 0:E], start=True, stop=True)
                mm(ps[:, BANK_B, E:N], later[:, :], both[:, E:N], start=True, stop=False)
                mm(ps[:, BANK_B, E:N], ones[:, :], both[:, 0:E], start=False, stop=True)
                mm(ps[:, BANK_B, N:N + E], ones[:, :], both[:, 0:E], start=True, stop=False)
                mm(ps[:, BANK_B, N:N + E], ones[:, :], both[:, E:N], start=False, stop=True).then_inc(rank_ps, 1)

                c0 = (PAIRS + 1) * layer

                def add_up(matrix, rows_):
                    for t in range(TT):
                        for j in range(2):
                            last = mm(ps[:, 2 * t + j, :], matrix[:, t * P:(t + 1) * P], rows_[:, j * COLS:(j + 1) * COLS],
                                      start=False, stop=True, skip_group_check=True)
                    return last

                def gather_pair():
                    for k in range(KT):
                        at = (k % 4) * P
                        for t in range(TT):
                            last = mm(ps[:, (BANK_C, BANK_D)[k // 4], at:at + P], x[:, t, k * P:(k + 1) * P],
                                      pick[:, t, :, :].rearrange("p e s -> p (e s)"), start=t == 0, stop=t == TT - 1)
                    last.then_inc(xe_ps, 1)

                def both_experts(bank, tokens, w, tiles, first):
                    for k in range(tiles):
                        for e in range(2):
                            half = slice(e * SLOTS, (e + 1) * SLOTS)
                            last = mm(ps[half, bank, :], tokens[:, k, half], w[:, e, k, first:first + COLS],
                                      start=k == 0, stop=k == tiles - 1)
                    return last

                def overflow(e, count, i, done):
                    lower, upper = slice(0, SLOTS), slice(SLOTS, P)
                    with pe.If(count > 1):
                        with pe.Fori(1, count, 1):
                            pe.wait_ge(op_ready, done)
                            for k in range(KT):
                                for t in range(TT):
                                    last = mm(ps[:, BANK_A, k * SLOTS:(k + 1) * SLOTS], x[:, t, k * P:(k + 1) * P],
                                              o_pick[:, t, :], start=t == 0, stop=t == TT - 1)
                            last.then_inc(oxe_ps, 1)
                            pe.wait_ge(opg_ready, done)
                            pe.wait_ge(put_done, c0 + i + 2)
                            for t in range(TT):
                                last = mm(ps[lower, BANK_B, t * P:(t + 1) * P], o_pick_g[:, t, :], ident[:, :],
                                          start=True, stop=True)
                            last.then_inc(oput_ps, 1)
                            pe.wait_ge(oxe_ready, done)
                            pe.wait_ge(ys_act, c0 + i + 2)
                            pe.wait_ge(ys_dve, c0 + i + 2)
                            for k in range(KT):
                                mm(ps[lower, BANK_C, :], o_xe[:, k, :], w_gate[:, e, k, :], start=k == 0, stop=k == KT - 1)
                                last = mm(ps[upper, BANK_D, :], o_xe[:, k, :], w_up[:, e, k, :],
                                          start=k == 0, stop=k == KT - 1)
                            last.then_inc(ogu_ps, 1)
                            pe.wait_ge(oh_done, done)
                            for j in range(FT):
                                last = mm(ps[:, BANK_A, j * SLOTS:(j + 1) * SLOTS], o_h[:, j * P:(j + 1) * P],
                                          ident[lower, lower], start=True, stop=True)
                            last.then_inc(oht_ps, 1)
                            pe.wait_ge(oht_ready, done)
                            for j in range(FT):
                                mm(ps[lower, BANK_C, :], o_hT[:, j, :], w_down[:, e, j, 0:COLS],
                                   start=j == 0, stop=j == FT - 1)
                                last = mm(ps[upper, BANK_D, :], o_hT[:, j, :], w_down[:, e, j, COLS:D],
                                          start=j == 0, stop=j == FT - 1)
                            last.then_inc(oy_ps, 1)
                            pe.wait_ge(oput_done, done)
                            pe.wait_ge(oys_done, done)
                            add_up(o_put, o_ys).then_inc(o_free, 1)
                            pe.reg_add(done, done, 1)

                pe.wait_ge(slots_ready, layer + 1)
                pe.wait_ge(pick_ready, c0 + 1)
                gather_pair()
                with pe.Fori(0, PAIRS, 1) as i:
                    count_a = pe.value_load(chunks[0:1, bass.ds(2 * i, 1)], min_val=0, max_val=T // SLOTS)
                    count_b = pe.value_load(chunks[0:1, bass.ds(2 * i + 1, 1)], min_val=0, max_val=T // SLOTS)
                    pair = PAIRS * layer + i
                    pe.wait_ge(gate_in, 32 * pair + 32)
                    pe.wait_ge(xe_act, c0 + i + 1)
                    pe.wait_ge(xe_dve, c0 + i + 1)
                    both_experts(BANK_A, xe, w_gate, KT, 0).then_inc(gate_ps, 1)
                    pe.wait_ge(up_in, 32 * pair + 32)
                    pe.wait_ge(put_done, c0 + i + 1)
                    both_experts(BANK_B, xe, w_up, KT, 0).then_inc(up_ps, 1)
                    pe.wait_ge(pick_ready, c0 + i + 2)
                    pe.wait_ge(ys_act, c0 + i + 1)
                    pe.wait_ge(ys_dve, c0 + i + 1)
                    gather_pair()
                    pe.wait_ge(h_ready, pair + 1)
                    for j in range(FT):
                        last = nc.tensor.transpose(ps[:, BANK_A, j * P:(j + 1) * P], hid[:, j * P:(j + 1) * P], ident[:, :])
                    last.then_inc(ht_ps, 1)
                    add_up(put, ys).then_inc(acc_ps, 1)
                    pe.wait_ge(pickg_ready, pair + 1)
                    for t in range(TT):
                        last = nc.tensor.transpose(ps[:, BANK_B, t * P:(t + 1) * P],
                                                   pick_g[:, t, :, :].rearrange("p e s -> p (e s)"), ident[:, :])
                    last.then_inc(put_ps, 1)
                    pe.wait_ge(down_in, 32 * pair + 32)
                    pe.wait_ge(ht_ready, pair + 1)
                    pe.wait_ge(xe_act, c0 + i + 2)
                    pe.wait_ge(xe_dve, c0 + i + 2)
                    both_experts(BANK_C, hT, w_down, FT, 0).then_inc(yc_ps, 1)
                    both_experts(BANK_D, hT, w_down, FT, COLS).then_inc(yd_ps, 1)
                    overflow(0, count_a, i, done)
                    overflow(1, count_b, i, done)
                pe.wait_ge(put_done, c0 + PAIRS + 1)
                pe.wait_ge(ys_act, c0 + PAIRS + 1)
                pe.wait_ge(ys_dve, c0 + PAIRS + 1)
                add_up(put, ys).then_inc(acc_ps, 1)

            done = pe.alloc_register("pe_done")
            pe.reg_mov(done, 1)
            pe.sem_inc(o_free, 1)
            pe.sem_inc(put_ps, 1)
            transpose_all(2, x, x_done, 1)
            moe(0)

            transpose_all(3, x, x_done, 2)

            def attention_scores(h):
                u = h % 2
                if h >= 2:
                    pe.wait_ge(s_ready_raw, h - 1)
                for c in range(2):
                    part = slice(c * DH, (c + 1) * DH)
                    mm(ps[:, 2 * u + c, 0:P], qT[part, h, 0:P], kT[part, h, 0:P], start=True, stop=True)
                    last = mm(ps[:, 2 * u + c, P:3 * P], qT[part, h, P:T], kT[part, h, :], start=True, stop=True)
                last.then_inc(s_ps, 1)

            def block_of(n, part, between=()):
                arrive(n)
                part(n, 0)
                for h in between[:1]:
                    attention_scores(h)
                part(n, 1)
                for h in between[1:]:
                    attention_scores(h)

            block_of(K0, columns)
            block_of(Q0, columns)
            arrive(K1)
            columns(K1, 0)
            pe.wait_ge(kq_act, 2)
            pe.wait_ge(kq_dve, 2)
            attention_scores(0)
            attention_scores(1)
            columns(K1, 1)
            block_of(Q1, columns, (2, 3))
            arrive(BV0)
            rows(BV0, 0)
            pe.wait_ge(kq_act, 4)
            pe.wait_ge(kq_dve, 4)
            attention_scores(4)
            rows(BV0, 1)
            attention_scores(5)
            block_of(BV1, rows, (6, 7))
            pe.wait_ge(v_act, 4)
            pe.wait_ge(v_dve, 4)

            def attention_turn(h):
                pe.wait_ge(a_ready, h + 1)
                if h == 0:
                    pe.wait_ge(s_ready_raw, HEADS)
                if h >= 2:
                    pe.wait_ge(at_ready, h - 1)
                for s in range(3):
                    last = nc.tensor.transpose(ps[:, h % 2, s * P:(s + 1) * P], o3[:, s, h * P:(h + 1) * P],
                                               ident[:, :])
                last.then_inc(at_ps, 1)

            def attention_out(h):
                hp, u = divmod(h, 2)
                pe.wait_ge(at_ready, h + 1)
                if hp >= 2 and u == 0:
                    pe.wait_ge(o_ready, 4 + hp - 1)
                bank = 2 + hp % 2
                cols = slice(h * P, (h + 1) * P)
                at = 2 * u * P
                mm(ps[:, bank, at:at + P], aT[:, u, 0, :], v[:, 0, cols], start=True, stop=True)
                mm(ps[:, bank, at + P:at + 2 * P], aT[:, u, 1, :], v[:, 0, cols], start=True, stop=False)
                last = mm(ps[:, bank, at + P:at + 2 * P], aT[:, u, 2, :], v[:, 1, cols], start=False, stop=True)
                if u:
                    last.then_inc(o_ps, 1)

            attention_turn(0)
            for h in range(HEADS):
                if h + 1 < HEADS:
                    attention_turn(h + 1)
                attention_out(h)
            transpose_all(4, o, o_done, 2)
            for n in (BO0, BO1):
                arrive(n)
                rows(n, 0)
                rows(n, 1)
            transpose_all(5, x, x_done, 3)
            moe(1)


def kernel(**inputs):
    import numpy as _np
    import concourse.bacc as _bacc
    from concourse import mybir as _mybir
    from concourse.bass_utils import run_bass_kernel_spmd as _run

    nc = _bacc.Bacc("TRN2", target_bir_lowering=False, num_devices=1, dynamic_dma_scratch_size=1024)
    arrays, aps = {}, {}
    for name, a in inputs.items():
        a = _np.ascontiguousarray(a)
        arrays[f"in_{name}"] = a
        aps[name] = nc.dram_tensor(f"in_{name}", a.shape, _mybir.dt.from_np(a.dtype), kind="ExternalInput").ap()
    out = nc.dram_tensor("out", (1, T, D), _mybir.dt.float32, kind="ExternalOutput").ap()
    build(nc, aps, out)
    r = _run(nc, [arrays], core_ids=[0])
    return r.results[0]["out"]
```

```python
import math
from contextlib import ExitStack

import concourse.bass as bass
from concourse import mybir

F32 = mybir.dt.float32
F32R = mybir.dt.float32r
BF16 = mybir.dt.bfloat16
I32 = mybir.dt.int32
ALU = mybir.AluOpType
ACT = mybir.ActivationFunctionType
AX = mybir.AxisListType

P = 128
D = 1024
T = 256
TT = T // P
KT = D // P
LAYERS = 2
HEADS = 8
CHUNK = 64
DH = 64
E = 16
GROUPS = 4
F = 512
FT = F // P
SLOTS = 64
PAIRS = E // 2
COLS = 512
ALPHA = (2.0 * LAYERS) ** 0.25
LAMBDA_INIT = 0.8 - 0.6 * math.exp(-0.3 * 1)
LN_EPS = 1e-5
RMS_EPS = 1e-6
BIG = 1e30
SCALE = DH ** -0.5

SMALL = 8 * 16
(V0, V1, HP0, HP1, HP2, HP3, G0, G1, AO0, AO1,
 K0, Q0, K1, Q1, BV0, BV1, BO0, BO1) = range(18)
HP = [HP0, HP1, HP2, HP3]
COLUMNS = HP + [K0, Q0, K1, Q1]
SPLIT = [n for n in range(18) if n not in (V0, K0)]
POOL_HALVES = [(BV0, 0), (BV1, 0), (BO0, 0)]
PARTS = 3
HALF = COLS // 2
BANK_A, BANK_B, BANK_C, BANK_D = 4, 5, 6, 7


def build(nc, ins, out):
    ctx = ExitStack()
    with ctx:
        def sb(name, shape, dt=F32):
            return ctx.enter_context(nc.sbuf_tensor(name, shape, dt))

        def sem(name):
            return ctx.enter_context(nc.semaphore(name))

        dense = sb("dense", [P, 2, KT, COLS])
        with nc.sbuf_tensor("w_hi", [P, PARTS, KT, HALF], F32R) as w_hi, \
                nc.sbuf_tensor("w_lo", [P, PARTS, KT, HALF], F32R) as w_lo, \
                nc.sbuf_tensor("x_hi", [P, KT, T], F32R) as x_hi, \
                nc.sbuf_tensor("x_lo", [P, KT, T], F32R) as x_lo:
            pass
        w_gate = sb("w_gate", [P, 2, KT, F])
        w_up = sb("w_up", [P, 2, KT, F])
        w_down = sb("w_down", [P, 2, FT, D])
        x = sb("x_sb", [P, TT, D])
        xT = sb("xT", [P, KT, T])
        ln_gb = sb("ln_gb", [P, 2, D])
        ident = sb("ident", [P, P])
        causal = sb("causal", [P, P], I32)
        later = sb("later", [P, P])
        ones = sb("ones", [P, P])
        zeros16 = sb("zeros16", [P, P], BF16)
        iota = sb("iota", [P, T])
        seg = sb("seg", [P, 2 * T])
        amask = sb("amask", [P, 3 * P])
        first_g = sb("first_g", [P, GROUPS])
        beats = sb("beats", [P, 4, 8])
        prow = sb("prow", [25 + 8 * KT, P])
        pcol = sb("pcol", [P, 25 + 8 * KT])
        lb = sb("lb", [P, 2 * HEADS])
        lam_in = sb("lam_in", [P, 4, DH])
        lam = sb("lam", [P, 8])
        lam_p = sb("lam_p", [P, 2, DH])
        router = sb("router", [P, KT, 2 * E])
        logit_parts = sb("logit_parts", [P, T])
        fold = sb("fold", [P, E])
        router_bias = sb("router_bias", [P, E])
        stats = sb("stats", [P, TT, 2, 6])
        mv = sb("mv", [P, TT, 2])
        rs = sb("rs", [P, 5, 2 * HEADS])
        ss = sb("ss", [P, 2 * HEADS])
        o3 = sb("o3", [P, 3, D])
        o = o3[:, 0:TT, :]
        scratch = sb("scratch", [P, 2 * TT * D + 12 * 2 * T])
        place = [0]

        def carve(*shape, parts=P):
            size = math.prod(shape)
            ap = scratch[0:parts, place[0]:place[0] + size]
            place[0] += size
            names = "abc"[:len(shape)]
            if len(shape) == 1:
                return ap
            return ap.rearrange(f"p ({' '.join(names)}) -> p {' '.join(names)}", **dict(zip(names, shape)))

        v = carve(TT, D)
        g = carve(TT, D)
        mix = carve(12, 2 * T)
        sg, kk, b, d1, d2, e1, qe, qb, ke, kb, scm, f = (mix[:, i, :] for i in range(12))
        lf, e3, e2, e4 = sg, b, d1, d2
        third = o3[:, 2, :].rearrange("p (a h n) -> p a h n", a=4, h=2)
        kbs, kbT, state = third[:, 0], third[:, 1], third[:, 2]
        qbs = sb("qbs", [P, 2, 2, P])
        iota_i = e1[:, 0:T].bitcast(I32)
        qT = g[:, :, :].rearrange("p a (h t) -> p (a h) t", t=T)
        kT = mix[:, 0:4, :].rearrange("p a (h t) -> p (a h) t", t=T)
        s_in = mix[:, 4:8, :].rearrange("p (u c) n -> p u c n", u=2)
        s_ex = mix[:, 8:12, :].rearrange("p (u c) n -> p u c n", u=2)
        aT = mix[:, 4:6, :].rearrange("p u (s n) -> p u s n", n=P)
        amx = sb("amx", [P, 2, 4])
        asum = sb("asum", [P, 2, 4])
        arec = sb("arec", [P, 2, 4])
        rt = sb("rt", [P, 12, TT * E])
        rg = sb("rg", [P, 12, TT * E])
        versus = sb("versus", [P, TT * GROUPS, 4, 8])
        slot = sb("slot", [P, TT, E + 2])
        gate = sb("gate", [P, TT, E + 2])
        count_f = sb("count_f", [1, 4, E])
        chunks = sb("chunks", [1, E], I32)
        extra = sb("extra", [1, E], I32)
        place[0] = 0
        pick = carve(TT, 2, SLOTS)
        pick_g = carve(TT, 2, SLOTS)
        xe = carve(KT, 2 * SLOTS)
        silu = carve(F)
        hid = carve(F)
        hT = carve(FT, 2 * SLOTS)
        ys = carve(D)
        put = carve(T)
        o_pick = carve(TT, SLOTS)
        o_pick_g = carve(TT, SLOTS)
        o_xe = carve(KT, SLOTS)
        o_silu = carve(F)
        o_h = carve(F, parts=SLOTS)
        o_hT = carve(FT, SLOTS)
        o_ys = carve(D, parts=SLOTS)
        o_put = carve(T, parts=SLOTS)
        assert place[0] <= scratch.shape[1]

        ps = ctx.enter_context(nc.psum_tensor("ps", [P, 8, COLS], F32))

        x_in = sem("x_in")
        small_in = sem("small_in")
        router_in = sem("router_in")
        ln_in = sem("ln_in")
        dense_in = [[sem(f"dense_in{r}_{j}") for j in range(2)] for r in range(2)]
        hi_ready = sem("hi_ready")
        lo_ready = sem("lo_ready")
        lo_pool = sem("lo_pool")
        x_hi_ready = sem("x_hi_ready")
        x_hi_dve = sem("x_hi_dve")
        x_lo_ready = sem("x_lo_ready")
        rows_half = sem("rows_half")
        odd_gate_in = sem("odd_gate_in")
        up_in = sem("up_in")
        down_in = sem("down_in")
        even_gate_in = sem("even_gate_in")
        out_sem = sem("out_sem")
        consts_ready = sem("consts_ready")
        pool_step = sem("pool_step")
        dve_step = sem("dve_step")
        table_loaded = sem("table_loaded")
        pcol_ready = sem("pcol_ready")
        lam_exp_ready = sem("lam_exp_ready")
        lam_sum_ready = sem("lam_sum_ready")
        proj_ready = sem("proj_ready")
        tp_ready = sem("tp_ready")
        xT_act = sem("xT_act")
        xT_dve = sem("xT_dve")
        v_act = sem("v_act")
        v_dve = sem("v_dve")
        sg_ready = sem("sg_ready")
        f_ready = sem("f_ready")
        lf_ready = sem("lf_ready")
        d_ready = sem("d_ready")
        kk_ready = sem("kk_ready")
        ex_ready = sem("ex_ready")
        q_used = sem("q_used")
        q_ready = sem("q_ready")
        k_ready = sem("k_ready")
        sc_ready = sem("sc_ready")
        scm_ready = sem("scm_ready")
        kbt_ps = sem("kbt_ps")
        kbt_ready = sem("kbt_ready")
        st_ps = sem("st_ps")
        st_ready = sem("st_ready")
        o_ps = sem("o_ps")
        o_ready = sem("o_ready")
        g_ready = sem("g_ready")
        var_ready = sem("var_ready")
        root_ready = sem("root_ready")
        o_done = [sem(f"o_done{t}") for t in range(TT)]
        res_done = sem("res_done")
        ln_stat = sem("ln_stat")
        x_done = [sem(f"x_done{t}") for t in range(TT)]
        x_affine = sem("x_affine")
        x_final = sem("x_final")
        kq_act = sem("kq_act")
        kq_dve = sem("kq_dve")
        s_ps = sem("s_ps")
        s_ready = sem("s_ready")
        s_ready_raw = sem("s_ready_raw")
        p_ready = sem("p_ready")
        a_ready = sem("a_ready")
        at_ps = sem("at_ps")
        at_ready = sem("at_ready")
        parts_ps = sem("parts_ps")
        parts_ready = sem("parts_ready")
        logit_ps = sem("logit_ps")
        logit_ready = sem("logit_ready")
        rexp_ready = sem("rexp_ready")
        routed = sem("routed")
        rank_ps = sem("rank_ps")
        slots_ready = sem("slots_ready")
        pick_ready = sem("pick_ready")
        pickg_ready = sem("pickg_ready")
        xe_ps = sem("xe_ps")
        xe_act = sem("xe_act")
        xe_dve = sem("xe_dve")
        gate_ps = sem("gate_ps")
        silu_ready = sem("silu_ready")
        up_ps = sem("up_ps")
        h_ready = sem("h_ready")
        ht_ps = sem("ht_ps")
        ht_ready = sem("ht_ready")
        put_ps = sem("put_ps")
        put_done = sem("put_done")
        yc_ps = sem("yc_ps")
        yd_ps = sem("yd_ps")
        ys_act = sem("ys_act")
        ys_dve = sem("ys_dve")
        acc_ps = sem("acc_ps")
        o_free = sem("o_free")
        op_ready = sem("op_ready")
        opg_ready = sem("opg_ready")
        oxe_ps = sem("oxe_ps")
        oxe_ready = sem("oxe_ready")
        oput_ps = sem("oput_ps")
        oput_done = sem("oput_done")
        ogu_ps = sem("ogu_ps")
        osilu_ready = sem("osilu_ready")
        oh_done = sem("oh_done")
        oht_ps = sem("oht_ps")
        oht_ready = sem("oht_ready")
        oy_ps = sem("oy_ps")
        oys_act = sem("oys_act")
        oys_done = sem("oys_done")

        taken = {}
        for n in (V0, V1):
            taken[n, 0], taken[n, 1] = (v_act, n + 1), (v_dve, n + 1)
        for hp, n in enumerate(HP):
            taken[n, 0], taken[n, 1] = (sg_ready, hp + 1), (q_used, hp + 1)
        for i, n in enumerate((G0, G1)):
            taken[n, 0], taken[n, 1] = (g_ready, 2 * i + 1), (g_ready, 2 * i + 2)
        for i, n in enumerate((AO0, AO1)):
            taken[n, 0], taken[n, 1] = (res_done, 2 * i + 1), (res_done, 2 * i + 2)
        for i, n in enumerate((K0, Q0, K1, Q1)):
            taken[n, 0], taken[n, 1] = (kq_act, i + 1), (kq_dve, i + 1)
        for i, n in enumerate((BV0, BV1)):
            taken[n, 0], taken[n, 1] = (v_act, i + 3), (v_dve, i + 3)

        def ln_col(i, bias, k):
            layer, which = divmod(i, 2)
            at = 25 + (4 * which + 2 * bias + layer) * KT + k
            return pcol[:, at:at + 1]

        def place_of(n):
            return int(n in (V1, Q0))

        def before(n):
            return max((m for m in range(n) if place_of(m) == place_of(n)), default=None)

        def arrival(n, j):
            return dense_in[place_of(n)][j], 16 * sum(place_of(m) == place_of(n) for m in range(n + 1))

        def multiplied(n, j):
            if j or n in COLUMNS:
                return proj_ready, 2 * n + j + 1
            return rows_half, sum(m not in COLUMNS for m in range(n + 1))

        def parts_of(n, j):
            i = 2 * SPLIT.index(n) + j
            return i % PARTS, i + 1

        def half_before(n, j):
            i = 2 * SPLIT.index(n) + j - PARTS
            return (SPLIT[i // 2], i % 2) if i >= 0 else None

        def low_made(n, j):
            by_pool = (n, j) in POOL_HALVES
            count = sum(((m, i) in POOL_HALVES) == by_pool for m in SPLIT for i in range(2) if (m, i) <= (n, j))
            return (lo_pool if by_pool else lo_ready), count

        block = ctx.enter_context(nc.Block())

        @block.sync
        def _(sp):
            def cols(w, first):
                return w[:, first:first + COLS].rearrange("(k p) n -> p k n", p=P)

            w_in, kv = ins["a_w_in"][0], ins["kv_w"]
            w_q, a_out, b_out = ins["b_w_q"][0], ins["a_w_out"][0], ins["b_w_out"][0]
            source = {V0: (w_in, 2 * D), V1: (w_in, 2 * D + COLS), G0: (w_in, 3 * D), G1: (w_in, 3 * D + COLS),
                      AO0: (a_out, 0), AO1: (a_out, COLS), K0: (kv, 0), K1: (kv, COLS), Q0: (w_q, 0),
                      Q1: (w_q, COLS), BV0: (kv, D), BV1: (kv, D + COLS), BO0: (b_out, 0), BO1: (b_out, COLS)}

            def used(n, j):
                if n in SPLIT:
                    sp.wait_ge(*low_made(n, j))
                else:
                    sp.wait_ge(*multiplied(n, j))

            def load_dense(n):
                for j in range(2):
                    if before(n) is not None:
                        used(before(n), j)
                    if n in HP:
                        at = (D, 0)[j] + (n - HP0) * HALF
                        w = w_in[:, at:at + HALF].rearrange("(k p) n -> p k n", p=P)
                    else:
                        w = cols(*source[n])[:, :, j * HALF:(j + 1) * HALF]
                    sp.dma_start(dense[:, place_of(n), :, j * HALF:(j + 1) * HALF], w
                                 ).then_inc(dense_in[place_of(n)][j], 16)

            wg, wu, wd = ins["moe_w_gate"], ins["moe_w_up"], ins["moe_w_down"]

            UP, DOWN, ODD_GATE, EVEN_GATE = range(4)

            def load_matrix(layer, which, e, index):
                src, dst, arrived = ((wu, w_up, up_in), (wd, w_down, down_in), (wg, w_gate, odd_gate_in),
                                     (wg, dense, even_gate_in))[which]
                sp.dma_start(dst[:, e, :, :], src[layer, bass.ds(index, 1)].rearrange("one (k p) n -> p (one k) n", p=P)
                             ).then_inc(arrived, 16)

            def read_by(which, pairs):
                sp.wait_ge((up_ps, yd_ps, gate_ps, gate_ps)[which], pairs)

            finished = sp.alloc_register("sp_finished")
            sp.reg_mov(finished, 1)

            def count_overflow(pair):
                for e in range(2):
                    count = sp.value_load(extra[0:1, bass.ds(2 * pair + e, 1)], min_val=0, max_val=T // SLOTS)
                    sp.reg_add(finished, finished, count)

            sp.dma_start(x[:, 0, :], ins["x"][0, 0:P, :]).then_inc(x_in, 16)
            sp.dma_start(x[:, 1, :], ins["x"][0, P:T, :]).then_inc(x_in, 16)
            for layer in range(LAYERS):
                blocks = range(V0, AO1 + 1) if layer == 0 else range(K0 + 2, BO1 + 1)
                if layer == 0:
                    load_dense(V0)
                    load_dense(V1)
                    blocks = blocks[2:]
                if layer:
                    read_by(DOWN, PAIRS)
                load_dense(blocks[0])
                load_matrix(layer, DOWN, 0, 0)
                load_dense(blocks[1])
                used((V1, Q0)[layer], 1)
                load_matrix(layer, EVEN_GATE, 1, 1)
                for n in blocks[2:]:
                    load_dense(n)
                    if n == blocks[2]:
                        load_matrix(layer, DOWN, 1, 1)
                used(blocks[-1], 1)
                load_matrix(layer, EVEN_GATE, 0, 0)
                sp.wait_ge(*multiplied(blocks[-1], 1))
                load_matrix(layer, UP, 0, 0)
                load_matrix(layer, UP, 1, 1)
                for e in range(2):
                    load_matrix(layer, ODD_GATE, e, 2 + e)
                sp.wait_ge(slots_ready, layer + 1)

                def load_pair(which, pair, pairs):
                    read_by(which, pairs)
                    sp.wait_ge(o_free, finished)
                    for e in range(2):
                        load_matrix(layer, which, e, 2 * pair + e)

                def load_step(p, pairs, gate):
                    count_overflow(p - 1)
                    load_pair(gate, p + 1, pairs)
                    load_pair(UP, p, pairs)
                    load_pair(DOWN, p, pairs)

                done_pairs = PAIRS * layer
                with sp.Fori(1, PAIRS - 3, 2) as p:
                    odd_pairs, even_pairs = done_pairs + p, done_pairs + p + 1
                    load_step(p, odd_pairs, EVEN_GATE)
                    load_step(p + 1, even_pairs, ODD_GATE)
                load_step(PAIRS - 3, done_pairs + PAIRS - 3, EVEN_GATE)
                for p in (PAIRS - 2, PAIRS - 1):
                    count_overflow(p - 1)
                    if p == PAIRS - 1:
                        load_pair(ODD_GATE, p, done_pairs + PAIRS - 2)
                    load_pair(UP, p, done_pairs + p)
                    load_pair(DOWN, p, done_pairs + p)
                count_overflow(PAIRS - 1)
                if layer == 0:
                    load_dense(K0)
                    load_dense(Q0)
            for t in range(TT):
                sp.wait_ge(x_final, t + 1)
                sp.dma_start(out[0, t * P:(t + 1) * P, :], x[:, t, :]).then_inc(out_sem, 16)
            sp.wait_ge(out_sem, 16 * TT)

        @block.gpsimd
        def _(pool):
            steps = [0]

            def step(instr):
                steps[0] += 1
                instr.then_inc(pool_step, 1)
                pool.wait_ge(pool_step, steps[0])

            step(pool.memset(ones[:, :], 1.0))
            pool.affine_select(out=ident[:, :], in_=ones[:, :], compare_op=ALU.is_equal, fill=0.0,
                               base=0, pattern=[[-1, P]], channel_multiplier=1).then_inc(consts_ready, 1)
            pool.wait_ge(consts_ready, 1)
            pool.affine_select(out=later[:, :], in_=ones[:, :], compare_op=ALU.is_gt, fill=0.0,
                               base=0, pattern=[[1, P]], channel_multiplier=-1).then_inc(consts_ready, 1)
            step(pool.memset(causal[:, :], 1))
            step(pool.affine_select(out=causal[:, :], in_=causal[:, :], compare_op=ALU.is_ge, fill=0.0,
                                    base=0, pattern=[[1, P]], channel_multiplier=-1))
            step(pool.memset(seg[:, :], 1.0))
            pool.memset(seg[:, :].rearrange("p (c n) -> p c n", n=CHUNK)[:, :, 0:1], 0.0).then_inc(consts_ready, 1)
            step(pool.memset(amask[:, :], 0.0))
            for at in (0, 2 * P):
                part = amask[:, at:at + P]
                step(pool.affine_select(out=part, in_=part, compare_op=ALU.is_ge, fill=-BIG,
                                        base=0, pattern=[[-1, P]], channel_multiplier=1))
            step(pool.iota(iota_i[:, :], pattern=[[1, T]], base=0, channel_multiplier=0))
            step(pool.tensor_copy(iota[:, :], iota_i[:, :]))
            step(pool.tensor_scalar(first_g[:, :], iota[:, 0:GROUPS], -1.0, float(GROUPS), ALU.mult, ALU.add))
            step(pool.memset(beats[:, :, :], 1.0))
            for half, sign in ((slice(0, 4), 1), (slice(4, 8), -1)):
                step(pool.affine_select(out=beats[:, :, half], in_=beats[:, :, half], compare_op=ALU.is_gt, fill=0.0,
                                        base=0, pattern=[[-sign, 4], [sign, 4]], channel_multiplier=0))
            step(pool.memset(router[:, :, E:2 * E], 0.0))
            step(pool.tensor_tensor(fold[:, :], ident[:, 0:E], ident[:, 2 * E:3 * E], ALU.add))
            for q in (2, 3):
                step(pool.tensor_tensor(fold[:, :], fold[:, :], ident[:, 2 * q * E:(2 * q + 1) * E], ALU.add))
            step(pool.memset(zeros16[:, :], 0.0))
            step(pool.memset(slot[:, :, :], -1.0))
            step(pool.memset(gate[:, :, :], 0.0))
            pool.memset(scm, 0.0).then_inc(consts_ready, 1)

            for hp in range(4):
                pool.wait_ge(ex_ready, hp + 1)
                pool.wait_ge(kk_ready, hp + 1)
                if hp:
                    pool.wait_ge(kbt_ps, hp)
                pool.tensor_tensor(ke, kk, e2, ALU.mult).then_inc(pool_step, 1)
                pool.tensor_tensor(kb, kk, e4, ALU.mult).then_inc(pool_step, 1)
                steps[0] += 2
                pool.wait_ge(pool_step, steps[0])
                for h in range(2):
                    at = h * T
                    pool.tensor_scalar(kbs[:, h, 0:CHUNK], kb[:, at:at + CHUNK],
                                       e3[:, at + 2 * CHUNK - 1:at + 2 * CHUNK], None, ALU.mult)
                    last = pool.tensor_copy(kbs[:, h, CHUNK:P], kb[:, at + CHUNK:at + P])
                last.then_inc(k_ready, 1)

            def affine(i, call):
                pool.wait_ge(ln_in, 32 * (i + 1))
                pool.wait_ge(tp_ready, 4 * call + 4)
                for j, op in enumerate((ALU.mult, ALU.add)):
                    last = pool.tensor_tensor(x[:, :, :], x[:, :, :],
                                              ln_gb[:, j, :].unsqueeze(1).to_broadcast([P, TT, D]), op)
                    if j == 0:
                        step(last)
                last.then_inc(x_affine, 1)

            for layer in range(LAYERS):
                affine(2 * layer, 3 * layer + 2)
                with pool.Fori(0, PAIRS, 1) as i:
                    pool.wait_ge(put_ps, PAIRS * layer + i + 1)
                    pool.wait_ge(pick_ready, PAIRS * layer + i + 1)
                    pool.wait_ge(slots_ready, layer + 1)
                    pool.tensor_tensor(pick_g[:, :, :, :], pick[:, :, :, :],
                                       gate[:, :, bass.ds(2 * i, 2)].unsqueeze(3).to_broadcast([P, TT, 2, SLOTS]),
                                       ALU.mult).then_inc(pickg_ready, 1)
                if layer == 0:
                    affine(1, 3)
                    for n, j in POOL_HALVES:
                        slot_, count = parts_of(n, j)
                        pool.wait_ge(hi_ready, count)
                        cols = slice(j * HALF, (j + 1) * HALF)
                        pool.tensor_tensor(w_lo[:, slot_], dense[:, place_of(n), :, cols],
                                           w_hi[:, slot_].bitcast(F32), ALU.subtract).then_inc(lo_pool, 1)

        @block.scalar
        def _(act):
            def load_ln(i):
                layer, which = divmod(i, 2)
                for j, name in enumerate(("g", "b")):
                    row = ins[f"ln{which + 1}_{name}"][layer:layer + 1, :]
                    act.dma_start(ln_gb[:, j, :], row.broadcast_to([P, D])).then_inc(ln_in, 16)

            act.dma_start(prow[0:16, :], ins["a_lb"].rearrange("l (h d) -> (l h) d", d=P)).then_inc(small_in, 16)
            act.dma_start(prow[16:24, :], ins["a_norm_g"][0]).then_inc(small_in, 16)
            act.dma_start(prow[24:25, :], ins["b_subln_g"]).then_inc(small_in, 16)
            for i, name in enumerate(("ln1_g", "ln1_b", "ln2_g", "ln2_b")):
                at = 25 + 2 * KT * i
                act.dma_start(prow[at:at + 2 * KT, :], ins[name].rearrange("l (k d) -> (l k) d", d=P)
                              ).then_inc(small_in, 16)
            act.dma_start(lam_in[:, :, :].rearrange("p a d -> p (a d)"),
                           ins["b_lam"].rearrange("l a d -> l (a d)").broadcast_to([P, 4 * DH])).then_inc(small_in, 16)
            act.dma_start(router[:, :, 0:E], ins["router_w"].rearrange("(k p) e -> p k e", p=P)).then_inc(router_in, 16)
            act.dma_start(router_bias[:, :], ins["router_b"].rearrange("(a e) -> a e", a=1)
                           .broadcast_to([P, E])).then_inc(router_in, 16)
            load_ln(0)

            def reload_ln(i):
                act.wait_ge(x_affine, i)
                load_ln(i)

            def normalise(i):
                act.wait_ge(ln_stat, i + 1)
                nc.scalar.activation(x[:, 1, :], x[:, 1, :], ACT.Identity, scale=rs[:, 2, 1:2], bias=rs[:, 4, 1:2]
                                     ).then_inc(x_done[1], 1)

            act.wait_ge(consts_ready, 1)
            nc.scalar.activation(rs[:, 4, 0:1], ones[:, 0:1], ACT.Copy).then_inc(table_loaded, 1)
            xt_calls = [0]

            def transposed(call, ln=None):
                xt_calls[0] += 2
                for bank in (0, 2):
                    act.wait_ge(tp_ready, 4 * call + bank + 1)
                    if ln is None:
                        last = nc.scalar.activation(xT[:, 2 * bank:2 * bank + 2, :].rearrange("p k t -> p (k t)"),
                                                    ps[:, bank, :], ACT.Copy)
                    else:
                        for j in range(2):
                            k = 2 * bank + j
                            last = nc.scalar.activation(xT[:, k, :], ps[:, bank, j * T:(j + 1) * T], ACT.Identity,
                                                        scale=ln_col(ln, 0, k), bias=ln_col(ln, 1, k))
                    last.then_inc(xT_act, 1)

            def split_x():
                act.wait_ge(xT_act, xt_calls[0])
                act.wait_ge(xT_dve, xt_calls[0])
                nc.scalar.activation(x_hi[:, :, :].rearrange("p k t -> p (k t)"), xT[:, :, :].rearrange("p k t -> p (k t)"),
                                     ACT.Copy).then_inc(x_hi_ready, 1)

            def split_scaled(call, scale):
                for bank in (0, 2):
                    act.wait_ge(tp_ready, 4 * call + bank + 1)
                    for j in range(2):
                        last = nc.scalar.activation(x_hi[:, 2 * bank + j, :], ps[:, bank, j * T:(j + 1) * T],
                                                    ACT.Identity, scale=scale(2 * bank + j))
                    last.then_inc(x_hi_ready, 1)

            def split(n, halves=(0, 1)):
                for j in halves:
                    slot_, _ = parts_of(n, j)
                    if half_before(n, j):
                        act.wait_ge(*multiplied(*half_before(n, j)))
                    act.wait_ge(*arrival(n, j))
                    cols = slice(j * HALF, (j + 1) * HALF)
                    nc.scalar.activation(w_hi[:, slot_], dense[:, place_of(n), :, cols],
                                         ACT.Copy).then_inc(hi_ready, 1)

            def take(n, j, dst, sem_done, func=ACT.Copy):
                act.wait_ge(proj_ready, 2 * n + j + 1)
                nc.scalar.activation(dst, ps[:, 4 + 2 * (n % 2) + j, :], func).then_inc(sem_done, 1)

            def heads_out(k):
                if k > 4:
                    act.wait_ge(o_ready, k)
                act.wait_ge(o_ps, k + 1)
                hp = k % 4
                bank = 3 if k < 4 else 2 + k % 2
                junk = f if k < 4 else mix[:, 6, :]
                src = ps[:, bank, :].rearrange("p (h t d) -> p h t d", h=2, t=TT)
                for h in range(2):
                    for t in range(TT):
                        at = 2 * hp + h
                        nc.scalar.activation(junk[:, (2 * h + t) * P:(2 * h + t + 1) * P], src[:, h, t, :], ACT.Square,
                                             accum_out=ss[:, t * HEADS + at:t * HEADS + at + 1])
                last = nc.scalar.activation(o[:, :, 2 * hp * P:(2 * hp + 2) * P].rearrange("p t (h d) -> p h t d", h=2),
                                            src, ACT.Copy)
                last.then_inc(o_ready, 1)

            def root(i, width):
                act.wait_ge(var_ready, i + 1)
                nc.scalar.activation(rs[:, 1, 0:width], rs[:, 0, 0:width], ACT.Sqrt).then_inc(root_ready, 1)

            roots = iter(range(6))
            transposed(0)
            split(V1)
            split_x()
            split(HP0, (0,))
            act.wait_ge(pcol_ready, 2)
            nc.scalar.activation(lb[:, :], lb[:, :], ACT.Exp).then_inc(lam_exp_ready, 1)
            act.wait_ge(lam_sum_ready, 2)
            nc.scalar.activation(lam[:, 2:4], lam[:, 0:2], ACT.Exp).then_inc(lam_exp_ready, 1)
            take(V0, 0, v[:, 0, 0:COLS], v_act)
            split(HP0, (1,))
            take(V1, 0, v[:, 0, COLS:D], v_act)
            split(HP1)
            for hp in range(4):
                take(HP[hp], 0, sg, sg_ready, ACT.Sigmoid)
                act.wait_ge(f_ready, hp + 1)
                nc.scalar.activation(lf, f, ACT.Ln).then_inc(lf_ready, 1)
                act.wait_ge(d_ready, hp + 1)
                if hp:
                    act.wait_ge(k_ready, hp)
                    act.wait_ge(q_ready, hp)
                nc.scalar.activation(e3, b, ACT.Exp)
                nc.scalar.activation(e1, d1, ACT.Exp)
                nc.scalar.activation(e2, d1, ACT.Exp, scale=-1.0)
                nc.scalar.activation(e4, d2, ACT.Exp).then_inc(ex_ready, 1)
                split(HP[hp] + 2)
                if hp:
                    heads_out(hp - 1)
                act.wait_ge(kbt_ps, hp + 1)
                nc.scalar.activation(kbT[:, :, :].rearrange("p h d -> p (h d)"), ps[:, 1, 0:2 * P],
                                     ACT.Copy).then_inc(kbt_ready, 1)
            for i, n in enumerate((G0, G1)):
                for j in range(2):
                    take(n, j, g[:, j, i * COLS:(i + 1) * COLS], g_ready, ACT.Sigmoid)
                if i == 0:
                    split(AO0)
            heads_out(3)
            root(next(roots), 2 * HEADS)
            split_scaled(1, lambda k: pcol[:, 16 + k:17 + k])
            split(AO1)

            def moe(layer):
                def overflow(count, done):
                    with act.If(count > 1):
                        with act.Fori(1, count, 1):
                            act.wait_ge(oxe_ps, done)
                            nc.scalar.activation(o_xe[:, :, :].rearrange("p k s -> p (k s)"), ps[:, BANK_A, :],
                                                 ACT.Copy).then_inc(oxe_ready, 1)
                            act.wait_ge(ogu_ps, done)
                            nc.scalar.activation(o_silu[SLOTS:P, :], ps[0:SLOTS, BANK_C, :],
                                                 ACT.Silu).then_inc(osilu_ready, 1)
                            act.wait_ge(oht_ps, done)
                            nc.scalar.activation(o_hT[:, :, :].rearrange("p j s -> p (j s)"),
                                                 ps[:, BANK_A, 0:FT * SLOTS], ACT.Copy).then_inc(oht_ready, 1)
                            act.wait_ge(oy_ps, done)
                            nc.scalar.activation(o_ys[:, 0:COLS], ps[0:SLOTS, BANK_C, :], ACT.Copy).then_inc(oys_act, 1)
                            act.reg_add(done, done, 1)

                def take_xe(value):
                    act.wait_ge(xe_ps, value)
                    nc.scalar.activation(xe[:, 0:KT // 2, :].rearrange("p k s -> p (k s)"), ps[:, BANK_C, :],
                                         ACT.Copy).then_inc(xe_act, 1)

                act.wait_ge(routed, layer + 1)
                nc.scalar.activation(ys[:, 0:COLS], seg[:, :], ACT.Copy, scale=0.0).then_inc(ys_act, 1)
                take_xe(PAIRS * layer + 1)
                act.wait_ge(slots_ready, layer + 1)

                def experts(i, last=False):
                    count_a = act.value_load(chunks[0:1, bass.ds(2 * i, 1)], min_val=0, max_val=T // SLOTS)
                    count_b = act.value_load(chunks[0:1, bass.ds(2 * i + 1, 1)], min_val=0, max_val=T // SLOTS)
                    pair = PAIRS * layer + i
                    act.wait_ge(gate_ps, pair + 1)
                    nc.scalar.activation(silu[:, :], ps[:, BANK_A, :], ACT.Silu).then_inc(silu_ready, 1)
                    overflow(count_a, done)
                    overflow(count_b, done)
                    if not last:
                        take_xe(pair + 2)
                    act.wait_ge(ht_ps, pair + 1)
                    nc.scalar.activation(hT[:, :, :].rearrange("p j s -> p (j s)"), ps[:, BANK_A, :],
                                         ACT.Copy).then_inc(ht_ready, 1)
                    act.wait_ge(yc_ps, pair + 1)
                    nc.scalar.activation(ys[:, 0:COLS], ps[:, BANK_C, :], ACT.Copy).then_inc(ys_act, 1)

                with act.Fori(0, PAIRS - 1, 1) as i:
                    experts(i)
                experts(PAIRS - 1, last=True)

            def router_exp(layer):
                act.wait_ge(logit_ready, layer + 1)
                nc.scalar.activation(rt[:, 1, :], rt[:, 0, :], ACT.Exp).then_inc(rexp_ready, 1)

            done = act.alloc_register("act_done")
            act.reg_mov(done, 1)
            root(next(roots), TT)
            normalise(0)
            transposed(2, 0)
            router_exp(0)
            reload_ln(1)
            moe(0)
            root(next(roots), TT)
            normalise(1)
            act.wait_ge(acc_ps, PAIRS + 2)
            split(Q0)
            transposed(3, 1)
            split_x()
            split(K1, (0,))
            reload_ln(2)
            def take_kq(i):
                dst = (kT, qT)[i % 2]
                take((K0, Q0, K1, Q1)[i], 0, dst[:, 4 * (i // 2):4 * (i // 2) + 2, :].rearrange("p h t -> p (h t)"), kq_act)

            def probabilities(h):
                u = h % 2
                act.wait_ge(s_ready, h + 1)
                if h >= 2:
                    act.wait_ge(a_ready, h - 1)
                for c in range(2):
                    for qt, (lo, hi) in enumerate(((0, P), (P, 3 * P))):
                        at = 2 * qt + c
                        last = nc.scalar.activation(s_ex[:, u, c, lo:hi], s_in[:, u, c, lo:hi], ACT.Exp,
                                                    bias=amx[:, u, at:at + 1], scale=SCALE,
                                                    accum_out=asum[:, u, at:at + 1])
                last.then_inc(p_ready, 1)

            take_kq(0)
            take_kq(1)
            split(K1, (1,))
            split(Q1, (0,))
            take_kq(2)
            split(Q1, (1,))
            split(BV0, (0,))
            probabilities(0)
            probabilities(1)
            take_kq(3)
            split(BV0, (1,))
            split(BV1, (0,))
            for h in range(2, 4):
                probabilities(h)
            take(BV0, 0, v[:, 0, 0:COLS], v_act)
            split(BV1, (1,))
            split(BO0, (0,))
            for h in range(4, 6):
                probabilities(h)
            take(BV1, 0, v[:, 0, COLS:D], v_act)
            for h in range(6, 8):
                probabilities(h)
            split(BO0, (1,))
            act.wait_ge(p_ready, HEADS)
            for hp in range(4):
                for h in (2 * hp, 2 * hp + 1):
                    act.wait_ge(at_ps, h + 1)
                    nc.scalar.activation(aT[:, h % 2, 0:3, :].rearrange("p s n -> p (s n)"), ps[:, h % 2, 0:3 * P],
                                         ACT.Copy).then_inc(at_ready, 1)
                if hp:
                    heads_out(4 + hp - 1)
            heads_out(7)
            root(next(roots), 2 * HEADS)
            split_scaled(4, lambda k: pcol[:, 24:25])
            split(BO1)
            root(next(roots), TT)
            normalise(2)
            transposed(5, 2)
            router_exp(1)
            reload_ln(3)
            moe(1)
            root(next(roots), TT)

        @block.vector
        def _(dve):
            V = nc.vector
            steps = [0]

            def step(instr):
                steps[0] += 1
                instr.then_inc(dve_step, 1)
                dve.wait_ge(dve_step, steps[0])

            def transposed(call, ln=None):
                for bank in (1, 3):
                    dve.wait_ge(tp_ready, 4 * call + bank + 1)
                    if ln is None:
                        last = V.tensor_copy(xT[:, 2 * bank:2 * bank + 2, :].rearrange("p k t -> p (k t)"),
                                             ps[:, bank, :])
                    else:
                        for j in range(2):
                            k = 2 * bank + j
                            last = V.tensor_scalar(xT[:, k, :], ps[:, bank, j * T:(j + 1) * T], ln_col(ln, 0, k),
                                                   ln_col(ln, 1, k), ALU.mult, ALU.add)
                    last.then_inc(xT_dve, 1)

            def split_x(high):
                dve.wait_ge(x_hi_ready, high)
                V.tensor_tensor(x_lo[:, :, :], xT[:, :, :], x_hi[:, :, :].bitcast(F32), ALU.subtract).then_inc(x_lo_ready, 1)

            def split_scaled(i, call, high, scale):
                for bank in (1, 3):
                    dve.wait_ge(tp_ready, 4 * call + bank + 1)
                    for j in range(2):
                        k = 2 * bank + j
                        last = V.tensor_scalar(x_hi[:, k, :], ps[:, bank, j * T:(j + 1) * T], scale(k), None, ALU.mult)
                    last.then_inc(x_hi_dve, 1)
                dve.wait_ge(x_hi_ready, high)
                dve.wait_ge(x_hi_dve, 2 * i + 2)
                for k in range(KT):
                    last = V.scalar_tensor_tensor(x_lo[:, k, :], ps[:, k // 2, (k % 2) * T:(k % 2 + 1) * T], scale(k),
                                                  x_hi[:, k, :].bitcast(F32), ALU.mult, ALU.subtract)
                last.then_inc(x_lo_ready, 1)

            def split(n, halves=(0, 1)):
                for j in halves:
                    if (n, j) in POOL_HALVES:
                        continue
                    slot_, count = parts_of(n, j)
                    dve.wait_ge(hi_ready, count)
                    cols = slice(j * HALF, (j + 1) * HALF)
                    V.tensor_tensor(w_lo[:, slot_], dense[:, place_of(n), :, cols],
                                    w_hi[:, slot_].bitcast(F32), ALU.subtract).then_inc(lo_ready, 1)

            def take(n, j, dst, sem_done):
                dve.wait_ge(proj_ready, 2 * n + j + 1)
                V.tensor_copy(dst, ps[:, 4 + 2 * (n % 2) + j, :]).then_inc(sem_done, 1)

            def rstd(i, width):
                dve.wait_ge(root_ready, i + 1)
                var, root, y, t = (rs[:, r, 0:width] for r in range(4))
                step(V.reciprocal(y, root))
                step(V.tensor_tensor(t, y, y, ALU.mult))
                step(V.tensor_tensor(t, t, var, ALU.mult))
                step(V.tensor_scalar(t, t, -0.5, 1.5, ALU.mult, ALU.add))
                return V.tensor_tensor(y, y, t, ALU.mult)

            norms = iter(range(4))
            roots = iter(range(6))

            def layer_norm(final=False):
                i = next(norms)
                step(V.memset(rs[:, 4, :], 0.0))
                for t in range(TT):
                    last = V.bn_aggr(mv[:, t, :], stats[:, t, :, :].rearrange("p a b -> p (a b)"))
                step(last)
                V.tensor_scalar(rs[:, 0, 0:TT].unsqueeze(2), mv[:, :, 1:2], LN_EPS, None, ALU.add).then_inc(var_ready, 1)
                step(rstd(next(roots), TT))
                if final:
                    dve.wait_ge(ln_in, 32 * (i + 1))
                    for t in range(TT):
                        step(V.scalar_tensor_tensor(x[:, t, :], x[:, t, :], mv[:, t, 0:1], ln_gb[:, 0, :],
                                                    ALU.subtract, ALU.mult))
                        V.scalar_tensor_tensor(x[:, t, :], x[:, t, :], rs[:, 2, t:t + 1], ln_gb[:, 1, :],
                                               ALU.mult, ALU.add).then_inc(x_final, 1)
                    return
                V.scalar_tensor_tensor(rs[:, 4, 1:2], mv[:, 1, 0:1], -1.0, rs[:, 2, 1:2], ALU.mult, ALU.mult
                                       ).then_inc(ln_stat, 1)
                V.tensor_scalar(x[:, 0, :], x[:, 0, :], mv[:, 0, 0:1], rs[:, 2, 0:1], ALU.subtract, ALU.mult
                                ).then_inc(x_done[0], 1)

            added = [0]

            def residual(t, half, addend):
                cols = x[:, t, half * COLS:(half + 1) * COLS]
                added[0] += 1
                V.scalar_tensor_tensor(cols, cols, ALPHA, addend, ALU.mult, ALU.add).then_inc(res_done, 1)
                dve.wait_ge(res_done, added[0])
                V.bn_stats(stats[:, t, half, :], cols)

            def residual_projection(n):
                for t in range(TT):
                    dve.wait_ge(proj_ready, 2 * n + t + 1)
                    residual(t, n % 2, ps[:, 4 + 2 * (n % 2) + t, :])

            transposed(0)
            split(V1)
            split_x(1)
            dve.wait_ge(consts_ready, 4)
            split(HP0, (0,))
            dve.wait_ge(small_in, SMALL)
            for i in range(2):
                step(V.tensor_tensor(lam_p[:, i, :], lam_in[:, 2 * i, :], lam_in[:, 2 * i + 1, :], ALU.mult))
                V.reduce_sum(lam[:, i:i + 1], lam_p[:, i, :], axis=AX.X).then_inc(lam_sum_ready, 1)
            dve.wait_ge(pcol_ready, 1)
            step(V.tensor_copy(pcol[:, :], ps[:, 0, 0:25 + 8 * KT]))
            a0, a1 = pcol[:, 0:8], pcol[:, 8:16]
            step(V.tensor_tensor(rs[:, 0, 0:8], a0, a1, ALU.max))
            step(V.tensor_tensor(lb[:, 0:8], a0, rs[:, 0, 0:8], ALU.subtract))
            V.tensor_tensor(lb[:, 8:16], a1, rs[:, 0, 0:8], ALU.subtract).then_inc(pcol_ready, 1)
            dve.wait_ge(lam_exp_ready, 1)
            step(V.tensor_tensor(rs[:, 0, 0:8], lb[:, 0:8], lb[:, 8:16], ALU.add))
            step(V.reciprocal(rs[:, 1, 0:8], rs[:, 0, 0:8]))
            step(V.tensor_tensor(lb[:, 0:8], lb[:, 0:8], rs[:, 1, 0:8], ALU.mult))
            step(V.tensor_scalar(lb[:, 8:16], lb[:, 0:8], -1.0, 1.0, ALU.mult, ALU.add))
            step(V.tensor_scalar(pcol[:, 24:25], pcol[:, 24:25], 1.0 - LAMBDA_INIT, None, ALU.mult))
            dve.wait_ge(lam_exp_ready, 2)
            step(V.tensor_tensor(lam[:, 5:6], lam[:, 3:4], lam[:, 2:3], ALU.subtract))
            step(V.tensor_scalar(lam[:, 4:5], lam[:, 5:6], -LAMBDA_INIT, None, ALU.add))
            take(V0, 1, v[:, 1, 0:COLS], v_dve)
            split(HP0, (1,))
            take(V1, 1, v[:, 1, COLS:D], v_dve)
            split(HP1)

            def chunks_of(ap):
                return ap.rearrange("p (c n) -> p c n", n=CHUNK)

            def state_out(hp):
                dve.wait_ge(st_ps, hp + 1)
                V.tensor_copy(state[:, :, :].rearrange("p h d -> p (h d)"), ps[:, 2, 0:2 * P]).then_inc(st_ready, 1)

            for hp in range(4):
                dve.wait_ge(sg_ready, hp + 1)
                if hp:
                    dve.wait_ge(k_ready, hp)
                for h in range(2):
                    at = 2 * hp + h
                    last = V.tensor_scalar(f[:, h * T:(h + 1) * T], sg[:, h * T:(h + 1) * T],
                                           lb[:, 8 + at:9 + at], lb[:, at:at + 1], ALU.mult, ALU.add)
                last.then_inc(f_ready, 1)
                dve.wait_ge(f_ready, hp + 1)
                V.tensor_scalar(kk, f, -1.0, 1.0, ALU.mult, ALU.add).then_inc(kk_ready, 1)
                dve.wait_ge(lf_ready, hp + 1)
                step(V.tensor_tensor_scan(b, seg[:, :], lf, 0.0, ALU.mult, ALU.add))
                bc = chunks_of(b)
                V.tensor_tensor(chunks_of(d1), bc, bc[:, :, CHUNK // 2 - 1:CHUNK // 2].to_broadcast([P, 8, CHUNK]),
                                ALU.subtract)
                V.tensor_tensor(chunks_of(d2), bc[:, :, CHUNK - 1:CHUNK].to_broadcast([P, 8, CHUNK]), bc,
                                ALU.subtract).then_inc(d_ready, 1)
                if hp:
                    state_out(hp - 1)
                dve.wait_ge(ex_ready, hp + 1)
                dve.wait_ge(proj_ready, 2 * HP[hp] + 2)
                if hp:
                    dve.wait_ge(sc_ready, hp)
                q = ps[:, 4 + 2 * (HP[hp] % 2) + 1, :]
                V.tensor_tensor(qe, q, e1, ALU.mult)
                V.tensor_tensor(qb, q, e3, ALU.mult).then_inc(q_used, 1)
                dve.wait_ge(q_used, hp + 1)
                if hp >= 2:
                    dve.wait_ge(o_ps, hp - 1)
                for h in range(2):
                    at = h * T + P
                    V.tensor_copy(qbs[:, hp % 2, h, 0:CHUNK], qb[:, at:at + CHUNK])
                    last = V.tensor_scalar(qbs[:, hp % 2, h, CHUNK:P], qb[:, at + CHUNK:at + P],
                                           e3[:, at + CHUNK - 1:at + CHUNK], None, ALU.mult)
                last.then_inc(q_ready, 1)
                split(HP[hp] + 2)
                dve.wait_ge(sc_ready, hp + 1)
                V.copy_predicated(scm.rearrange("p (u t) -> p u t", t=P),
                                  causal[:, :].unsqueeze(1).to_broadcast([P, 4, P]),
                                  ps[:, 0, :].rearrange("p (u t) -> p u t", t=P)).then_inc(scm_ready, 1)
            state_out(3)
            split(AO0)

            def rms(call, pairs, meanwhile=None):
                dve.wait_ge(o_ready, pairs)
                instr = V.tensor_scalar(rs[:, 0, :], ss[:, :], 1.0 / P, RMS_EPS, ALU.mult, ALU.add)
                instr.then_inc(var_ready, 1)
                if meanwhile:
                    meanwhile()
                step(rstd(call, 2 * HEADS))

            def by_head(t):
                return (o[:, t, :].rearrange("p (h d) -> p h d", h=HEADS),
                        rs[:, 2, t * HEADS:(t + 1) * HEADS].unsqueeze(2).to_broadcast([P, HEADS, P]))

            dve.wait_ge(o_ready, 3)
            dve.wait_ge(g_ready, 4)
            most, rest = slice(0, D - 2 * P), slice(D - 2 * P, D)
            V.tensor_tensor(o[:, :, most], o[:, :, most], g[:, :, most], ALU.mult)
            rms(next(roots), 4, lambda: step(V.tensor_tensor(o[:, :, rest], o[:, :, rest], g[:, :, rest], ALU.mult)))
            for t in range(TT):
                oh, r = by_head(t)
                V.tensor_tensor(oh, oh, r, ALU.mult).then_inc(o_done[t], 1)
            split_scaled(0, 1, 3, lambda k: pcol[:, 16 + k:17 + k])
            split(AO1)
            residual_projection(AO0)
            residual_projection(AO1)
            layer_norm()
            transposed(2, 0)

            def pick_pair(index):
                V.tensor_tensor(pick[:, :, :, :],
                                iota[:, 0:SLOTS].unsqueeze(1).unsqueeze(1).to_broadcast([P, TT, 2, SLOTS]),
                                slot[:, :, bass.ds(index, 2)].unsqueeze(3).to_broadcast([P, TT, 2, SLOTS]),
                                ALU.is_equal).then_inc(pick_ready, 1)

            def route(layer):
                N = TT * E

                def te(ap):
                    return ap.rearrange("p (t e) -> p t e", t=TT)

                def pick_first(src, width, const, tmp, result):
                    n = TT
                    m, eq, val = tmp
                    step(V.reduce_max(m, src, axis=AX.X))
                    step(V.tensor_tensor(eq, src, m.unsqueeze(2).to_broadcast([P, n, width]), ALU.is_equal))
                    step(V.tensor_tensor(val, eq, const.unsqueeze(1).to_broadcast([P, n, width]), ALU.mult))
                    step(V.reduce_max(m, val, axis=AX.X))
                    step(V.tensor_tensor(result, val, m.unsqueeze(2).to_broadcast([P, n, width]), ALU.is_equal))

                lg, ex, probs, sel, lost, in_top, best2 = (rt[:, i, :] for i in range(7))
                both, pm, tmp_a = (rt[:, i, :] for i in range(8, 11))
                m2 = rg[:, 0, 0:TT]
                dve.wait_ge(parts_ps, layer + 1)
                V.tensor_copy(logit_parts[:, :], ps[:, BANK_A, 0:T]).then_inc(parts_ready, 1)
                dve.wait_ge(logit_ps, layer + 1)
                raw = te(ps[:, BANK_A, 0:N])
                step(V.reduce_max(m2, raw, axis=AX.X))
                V.tensor_tensor(te(lg), raw, m2.unsqueeze(2).to_broadcast([P, TT, E]), ALU.subtract
                                ).then_inc(logit_ready, 1)
                dve.wait_ge(rexp_ready, layer + 1)
                step(V.reduce_sum(m2, te(ex), axis=AX.X))
                step(V.reciprocal(rg[:, 1, 0:TT], m2))
                step(V.tensor_tensor(te(probs), te(ex), rg[:, 1, 0:TT].unsqueeze(2).to_broadcast([P, TT, E]), ALU.mult))
                step(V.tensor_tensor(te(sel), te(probs), router_bias[:, :].unsqueeze(1).to_broadcast([P, TT, E]), ALU.add))
                NG = TT * GROUPS
                four = sel.rearrange("p (g e) -> p g e", e=4)
                other, this = (four.unsqueeze(axis).to_broadcast([P, NG, 4, 4]) for axis in (2, 3))
                V.tensor_tensor(versus[:, :, :, 0:4], other, this, ALU.is_gt)
                step(V.tensor_tensor(versus[:, :, :, 4:8], other, this, ALU.is_ge))
                step(V.tensor_tensor(versus[:, :, :, :], versus[:, :, :, :],
                                     beats[:, :, :].unsqueeze(1).to_broadcast([P, NG, 4, 8]), ALU.mult))
                step(V.reduce_sum(lost.rearrange("p (g e) -> p g e", e=4), versus[:, :, :, :], axis=AX.X))
                step(V.tensor_scalar(in_top, lost, 1.5, None, ALU.is_lt))
                step(V.tensor_tensor(best2, sel, in_top, ALU.mult))
                gs = rg[:, 7, 0:NG]
                step(V.reduce_sum(gs, best2.rearrange("p (g e) -> p g e", e=4), axis=AX.X))

                def tg(ap):
                    return ap.rearrange("p (t g) -> p t g", t=TT)

                ohg = rg[:, 8, 0:NG]
                pick_first(tg(gs), GROUPS, first_g[:, :], (m2, tg(rg[:, 9, 0:NG]), tg(rg[:, 10, 0:NG])), tg(ohg))
                V.tensor_tensor(both.rearrange("p (g e) -> p g e", e=4), in_top.rearrange("p (g e) -> p g e", e=4),
                                ohg.unsqueeze(2).to_broadcast([P, NG, 4]), ALU.mult).then_inc(routed, 1)
                dve.wait_ge(routed, layer + 1)
                step(V.tensor_tensor(pm, probs, both, ALU.mult))
                step(V.reduce_sum(m2, te(pm), axis=AX.X))
                step(V.reciprocal(rg[:, 1, 0:TT], m2))
                V.tensor_tensor(gate[:, :, 0:E], te(pm), rg[:, 1, 0:TT].unsqueeze(2).to_broadcast([P, TT, E]), ALU.mult)
                V.memset(ys[:, COLS:D], 0.0).then_inc(ys_dve, 1)
                V.memset(put[:, :], 0.0).then_inc(put_done, 1)
                dve.wait_ge(rank_ps, layer + 1)
                step(V.scalar_tensor_tensor(tmp_a, ps[:, BANK_B, 0:N], 1.0, both, ALU.add, ALU.mult))
                step(V.tensor_scalar(slot[:, :, 0:E], te(tmp_a), -1.0, None, ALU.add))
                pick_pair(0)
                step(V.tensor_copy(count_f[0:1, 0, :], ps[0:1, BANK_B, N:N + E]))
                step(V.tensor_scalar(count_f[0:1, 1, :], count_f[0:1, 0, :], float(SLOTS), None, ALU.is_gt))
                for c in range(2, T // SLOTS):
                    step(V.tensor_scalar(count_f[0:1, 2, :], count_f[0:1, 0, :], float(c * SLOTS), None, ALU.is_gt))
                    step(V.tensor_tensor(count_f[0:1, 1, :], count_f[0:1, 1, :], count_f[0:1, 2, :], ALU.add))
                V.tensor_copy(extra[:, :], count_f[0:1, 1, :])
                V.tensor_scalar(chunks[:, :], count_f[0:1, 1, :], 1.0, None, ALU.add).then_inc(slots_ready, 1)
                dve.wait_ge(slots_ready, layer + 1)

            def moe(layer):
                def overflow(count, done, index):
                    with dve.If(count > 1):
                        with dve.Fori(1, count, 1) as c:
                            dve.wait_ge(o_free, done)
                            V.tensor_tensor(o_pick, iota[:, bass.ds(SLOTS * c, SLOTS)].unsqueeze(1)
                                            .to_broadcast([P, TT, SLOTS]),
                                            slot[:, :, bass.ds(index, 1)].to_broadcast([P, TT, SLOTS]),
                                            ALU.is_equal).then_inc(op_ready, 1)
                            dve.wait_ge(op_ready, done)
                            V.tensor_tensor(o_pick_g, o_pick, gate[:, :, bass.ds(index, 1)].to_broadcast([P, TT, SLOTS]),
                                            ALU.mult).then_inc(opg_ready, 1)
                            dve.wait_ge(ogu_ps, done)
                            dve.wait_ge(osilu_ready, done)
                            V.tensor_tensor(o_h[:, :], ps[SLOTS:P, BANK_D, :], o_silu[SLOTS:P, :],
                                            ALU.mult).then_inc(oh_done, 1)
                            dve.wait_ge(oput_ps, done)
                            V.tensor_copy(o_put[:, :], ps[0:SLOTS, BANK_B, 0:T]).then_inc(oput_done, 1)
                            dve.wait_ge(oy_ps, done)
                            V.tensor_copy(o_ys[:, COLS:D], ps[SLOTS:P, BANK_D, :]).then_inc(oys_done, 1)
                            dve.reg_add(done, done, 1)

                def take_xe(value):
                    dve.wait_ge(xe_ps, value)
                    V.tensor_copy(xe[:, KT // 2:KT, :].rearrange("p k s -> p (k s)"), ps[:, BANK_D, :]
                                  ).then_inc(xe_dve, 1)

                take_xe(PAIRS * layer + 1)

                def experts(i, last=False):
                    count_a = dve.value_load(chunks[0:1, bass.ds(2 * i, 1)], min_val=0, max_val=T // SLOTS)
                    count_b = dve.value_load(chunks[0:1, bass.ds(2 * i + 1, 1)], min_val=0, max_val=T // SLOTS)
                    pair = PAIRS * layer + i
                    if not last:
                        dve.wait_ge(pickg_ready, pair + 1)
                        pick_pair(2 * i + 2)
                    dve.wait_ge(up_ps, pair + 1)
                    dve.wait_ge(silu_ready, pair + 1)
                    V.tensor_tensor(hid[:, :], ps[:, BANK_B, :], silu[:, :], ALU.mult).then_inc(h_ready, 1)
                    for e, count in enumerate((count_a, count_b)):
                        overflow(count, done, 2 * i + e)
                    if not last:
                        take_xe(pair + 2)
                    dve.wait_ge(put_ps, pair + 2)
                    V.tensor_copy(put[:, :], ps[:, BANK_B, 0:T]).then_inc(put_done, 1)
                    dve.wait_ge(yd_ps, pair + 1)
                    V.tensor_copy(ys[:, COLS:D], ps[:, BANK_D, :]).then_inc(ys_dve, 1)

                with dve.Fori(0, PAIRS - 1, 1) as i:
                    experts(i)
                experts(PAIRS - 1, last=True)
                dve.wait_ge(x_affine, 2 * layer + 1)
                for t in range(TT):
                    dve.wait_ge(acc_ps, (PAIRS + 2) * layer + PAIRS + 1 + t)
                    for j in range(2):
                        residual(t, j, ps[:, 2 * t + j, :])

            done = dve.alloc_register("dve_done")
            dve.reg_mov(done, 1)
            dve.wait_ge(router_in, 32)
            route(0)
            moe(0)
            layer_norm()
            transposed(3, 1)
            split(Q0)
            split_x(4)
            split(K1, (0,))

            def take_kq(i):
                dst = (kT, qT)[i % 2]
                take((K0, Q0, K1, Q1)[i], 1, dst[:, 4 * (i // 2) + 2:4 * (i // 2) + 4, :].rearrange("p h t -> p (h t)"),
                     kq_dve)

            def masked_scores(h):
                u = h % 2
                dve.wait_ge(s_ps, h + 1)
                if h >= 2:
                    dve.wait_ge(p_ready, h - 1)
                V.tensor_tensor(s_in[:, u, :, 0:3 * P], ps[:, 2 * u:2 * u + 2, 0:3 * P],
                                amask[:, :].unsqueeze(1).to_broadcast([P, 2, 3 * P]), ALU.add).then_inc(s_ready_raw, 1)
                dve.wait_ge(s_ready_raw, h + 1)
                V.reduce_max(amx[:, u, 0:2], s_in[:, u, :, 0:P], axis=AX.X)
                step(V.reduce_max(amx[:, u, 2:4], s_in[:, u, :, P:3 * P], axis=AX.X))
                V.tensor_scalar(amx[:, u, :], amx[:, u, :], -SCALE, None, ALU.mult).then_inc(s_ready, 1)

            def weights(h):
                u = h % 2
                dve.wait_ge(p_ready, h + 1)
                step(V.reciprocal(arec[:, u, :], asum[:, u, :]))
                r = arec[:, u, :].rearrange("p (t c) -> p t c", c=2)
                step(V.tensor_scalar(r[:, :, 1:2], r[:, :, 1:2], lam[:, 4:5], None, ALU.mult))
                spans = ((0, 1), (1, 3))

                def tiles(c, lo, hi):
                    return s_ex[:, u, c, lo * P:hi * P].rearrange("p (s n) -> p s n", n=P)

                a = o3[:, :, h * P:(h + 1) * P]
                for t, (lo, hi) in enumerate(spans):
                    last = V.tensor_scalar(a[:, lo:hi, :], tiles(0, lo, hi), arec[:, u, 2 * t:2 * t + 1],
                                           None, ALU.mult)
                step(last)
                for t, (lo, hi) in enumerate(spans):
                    last = V.scalar_tensor_tensor(a[:, lo:hi, :], tiles(1, lo, hi), arec[:, u, 2 * t + 1:2 * t + 2],
                                                  a[:, lo:hi, :], ALU.mult, ALU.add)
                last.then_inc(a_ready, 1)

            take_kq(0)
            take_kq(1)
            split(K1, (1,))
            split(Q1, (0,))
            masked_scores(0)
            for h in range(1, HEADS):
                masked_scores(h)
                if h == 1:
                    take_kq(2)
                    split(Q1, (1,))
                if h == 6:
                    take(BV1, 1, v[:, 1, COLS:D], v_dve)
                weights(h - 1)
                if h == 2:
                    take_kq(3)
                    split(BV0, (1,))
                if h == 4:
                    take(BV0, 1, v[:, 1, 0:COLS], v_dve)
                    split(BV1, (1,))
            weights(HEADS - 1)
            split(BO0, (1,))
            rms(next(roots), 8)
            for t in range(TT):
                oh, r = by_head(t)
                V.tensor_tensor(oh, oh, r, ALU.mult).then_inc(o_done[t], 1)
            split_scaled(1, 4, 6, lambda k: pcol[:, 24:25])
            split(BO1)
            dve.wait_ge(x_affine, 2)
            residual_projection(BO0)
            residual_projection(BO1)
            layer_norm()
            transposed(5, 2)
            route(1)
            moe(1)
            layer_norm(final=True)

        @block.tensor
        def _(pe):
            mm = nc.tensor.matmul

            def transposes(call, src):
                for t in range(TT):
                    for k in range(KT):
                        at = (k % 2) * T + t * P
                        last = nc.tensor.transpose(ps[:, k // 2, at:at + P], src[:, t, k * P:(k + 1) * P], ident[:, :])
                        if t == 1 and k % 2:
                            last.then_inc(tp_ready, 1)
                    if t == 0:
                        yield

            def transpose_all(call, src, ready, value):
                pe.wait_ge(ready[0], value)
                for _ in transposes(call, src):
                    pe.wait_ge(ready[1], value)
                if call in (1, 4):
                    pe.wait_ge(x_hi_ready, {1: 3, 4: 6}[call])
                    pe.wait_ge(x_hi_dve, {1: 2, 4: 4}[call])
                else:
                    copied = 2 * (call + 1 - (call > 1) - (call > 4))
                    pe.wait_ge(xT_act, copied)
                    pe.wait_ge(xT_dve, copied)

            def free(n, j):
                if (n - 2, j) in taken and n not in (K0, Q0):
                    pe.wait_ge(*taken[n - 2, j])

            def products(n, j):
                if n not in SPLIT:
                    pe.wait_ge(*arrival(n, j))
                    yield dense[:, place_of(n), :, j * HALF:(j + 1) * HALF], xT
                    return
                slot_, _ = parts_of(n, j)
                pe.wait_ge(*low_made(n, j))
                pe.wait_ge(x_hi_ready, 1 + 2 * (n >= AO0) + (n >= K0) + 2 * (n >= BO0))
                yield w_hi[:, slot_], x_hi
                yield w_lo[:, slot_], x_hi
                pe.wait_ge(x_lo_ready, 1 + (n >= AO0) + (n >= K0) + (n >= BO0))
                yield w_hi[:, slot_], x_lo

            def rows(n, j):
                cols = slice(j * HALF, (j + 1) * HALF)
                if j == 0:
                    free(n, 0)
                    free(n, 1)
                total = 3 if n in SPLIT else 1
                for i, (w, xs) in enumerate(products(n, j)):
                    for t in range(TT):
                        for k in range(KT):
                            last = mm(ps[:, 4 + 2 * (n % 2) + t, cols], xs[:, k, t * P:(t + 1) * P], w[:, k, :],
                                      start=i == 0 and k == 0, stop=i == total - 1 and k == KT - 1)
                        if j and i == total - 1:
                            last.then_inc(proj_ready, 1)
                if j == 0:
                    last.then_inc(rows_half, 1)

            def columns(n, j):
                free(n, j)
                terms = list(products(n, j))
                for i in range(2):
                    c = i * P
                    for m, (w, xs) in enumerate(terms):
                        for k in range(KT):
                            last = mm(ps[:, 4 + 2 * (n % 2) + j, i * T:(i + 1) * T], w[:, k, c:c + P], xs[:, k, :],
                                      start=m == 0 and k == 0, stop=m == len(terms) - 1 and k == KT - 1)
                last.then_inc(proj_ready, 1)

            pe.wait_ge(consts_ready, 1)
            pe.wait_ge(x_in, 32)
            for _ in transposes(0, x):
                pass

            pe.wait_ge(xT_act, 2)
            pe.wait_ge(xT_dve, 2)

            def scores(hp):
                pe.wait_ge(q_ready, hp + 1)
                pe.wait_ge(k_ready, hp + 1)
                if hp:
                    pe.wait_ge(scm_ready, hp)
                else:
                    pe.wait_ge(pcol_ready, 2)
                    pe.wait_ge(kbt_ready, hp)
                for u in range(4):
                    at = u * P
                    mm(ps[:, 0, at:at + P], ke[:, at:at + P], qe[:, at:at + P], start=True, stop=True)
                    last = mm(ps[0:CHUNK, 0, at + CHUNK:at + P], kb[:, at:at + CHUNK], qb[:, at + CHUNK:at + P],
                              start=True, stop=True)
                last.then_inc(sc_ready, 1)
                for h in range(2):
                    last = nc.tensor.transpose(ps[:, 1, h * P:(h + 1) * P], kbs[:, h, :], ident[:, :])
                last.then_inc(kbt_ps, 1)

            def states(hp):
                pe.wait_ge(kbt_ready, hp + 1)
                if hp == 0:
                    pe.wait_ge(v_act, 2)
                    pe.wait_ge(v_dve, 2)
                else:
                    pe.wait_ge(st_ready, hp)
                for h in range(2):
                    head = (2 * hp + h) * P
                    last = mm(ps[:, 2, h * P:(h + 1) * P], kbT[:, h, :], v[:, 0, head:head + P], start=True, stop=True)
                last.then_inc(st_ps, 1)

            def outputs(hp):
                pe.wait_ge(scm_ready, hp + 1)
                pe.wait_ge(st_ready, hp + 1)
                if hp:
                    pe.wait_ge(o_ready, hp)
                for h in range(2):
                    head = (2 * hp + h) * P
                    for t in range(TT):
                        at = (2 * h + t) * P
                        last = mm(ps[:, 3, at:at + P], scm[:, at:at + P], v[:, t, head:head + P],
                                  start=True, stop=t == 0)
                        if t:
                            last = mm(ps[:, 3, at:at + P], qbs[:, hp % 2, h, :], state[:, h, :], start=False, stop=True)
                last.then_inc(o_ps, 1)

            rows(V0, 0)
            rows(V0, 1)
            rows(V1, 0)
            pe.wait_ge(small_in, SMALL)
            nc.tensor.transpose(ps[:, 0, 0:25 + 8 * KT], prow[:, :], ident[0:25 + 8 * KT, 0:25 + 8 * KT]).then_inc(pcol_ready, 1)
            rows(V1, 1)
            columns(HP0, 0)
            columns(HP0, 1)
            for hp, n in enumerate((HP1, HP2, HP3, G0, G1)):
                part = columns if n in HP else rows
                part(n, 0)
                if hp >= 1:
                    states(hp - 1)
                part(n, 1)
                if hp >= 1:
                    outputs(hp - 1)
                if hp < 4:
                    scores(hp)
            transpose_all(1, o, o_done, 1)
            for n in (AO0, AO1):
                rows(n, 0)
                rows(n, 1)

            def moe(layer):
                pe.wait_ge(router_in, 32)
                pe.wait_ge(consts_ready, 4)
                for i in range(2):
                    for q in range(4):
                        last = mm(ps[32 * q:32 * q + 32, BANK_A, 0:T], router[:, 2 * q + i, :], xT[:, 2 * q + i, :],
                                  start=i == 0, stop=i == 1, tile_position=(0, 32 * q))
                last.then_inc(parts_ps, 1)
                pe.wait_ge(parts_ready, layer + 1)
                for t in range(TT):
                    last = mm(ps[:, BANK_A, t * E:(t + 1) * E], logit_parts[:, t * P:(t + 1) * P], fold[:, :],
                              start=True, stop=True)
                last.then_inc(logit_ps, 1)
                for bank in range(4):
                    mm(ps[:, bank, :], zeros16[:, :], zeros16[:, :].unsqueeze(1).to_broadcast([P, COLS // P, P]),
                       start=True, stop=True)
                pe.wait_ge(routed, layer + 1)
                both = rt[:, 8, :]
                N = TT * E
                mm(ps[:, BANK_B, 0:E], later[:, :], both[:, 0:E], start=True, stop=True)
                mm(ps[:, BANK_B, E:N], later[:, :], both[:, E:N], start=True, stop=False)
                mm(ps[:, BANK_B, E:N], ones[:, :], both[:, 0:E], start=False, stop=True)
                mm(ps[:, BANK_B, N:N + E], ones[:, :], both[:, 0:E], start=True, stop=False)
                mm(ps[:, BANK_B, N:N + E], ones[:, :], both[:, E:N], start=False, stop=True).then_inc(rank_ps, 1)

                c0 = (PAIRS + 1) * layer

                def add_up(matrix, rows_, ends=None):
                    for t in range(TT):
                        if ends and t:
                            last.then_inc(ends, 1)
                        for j in range(2):
                            last = mm(ps[:, 2 * t + j, :], matrix[:, t * P:(t + 1) * P], rows_[:, j * COLS:(j + 1) * COLS],
                                      start=False, stop=True, skip_group_check=True)
                    if ends:
                        last.then_inc(ends, 1)
                    return last

                def gather_pair():
                    for k in range(KT):
                        at = (k % 4) * P
                        for t in range(TT):
                            last = mm(ps[:, (BANK_C, BANK_D)[k // 4], at:at + P], x[:, t, k * P:(k + 1) * P],
                                      pick[:, t, :, :].rearrange("p e s -> p (e s)"), start=t == 0, stop=t == TT - 1)
                    last.then_inc(xe_ps, 1)

                def both_experts(bank, tokens, w, tiles, first):
                    for k in range(tiles):
                        for e in range(2):
                            half = slice(e * SLOTS, (e + 1) * SLOTS)
                            last = mm(ps[half, bank, :], tokens[:, k, half], w[:, e, k, first:first + COLS],
                                      start=k == 0, stop=k == tiles - 1)
                    return last

                def overflow(e, count, i, pair, gate_w, done):
                    lower, upper = slice(0, SLOTS), slice(SLOTS, P)
                    with pe.If(count > 1):
                        with pe.Fori(1, count, 1):
                            pe.wait_ge(silu_ready, pair + 1)
                            pe.wait_ge(op_ready, done)
                            for k in range(KT):
                                for t in range(TT):
                                    last = mm(ps[:, BANK_A, k * SLOTS:(k + 1) * SLOTS], x[:, t, k * P:(k + 1) * P],
                                              o_pick[:, t, :], start=t == 0, stop=t == TT - 1)
                            last.then_inc(oxe_ps, 1)
                            pe.wait_ge(oxe_ready, done)
                            pe.wait_ge(ys_act, c0 + i + 1)
                            pe.wait_ge(ys_dve, c0 + i + 1)
                            for k in range(KT):
                                mm(ps[lower, BANK_C, :], o_xe[:, k, :], gate_w[:, e, k, :], start=k == 0, stop=k == KT - 1)
                                last = mm(ps[upper, BANK_D, :], o_xe[:, k, :], w_up[:, e, k, :],
                                          start=k == 0, stop=k == KT - 1)
                            last.then_inc(ogu_ps, 1)
                            pe.wait_ge(opg_ready, done)
                            pe.wait_ge(h_ready, pair + 1)
                            for t in range(TT):
                                last = mm(ps[lower, BANK_B, t * P:(t + 1) * P], o_pick_g[:, t, :], ident[:, :],
                                          start=True, stop=True)
                            last.then_inc(oput_ps, 1)
                            pe.wait_ge(oh_done, done)
                            for j in range(FT):
                                last = mm(ps[:, BANK_A, j * SLOTS:(j + 1) * SLOTS], o_h[:, j * P:(j + 1) * P],
                                          ident[lower, lower], start=True, stop=True)
                            last.then_inc(oht_ps, 1)
                            pe.wait_ge(down_in, 32 * pair + 32)
                            pe.wait_ge(oht_ready, done)
                            for j in range(FT):
                                mm(ps[lower, BANK_C, :], o_hT[:, j, :], w_down[:, e, j, 0:COLS],
                                   start=j == 0, stop=j == FT - 1)
                                last = mm(ps[upper, BANK_D, :], o_hT[:, j, :], w_down[:, e, j, COLS:D],
                                          start=j == 0, stop=j == FT - 1)
                            last.then_inc(oy_ps, 1)
                            pe.wait_ge(oput_done, done)
                            pe.wait_ge(oys_act, done)
                            pe.wait_ge(oys_done, done)
                            add_up(o_put, o_ys).then_inc(o_free, 1)
                            pe.reg_add(done, done, 1)

                pe.wait_ge(x_affine, 2 * layer + 1)
                pe.wait_ge(pick_ready, PAIRS * layer + 1)
                gather_pair()
                pe.wait_ge(slots_ready, layer + 1)

                def experts(i, gate_w, gate_in, loads, last_pair=False):
                    count_a = pe.value_load(chunks[0:1, bass.ds(2 * i, 1)], min_val=0, max_val=T // SLOTS)
                    count_b = pe.value_load(chunks[0:1, bass.ds(2 * i + 1, 1)], min_val=0, max_val=T // SLOTS)
                    pair = PAIRS * layer + i
                    pe.wait_ge(xe_act, pair + 1)
                    pe.wait_ge(xe_dve, pair + 1)
                    pe.wait_ge(gate_in, 32 * loads)
                    both_experts(BANK_A, xe, gate_w, KT, 0).then_inc(gate_ps, 1)
                    pe.wait_ge(put_done, c0 + i + 1)
                    if last_pair:
                        pe.wait_ge(ys_act, c0 + i + 1)
                        pe.wait_ge(ys_dve, c0 + i + 1)
                        add_up(put, ys).then_inc(acc_ps, 1)
                    pe.wait_ge(up_in, 32 * pair + 32)
                    both_experts(BANK_B, xe, w_up, KT, 0).then_inc(up_ps, 1)
                    overflow(0, count_a, i, pair, gate_w, done)
                    overflow(1, count_b, i, pair, gate_w, done)
                    pe.wait_ge(ys_act, c0 + i + 1)
                    pe.wait_ge(ys_dve, c0 + i + 1)
                    if not last_pair:
                        pe.wait_ge(pick_ready, pair + 2)
                        gather_pair()
                    pe.wait_ge(h_ready, pair + 1)
                    for j in range(FT):
                        last = nc.tensor.transpose(ps[:, BANK_A, j * P:(j + 1) * P], hid[:, j * P:(j + 1) * P], ident[:, :])
                    last.then_inc(ht_ps, 1)
                    if not last_pair:
                        add_up(put, ys).then_inc(acc_ps, 1)
                    pe.wait_ge(pickg_ready, pair + 1)
                    for t in range(TT):
                        last = nc.tensor.transpose(ps[:, BANK_B, t * P:(t + 1) * P],
                                                   pick_g[:, t, :, :].rearrange("p e s -> p (e s)"), ident[:, :])
                    last.then_inc(put_ps, 1)
                    pe.wait_ge(down_in, 32 * pair + 32)
                    pe.wait_ge(ht_ready, pair + 1)
                    if not last_pair:
                        pe.wait_ge(xe_act, pair + 2)
                        pe.wait_ge(xe_dve, pair + 2)
                    both_experts(BANK_C, hT, w_down, FT, 0).then_inc(yc_ps, 1)
                    both_experts(BANK_D, hT, w_down, FT, COLS).then_inc(yd_ps, 1)

                even, odd = (dense, even_gate_in), (w_gate, odd_gate_in)
                before = PAIRS // 2 * layer
                with pe.Fori(0, PAIRS // 2 - 1, 1) as two:
                    experts(2 * two, *even, before + two + 1)
                    experts(2 * two + 1, *odd, before + two + 1)
                experts(PAIRS - 2, *even, before + PAIRS // 2)
                experts(PAIRS - 1, *odd, before + PAIRS // 2, last_pair=True)
                pe.wait_ge(put_done, c0 + PAIRS + 1)
                pe.wait_ge(ys_act, c0 + PAIRS + 1)
                pe.wait_ge(ys_dve, c0 + PAIRS + 1)
                add_up(put, ys, ends=acc_ps)

            done = pe.alloc_register("pe_done")
            pe.reg_mov(done, 1)
            pe.sem_inc(o_free, 1)
            pe.sem_inc(put_ps, 1)
            transpose_all(2, x, x_done, 1)
            moe(0)

            transpose_all(3, x, x_done, 2)

            def attention_scores(h):
                u = h % 2
                if h >= 2:
                    pe.wait_ge(s_ready_raw, h - 1)
                for c in range(2):
                    part = slice(c * DH, (c + 1) * DH)
                    mm(ps[:, 2 * u + c, 0:P], qT[part, h, 0:P], kT[part, h, 0:P], start=True, stop=True)
                    last = mm(ps[:, 2 * u + c, P:3 * P], qT[part, h, P:T], kT[part, h, :], start=True, stop=True)
                last.then_inc(s_ps, 1)

            def block_of(n, part, between=()):
                part(n, 0)
                for h in between[:1]:
                    attention_scores(h)
                part(n, 1)
                for h in between[1:]:
                    attention_scores(h)

            block_of(K0, columns)
            block_of(Q0, columns)
            columns(K1, 0)
            pe.wait_ge(kq_act, 2)
            pe.wait_ge(kq_dve, 2)
            attention_scores(0)
            attention_scores(1)
            columns(K1, 1)
            block_of(Q1, columns, (2, 3))
            rows(BV0, 0)
            pe.wait_ge(kq_act, 4)
            pe.wait_ge(kq_dve, 4)
            attention_scores(4)
            rows(BV0, 1)
            attention_scores(5)
            block_of(BV1, rows, (6, 7))
            pe.wait_ge(v_act, 4)
            pe.wait_ge(v_dve, 4)

            def attention_turn(h):
                pe.wait_ge(a_ready, h + 1)
                if h == 0:
                    pe.wait_ge(s_ready_raw, HEADS)
                if h >= 2:
                    pe.wait_ge(at_ready, h - 1)
                for s in range(3):
                    last = nc.tensor.transpose(ps[:, h % 2, s * P:(s + 1) * P], o3[:, s, h * P:(h + 1) * P],
                                               ident[:, :])
                last.then_inc(at_ps, 1)

            def attention_out(h):
                hp, u = divmod(h, 2)
                pe.wait_ge(at_ready, h + 1)
                if hp >= 2 and u == 0:
                    pe.wait_ge(o_ready, 4 + hp - 1)
                bank = 2 + hp % 2
                cols = slice(h * P, (h + 1) * P)
                at = 2 * u * P
                mm(ps[:, bank, at:at + P], aT[:, u, 0, :], v[:, 0, cols], start=True, stop=True)
                mm(ps[:, bank, at + P:at + 2 * P], aT[:, u, 1, :], v[:, 0, cols], start=True, stop=False)
                last = mm(ps[:, bank, at + P:at + 2 * P], aT[:, u, 2, :], v[:, 1, cols], start=False, stop=True)
                if u:
                    last.then_inc(o_ps, 1)

            attention_turn(0)
            for h in range(HEADS):
                if h + 1 < HEADS:
                    attention_turn(h + 1)
                attention_out(h)
            transpose_all(4, o, o_done, 2)
            for n in (BO0, BO1):
                rows(n, 0)
                rows(n, 1)
            transpose_all(5, x, x_done, 3)
            moe(1)


def kernel(**inputs):
    import numpy as _np
    import concourse.bacc as _bacc
    from concourse import mybir as _mybir
    from concourse.bass_utils import run_bass_kernel_spmd as _run

    nc = _bacc.Bacc("TRN2", target_bir_lowering=False, num_devices=1, dynamic_dma_scratch_size=1024)
    arrays, aps = {}, {}
    for name, a in inputs.items():
        a = _np.ascontiguousarray(a)
        arrays[f"in_{name}"] = a
        aps[name] = nc.dram_tensor(f"in_{name}", a.shape, _mybir.dt.from_np(a.dtype), kind="ExternalInput").ap()
    out = nc.dram_tensor("out", (1, T, D), _mybir.dt.float32, kind="ExternalOutput").ap()
    build(nc, aps, out)
    r = _run(nc, [arrays], core_ids=[0])
    return r.results[0]["out"]
```
